# Optimizing a Trainium2 kernel written in Bass

```python
import math
import jax, jax.numpy as jnp
from jax import lax
import numpy as np
import jax
import jax.numpy as jnp

D_MODEL = 1024
BATCH = 1
SEQ = 256
DEPTH = 1

GRID_W = 64
CTX_LEN = 256
MIX_W = D_MODEL
F_GROUPS = 4
F_DIM = D_MODEL // 8
FOURIER_W = F_GROUPS * F_DIM
GDN_HEADS = 4
GDN_DK = D_MODEL // 8
GDN_DV = D_MODEL // 8
QK_W = GDN_HEADS * GDN_DK
V_W = GDN_HEADS * GDN_DV
IN_W = FOURIER_W + 2 * QK_W + 2 * V_W + 4 * GDN_HEADS
SHORT_CONV = 3
CHUNK = 64
D_FF = ((8 * D_MODEL // 3 + 127) // 128) * 128
EPS = 1e-6


def rmsnorm(t, g):
    tf = t.astype(jnp.float32)
    y = tf * lax.rsqrt(jnp.mean(tf * tf, axis=-1, keepdims=True) + EPS)
    return y.astype(t.dtype) * g

def l2norm(t):
    tf = t.astype(jnp.float32)
    return (tf * lax.rsqrt(jnp.sum(tf * tf, axis=-1, keepdims=True) + EPS)).astype(t.dtype)

def modulate(h, shift, scale):
    return h * (1 + scale) + shift

def dwconv1d(t, w):
    k_w = w.shape[0]
    pad = k_w // 2
    length = t.shape[1]
    tp = jnp.pad(t, ((0, 0), (pad, pad), (0, 0)))
    out = tp[:, 0:length] * w[0]
    for j in range(1, k_w):
        out = out + tp[:, j:j + length] * w[j]
    return out

def gated_delta_chunked(q, k, v, beta, g, s0):
    f32 = jnp.float32
    bsz, length, heads, dk = q.shape
    dv = v.shape[-1]
    n_chunks = length // CHUNK

    def chunks(t):
        t = t.astype(f32).reshape(bsz, n_chunks, CHUNK, heads, t.shape[-1])
        return jnp.transpose(t, (1, 0, 3, 2, 4))

    def chunks_s(t):
        t = t.astype(f32).reshape(bsz, n_chunks, CHUNK, heads)
        return jnp.transpose(t, (1, 0, 3, 2))

    qc = chunks(q) * (dk ** -0.5)
    kc = chunks(k)
    vc = chunks(v)
    bc = chunks_s(beta)
    gc = jnp.cumsum(chunks_s(g), axis=-1)
    lower = jnp.tril(jnp.ones((CHUNK, CHUNK), dtype=bool))
    strict = jnp.tril(jnp.ones((CHUNK, CHUNK), dtype=bool), -1)
    diff = gc[..., :, None] - gc[..., None, :]
    decay = jnp.where(lower, jnp.exp(jnp.where(lower, diff, 0.0)), 0.0)

    kb = kc * bc[..., None]
    vb = vc * bc[..., None]
    a_mat = jnp.where(strict, jnp.einsum('nbhid,nbhjd->nbhij', kb, kc) * decay, 0.0)
    eye = jnp.eye(CHUNK, dtype=f32)
    t_inv = lax.linalg.triangular_solve(eye + a_mat, jnp.broadcast_to(eye, a_mat.shape),
                                        left_side=True, lower=True, unit_diagonal=True)
    u_val = jnp.einsum('nbhij,nbhjd->nbhid', t_inv, vb)
    w_key = jnp.einsum('nbhij,nbhjd->nbhid', t_inv, kb * jnp.exp(gc)[..., None])
    attn_intra = jnp.where(lower, jnp.einsum('nbhid,nbhjd->nbhij', qc, kc) * decay, 0.0)
    g_last = gc[..., -1]
    k_dec = kc * jnp.exp(g_last[..., None] - gc)[..., None]
    q_dec = qc * jnp.exp(gc)[..., None]

    def step(s, xs):
        u_i, w_i, a_i, qd_i, kd_i, gl_i = xs
        v_new = u_i - jnp.einsum('bhcd,bhde->bhce', w_i, s)
        o_i = jnp.einsum('bhcd,bhde->bhce', qd_i, s) + jnp.einsum('bhij,bhje->bhie', a_i, v_new)
        s = s * jnp.exp(gl_i)[..., None, None] + jnp.einsum('bhcd,bhce->bhde', kd_i, v_new)
        return s, o_i

    s_final, o = lax.scan(step, s0.astype(f32), (u_val, w_key, attn_intra, q_dec, k_dec, g_last))
    o = jnp.transpose(o, (1, 0, 3, 2, 4)).reshape(bsz, length, heads, dv)
    return o.astype(v.dtype), s_final

def bidir_gdn(q, k, v, beta, g, s0_f, s0_b):
    flip = lambda t: jnp.flip(t, axis=1)
    o_f, s_f = gated_delta_chunked(q, k, v, beta[:, :, 0], g[:, :, 0], s0_f)
    o_b, s_b = gated_delta_chunked(flip(q), flip(k), flip(v), flip(beta[:, :, 1]), flip(g[:, :, 1]), s0_b)
    return o_f + flip(o_b), s_f, s_b

def mixer_inputs(h, w_in_l, conv_l, a_log_l, dt_bias_l):
    bsz, length, _ = h.shape
    p = h @ w_in_l
    o1 = FOURIER_W
    o2 = o1 + 2 * QK_W + V_W
    o3 = o2 + V_W
    u = p[..., :o1]
    qkv = jax.nn.silu(dwconv1d(p[..., o1:o2], conv_l))
    z = p[..., o2:o3]
    ab = p[..., o3:].astype(jnp.float32).reshape(bsz, length, 4, GDN_HEADS)
    q = l2norm(qkv[..., :QK_W].reshape(bsz, length, GDN_HEADS, GDN_DK))
    k = l2norm(qkv[..., QK_W:2 * QK_W].reshape(bsz, length, GDN_HEADS, GDN_DK))
    v = qkv[..., 2 * QK_W:].reshape(bsz, length, GDN_HEADS, GDN_DV)
    beta = jax.nn.sigmoid(ab[:, :, 0:2])
    g = -jnp.exp(a_log_l.astype(jnp.float32)) * jax.nn.softplus(ab[:, :, 2:4] + dt_bias_l.astype(jnp.float32))
    return u, z, q, k, v, beta, g

def fourier_mix(u, w_f):
    bsz, length, _ = u.shape
    ug = u.astype(jnp.float32).reshape(bsz, length, F_GROUPS, F_DIM)
    y = jnp.fft.fft2(ug, axes=(1, 3), norm='ortho').real.astype(u.dtype)
    return jnp.einsum('blgc,gcd->blgd', y, w_f).reshape(bsz, length, FOURIER_W)

def mixer_out(u, o, z, w_f, g_gdn_l, w_out_l):
    bsz, length, _ = z.shape
    y_f = fourier_mix(u, w_f)
    y_d = rmsnorm(o, g_gdn_l) * jax.nn.silu(z).reshape(bsz, length, GDN_HEADS, GDN_DV)
    return jnp.concatenate([y_f, y_d.reshape(bsz, length, V_W)], axis=-1) @ w_out_l

def conv_ffn(h, w_up_l, w_dwc_l, w_down_l, on_grid):
    bsz, length, _ = h.shape
    p = h @ w_up_l
    val, gate = p[..., :D_FF], p[..., D_FF:]
    if on_grid:
        rows = length // GRID_W
        gate = lax.conv_general_dilated(
            gate.reshape(bsz, rows, GRID_W, D_FF), w_dwc_l[:, :, None, :],
            window_strides=(1, 1), padding='SAME',
            dimension_numbers=('NHWC', 'HWIO', 'NHWC'),
            feature_group_count=D_FF).reshape(bsz, length, D_FF)
    else:
        gate = dwconv1d(gate, w_dwc_l[1])
    return (jax.nn.silu(gate) * val) @ w_down_l

def first_inputs(seed: int = 0) -> dict:
    key = jax.random.key(seed)
    ks = jax.random.split(key, 20)
    f32 = jnp.float32

    def nrm(k, shape, s):
        return jax.random.normal(k, shape, f32) * s

    L = DEPTH
    x = nrm(ks[0], (BATCH, SEQ, D_MODEL), 1.0)
    c = nrm(ks[1], (BATCH, D_MODEL), 1.0)
    ctx = nrm(ks[2], (BATCH, CTX_LEN, D_MODEL), 1.0)
    c_ctx = nrm(ks[3], (D_MODEL,), 1.0)
    w_ada = nrm(ks[4], (L, D_MODEL, 6 * D_MODEL), 0.5 * D_MODEL ** -0.5)
    b_ada = nrm(ks[5], (L, 6 * D_MODEL), 0.02)
    g_pre_mix = 1.0 + nrm(ks[6], (L, D_MODEL), 0.1)
    g_post_mix = 1.0 + nrm(ks[7], (L, D_MODEL), 0.1)
    g_pre_ffn = 1.0 + nrm(ks[8], (L, D_MODEL), 0.1)
    g_post_ffn = 1.0 + nrm(ks[9], (L, D_MODEL), 0.1)
    w_in = nrm(ks[10], (L, D_MODEL, IN_W), D_MODEL ** -0.5)
    w_qkv_conv = nrm(ks[11], (L, SHORT_CONV, 2 * QK_W + V_W), SHORT_CONV ** -0.5)
    a_log = jnp.log(jax.random.uniform(ks[12], (L, 2, GDN_HEADS), f32, minval=1.0, maxval=16.0))
    dt = jnp.exp(jax.random.uniform(ks[13], (L, 2, GDN_HEADS), f32,
                                    minval=math.log(1e-3), maxval=math.log(1e-1)))
    dt_bias = dt + jnp.log(-jnp.expm1(-dt))
    g_gdn = 1.0 + nrm(ks[14], (L, GDN_DV), 0.1)
    w_fourier = nrm(ks[15], (L, F_GROUPS, F_DIM, F_DIM), F_DIM ** -0.5)
    w_out = nrm(ks[16], (L, MIX_W, D_MODEL), MIX_W ** -0.5)
    w_up = nrm(ks[17], (L, D_MODEL, 2 * D_FF), D_MODEL ** -0.5)
    w_dwc = nrm(ks[18], (L, 3, 3, D_FF), 1.0 / 3.0)
    w_down = nrm(ks[19], (L, D_FF, D_MODEL), D_FF ** -0.5)
    return {"x": x, "c": c, "ctx": ctx, "c_ctx": c_ctx, "w_ada": w_ada, "b_ada": b_ada,
            "g_pre_mix": g_pre_mix, "g_post_mix": g_post_mix, "g_pre_ffn": g_pre_ffn,
            "g_post_ffn": g_post_ffn, "w_in": w_in, "w_qkv_conv": w_qkv_conv, "a_log": a_log,
            "dt_bias": dt_bias, "g_gdn": g_gdn, "w_fourier": w_fourier, "w_out": w_out,
            "w_up": w_up, "w_dwc": w_dwc, "w_down": w_down}

def first_block(x, c, ctx, c_ctx, w_ada, b_ada, g_pre_mix, g_post_mix, g_pre_ffn, g_post_ffn,
              w_in, w_qkv_conv, a_log, dt_bias, g_gdn, w_fourier, w_out, w_up, w_dwc, w_down):
    xl, xc = x, ctx
    bsz = x.shape[0]
    silu_c = jax.nn.silu(c)
    silu_cc = jax.nn.silu(c_ctx)
    for i in range(DEPTH):
        update_ctx = i < DEPTH - 1
        mod_l = (silu_c @ w_ada[i] + b_ada[i])[:, None, :]
        mod_c = silu_cc @ w_ada[i] + b_ada[i]
        sh1l, sc1l, gt1l, sh2l, sc2l, gt2l = jnp.split(mod_l, 6, axis=-1)
        sh1c, sc1c, gt1c, sh2c, sc2c, gt2c = jnp.split(mod_c, 6, axis=-1)

        hl = modulate(rmsnorm(xl, g_pre_mix[i]), sh1l, sc1l)
        hc = modulate(rmsnorm(xc, g_pre_mix[i]), sh1c, sc1c)
        ul, zl, ql, kl, vl, bl, gl = mixer_inputs(hl, w_in[i], w_qkv_conv[i], a_log[i], dt_bias[i])
        uc, zc, qc, kc, vc, bc, gc = mixer_inputs(hc, w_in[i], w_qkv_conv[i], a_log[i], dt_bias[i])
        s_zero = jnp.zeros((bsz, GDN_HEADS, GDN_DK, GDN_DV), jnp.float32)
        oc, s_f, s_b = bidir_gdn(qc, kc, vc, bc, gc, s_zero, s_zero)
        ol, _, _ = bidir_gdn(ql, kl, vl, bl, gl, s_f, s_b)
        yl = mixer_out(ul, ol, zl, w_fourier[i], g_gdn[i], w_out[i])
        xl = xl + gt1l * rmsnorm(yl, g_post_mix[i])
        if update_ctx:
            yc = mixer_out(uc, oc, zc, w_fourier[i], g_gdn[i], w_out[i])
            xc = xc + gt1c * rmsnorm(yc, g_post_mix[i])

        hl = modulate(rmsnorm(xl, g_pre_ffn[i]), sh2l, sc2l)
        xl = xl + gt2l * rmsnorm(conv_ffn(hl, w_up[i], w_dwc[i], w_down[i], True), g_post_ffn[i])
        if update_ctx:
            hc = modulate(rmsnorm(xc, g_pre_ffn[i]), sh2c, sc2c)
            xc = xc + gt2c * rmsnorm(conv_ffn(hc, w_up[i], w_dwc[i], w_down[i], False), g_post_ffn[i])
    return xl


DEPTH_2 = 2

Q_BLOCK = 128
ROPE_BASE = 10000.0
RET_HEADS = 4
RET_DK = 128
RET_DV = 256
RET_QK = RET_HEADS * RET_DK
RET_V = RET_HEADS * RET_DV
LRU_WIDTH = D_MODEL
LRU_BLOCKS = 8
LRU_BW = LRU_WIDTH // LRU_BLOCKS
CONV_W = 4
LRU_C = 8.0
FOX_HEADS = 8
FOX_DH = 128
FOX_W = FOX_HEADS * FOX_DH
D_FF_2 = 4 * D_MODEL
N_BRANCH = 3
SPLITS = (RET_QK, RET_QK, RET_V, RET_V, LRU_WIDTH, LRU_WIDTH, FOX_W, FOX_W, FOX_W, FOX_HEADS, N_BRANCH * D_MODEL)
D_IN = 2 * RET_QK + 2 * RET_V + 2 * LRU_WIDTH + 3 * FOX_W + FOX_HEADS + N_BRANCH * D_MODEL


def rms_norm(x, g):
    xf = x.astype(jnp.float32)
    y = xf * lax.rsqrt(jnp.mean(xf * xf, axis=-1, keepdims=True) + EPS)
    return (y * g.astype(jnp.float32)).astype(x.dtype)

def head_norm(o):
    mu = jnp.mean(o, axis=-1, keepdims=True)
    var = jnp.mean(jnp.square(o - mu), axis=-1, keepdims=True)
    return (o - mu) * lax.rsqrt(var + EPS)

def rope(x, pos):
    half = x.shape[-1] // 2
    inv = ROPE_BASE ** (-jnp.arange(half, dtype=jnp.float32) / half)
    ang = pos.astype(jnp.float32)[:, None] * inv[None, :]
    cos = jnp.cos(ang)[None, :, None, :]
    sin = jnp.sin(ang)[None, :, None, :]
    xf = x.astype(jnp.float32)
    x1, x2 = xf[..., :half], xf[..., half:]
    return jnp.concatenate([x1 * cos - x2 * sin, x1 * sin + x2 * cos], axis=-1)

def retention(q, k, v):
    B, S, H, dk = q.shape
    nc = S // CHUNK
    log_g = jnp.log(1.0 - 2.0 ** (-5.0 - jnp.arange(H, dtype=jnp.float32)))
    idx = jnp.arange(CHUNK, dtype=jnp.float32)
    inner = jnp.exp(jnp.abs(idx[:, None] - idx[None, :])[None] * log_g[:, None, None])
    q_dec = jnp.exp((idx + 1.0)[None, :] * log_g[:, None])[None, :, :, None]
    k_dec = jnp.exp((CHUNK - 1.0 - idx)[None, :] * log_g[:, None])[None, :, :, None]
    chunk_dec = jnp.exp(CHUNK * log_g)[None, :, None, None]

    def to_chunks(t):
        return t.astype(jnp.float32).reshape(B, nc, CHUNK, H, t.shape[-1]).transpose(1, 0, 3, 2, 4)

    qc, kc, vc = to_chunks(q), to_chunks(k * RET_DK ** -0.5), to_chunks(v)

    def step(state, xs):
        qi, ki, vi = xs
        s = jnp.einsum('bhqd,bhkd->bhqk', qi, ki) * inner[None]
        o = jnp.einsum('bhqk,bhkv->bhqv', s, vi) + jnp.einsum('bhqd,bhdv->bhqv', qi * q_dec, state)
        state = state * chunk_dec + jnp.einsum('bhkd,bhkv->bhdv', ki * k_dec, vi)
        return state, o

    state0 = jnp.zeros((B, H, dk, v.shape[-1]), jnp.float32)
    _, o = lax.scan(step, state0, (qc, kc, vc))
    return o.transpose(1, 0, 3, 2, 4).reshape(B, S, H, v.shape[-1])

def causal_conv(x, w, b):
    S = x.shape[1]
    xp = jnp.pad(x, ((0, 0), (CONV_W - 1, 0), (0, 0)))
    out = xp[:, 0:S] * w[0]
    for i in range(1, CONV_W):
        out = out + xp[:, i:i + S] * w[i]
    return out + b

def rg_lru(x, w_a, b_a, w_x, b_x, lam):
    B, S, W = x.shape
    xb = x.reshape(B, S, LRU_BLOCKS, LRU_BW)
    r = jax.nn.sigmoid(jnp.einsum('bsni,nio->bsno', xb, w_a).reshape(B, S, W) + b_a)
    i = jax.nn.sigmoid(jnp.einsum('bsni,nio->bsno', xb, w_x).reshape(B, S, W) + b_x)
    log_a = -LRU_C * r.astype(jnp.float32) * jax.nn.softplus(-lam.astype(jnp.float32))
    a = jnp.exp(log_a)
    u = jnp.sqrt(jnp.maximum(-jnp.expm1(2.0 * log_a), 0.0)) * (i * x).astype(jnp.float32)

    def combine(left, right):
        a1, b1 = left
        a2, b2 = right
        return a1 * a2, a2 * b1 + b2

    _, h = lax.associative_scan(combine, (a, u), axis=1)
    return h.astype(x.dtype)

def forgetting_attention(q, k, v, log_f):
    B, S, H, D = q.shape
    nb = S // Q_BLOCK
    cum = jnp.cumsum(log_f, axis=1).transpose(0, 2, 1)
    kf = k.astype(jnp.float32)
    vf = v.astype(jnp.float32)
    qb = q.astype(jnp.float32).reshape(B, nb, Q_BLOCK, H, D).transpose(1, 0, 2, 3, 4)
    cq = cum.reshape(B, H, nb, Q_BLOCK).transpose(2, 0, 1, 3)
    kpos = jnp.arange(S)
    scale = D ** -0.5

    def block(args):
        qi, ci, start = args
        s = jnp.einsum('bqhd,bkhd->bhqk', qi, kf) * scale + (ci[..., None] - cum[:, :, None, :])
        qpos = start + jnp.arange(Q_BLOCK)
        s = jnp.where((kpos[None, :] <= qpos[:, None])[None, None], s, -jnp.inf)
        p = jax.nn.softmax(s, axis=-1)
        return jnp.einsum('bhqk,bkhd->bqhd', p, vf)

    o = lax.map(block, (qb, cq, jnp.arange(nb) * Q_BLOCK))
    return o.transpose(1, 0, 2, 3, 4).reshape(B, S, H, D)

def hybrid_layer(x, c, ada_w, ada_b, g_pre_mix, g_post_mix, g_pre_mlp, g_post_mlp, w_in, conv_w, conv_b,
                 w_a, b_a, w_x, b_x, lam, b_f, ret_w_o, lru_w_o, fox_w_o, w_out, w1, w2):
    B, S, _ = x.shape
    mod = jax.nn.silu(c) @ ada_w + ada_b
    sh_m, sc_m, gt_m, sh_f, sc_f, gt_f = [t[:, None, :] for t in jnp.split(mod, 6, axis=-1)]

    h = rms_norm(x, g_pre_mix) * (1.0 + sc_m) + sh_m
    proj = h @ w_in
    offs = [int(o) for o in np.cumsum(SPLITS)[:-1]]
    rq, rk, rv, rg, lx, ly, fq, fk, fv, ff, gates = jnp.split(proj, offs, axis=-1)
    pos = jnp.arange(S)

    rq = rope(rq.reshape(B, S, RET_HEADS, RET_DK), pos)
    rk = rope(rk.reshape(B, S, RET_HEADS, RET_DK), pos)
    ret = head_norm(retention(rq, rk, rv.reshape(B, S, RET_HEADS, RET_DV)))
    y_ret = jax.nn.silu(rg) * ret.reshape(B, S, RET_V).astype(x.dtype)

    u = causal_conv(lx, conv_w, conv_b)
    y_lru = jax.nn.gelu(ly) * rg_lru(u, w_a, b_a, w_x, b_x, lam)

    log_f = jax.nn.log_sigmoid((ff + b_f).astype(jnp.float32))
    fo = forgetting_attention(fq.reshape(B, S, FOX_HEADS, FOX_DH), fk.reshape(B, S, FOX_HEADS, FOX_DH),
                              fv.reshape(B, S, FOX_HEADS, FOX_DH), log_f)
    y_fox = fo.reshape(B, S, FOX_W).astype(x.dtype)

    g = jax.nn.sigmoid(gates).reshape(B, S, N_BRANCH, D_MODEL)
    merged = g[:, :, 0] * (y_ret @ ret_w_o) + g[:, :, 1] * (y_lru @ lru_w_o) + g[:, :, 2] * (y_fox @ fox_w_o)
    x = x + gt_m * rms_norm(merged @ w_out, g_post_mix)

    h = rms_norm(x, g_pre_mlp) * (1.0 + sc_f) + sh_f
    f = jnp.square(jax.nn.relu(h @ w1)) @ w2
    return x + gt_f * rms_norm(f, g_post_mlp)

def second_inputs(seed: int = 0) -> dict:
    key = jax.random.key(seed)
    ks = jax.random.split(key, 28)
    f32 = jnp.float32
    L, D = DEPTH_2, D_MODEL

    def nrm(k, shape, scale):
        return jax.random.normal(k, shape, f32) * scale

    a0 = jax.random.uniform(ks[14], (L, LRU_WIDTH), f32, 0.9, 0.999)
    s = a0 ** (1.0 / LRU_C)
    lam = jnp.log(s) - jnp.log1p(-s)
    return {
        'x': nrm(ks[0], (BATCH, SEQ, D), 1.0),
        'c': nrm(ks[1], (BATCH, D), 1.0),
        'ada_w': nrm(ks[2], (L, D, 6 * D), D ** -0.5),
        'ada_b': nrm(ks[3], (L, 6 * D), 0.02),
        'norm_pre_mix': 1.0 + nrm(ks[4], (L, D), 0.05),
        'norm_post_mix': 1.0 + nrm(ks[5], (L, D), 0.05),
        'norm_pre_mlp': 1.0 + nrm(ks[6], (L, D), 0.05),
        'norm_post_mlp': 1.0 + nrm(ks[7], (L, D), 0.05),
        'w_in': nrm(ks[8], (L, D, D_IN), D ** -0.5),
        'conv_w': nrm(ks[9], (L, CONV_W, LRU_WIDTH), CONV_W ** -0.5),
        'conv_b': nrm(ks[10], (L, LRU_WIDTH), 0.02),
        'lru_w_a': nrm(ks[11], (L, LRU_BLOCKS, LRU_BW, LRU_BW), LRU_BW ** -0.5),
        'lru_b_a': nrm(ks[12], (L, LRU_WIDTH), 0.02),
        'lru_w_x': nrm(ks[13], (L, LRU_BLOCKS, LRU_BW, LRU_BW), LRU_BW ** -0.5),
        'lru_b_x': nrm(ks[15], (L, LRU_WIDTH), 0.02),
        'lru_lambda': lam,
        'fox_b_f': jax.random.uniform(ks[16], (L, FOX_HEADS), f32, 1.0, 5.0),
        'ret_w_o': nrm(ks[17], (L, RET_V, D), RET_V ** -0.5),
        'lru_w_o': nrm(ks[18], (L, LRU_WIDTH, D), LRU_WIDTH ** -0.5),
        'fox_w_o': nrm(ks[19], (L, FOX_W, D), FOX_W ** -0.5),
        'w_out': nrm(ks[20], (L, D, D), D ** -0.5),
        'mlp_w1': nrm(ks[21], (L, D, D_FF_2), D ** -0.5),
        'mlp_w2': nrm(ks[22], (L, D_FF_2, D), D_FF_2 ** -0.5),
    }

def second_block(x, c, ada_w, ada_b, norm_pre_mix, norm_post_mix, norm_pre_mlp, norm_post_mlp, w_in, conv_w,
              conv_b, lru_w_a, lru_b_a, lru_w_x, lru_b_x, lru_lambda, fox_b_f, ret_w_o, lru_w_o, fox_w_o,
              w_out, mlp_w1, mlp_w2):
    for l in range(DEPTH_2):
        x = hybrid_layer(x, c, ada_w[l], ada_b[l], norm_pre_mix[l], norm_post_mix[l], norm_pre_mlp[l],
                         norm_post_mlp[l], w_in[l], conv_w[l], conv_b[l], lru_w_a[l], lru_b_a[l], lru_w_x[l],
                         lru_b_x[l], lru_lambda[l], fox_b_f[l], ret_w_o[l], lru_w_o[l], fox_w_o[l], w_out[l],
                         mlp_w1[l], mlp_w2[l])
    return x


def setup_inputs(seed=0):
    out = dict(first_inputs(seed))
    for name, value in second_inputs(seed + 1).items():
        if name != "x":
            out[name + "_2"] = value
    return out


def reference(
    x, c, ctx, c_ctx, w_ada, b_ada, g_pre_mix, g_post_mix, g_pre_ffn, g_post_ffn, w_in,
    w_qkv_conv, a_log, dt_bias, g_gdn, w_fourier, w_out, w_up, w_dwc, w_down, c_2, ada_w_2,
    ada_b_2, norm_pre_mix_2, norm_post_mix_2, norm_pre_mlp_2, norm_post_mlp_2, w_in_2, conv_w_2,
    conv_b_2, lru_w_a_2, lru_b_a_2, lru_w_x_2, lru_b_x_2, lru_lambda_2, fox_b_f_2, ret_w_o_2,
    lru_w_o_2, fox_w_o_2, w_out_2, mlp_w1_2, mlp_w2_2,
):
    x = first_block(
        x, c, ctx, c_ctx, w_ada, b_ada, g_pre_mix, g_post_mix, g_pre_ffn, g_post_ffn, w_in,
        w_qkv_conv, a_log, dt_bias, g_gdn, w_fourier, w_out, w_up, w_dwc, w_down,
    )
    return second_block(
        x, c_2, ada_w_2, ada_b_2, norm_pre_mix_2, norm_post_mix_2, norm_pre_mlp_2,
        norm_post_mlp_2, w_in_2, conv_w_2, conv_b_2, lru_w_a_2, lru_b_a_2, lru_w_x_2, lru_b_x_2,
        lru_lambda_2, fox_b_f_2, ret_w_o_2, lru_w_o_2, fox_w_o_2, w_out_2, mlp_w1_2, mlp_w2_2,
    )


_drawn_inputs = setup_inputs


def setup_inputs(seed=0):
    import zlib

    import numpy as np

    out = dict(_drawn_inputs(seed))
    spreads = {}
    factors = {'c_ctx': 3.913, 'conv_b_2': 3.066, 'lru_b_a_2': 38.095, 'lru_b_x_2': 8.0, 'ctx': 2.678}
    for name, (base, spread) in spreads.items():
        noise = np.random.default_rng([zlib.crc32(name.encode()), seed]).standard_normal(out[name].shape)
        drawn = base * np.exp(spread * noise) if base else spread * noise
        out[name] = jnp.asarray(drawn.astype(out[name].dtype))
    for name, factor in factors.items():
        out[name] = (out[name] * factor).astype(out[name].dtype)
    return out
```

```python
import math
from contextlib import ExitStack

import numpy as np

import concourse.bass as bass
from concourse import mybir

P = 128
D = 1024
KT = D // P
T = 256
TT = T // P
EPS = 1e-6
CH = 2048
RAW = 4
D_FF = 2816
FB = D_FF // P
GRID_W = 64
ROWS = T // GRID_W
HEADS = 4
MLP_B = 4096 // P
LRU_C = 8.0

N_Q, N_KV, N_UZ = 0, 2, 6
N_OUT1, N_UP, N_DOWN = 10, 14, 36
N_LAYER = 47
(L_RV, L_RQK, L_RETO, L_LX, L_LYG, L_LRU, L_LRUO, L_FV, L_FQK, L_FOXO, L_WOUT, L_MLP) = (
    0, 4, 16, 20, 24, 32, 33, 37, 41, 53, 57, 61)
LAYER_CH = 93
LAYERS = 2

V1 = {}
VL = {}


def _columns():
    at = 0
    for name, n in (("c", KT), ("c_ctx", KT), ("c_2", KT), ("b_ada", 48), ("g_pre_mix", KT), ("g_post_mix", KT),
                    ("g_pre_ffn", KT), ("g_post_ffn", KT), ("conv", 36), ("g_gdn", 1), ("dwc", 9 * FB),
                    ("dt_bias", 8), ("a_log", 8)):
        V1[name] = at
        at += n
    first = at
    at = 0
    for name, n in (("b_ada", 48), ("g_pre_mix", KT), ("g_post_mix", KT), ("g_pre_mlp", KT), ("g_post_mlp", KT),
                    ("conv_w", 32), ("conv_b", 8), ("b_a", 8), ("b_x", 8), ("lam", 8), ("b_f", 8)):
        VL[name] = at
        at += n
    return first, at


VEC_FIRST, VEC_LAYER = _columns()
NV = VEC_FIRST + LAYERS * VEC_LAYER

C_ID, C_TRIU, C_ONES, C_OMEAN = 0, 128, 256, 384
N_COMMON = 512
A_TRIL, A_STR, A_LVL, A_CC, A_SC, A_CL, A_SL = 0, 128, 384, 384 + 14 * 128, 384 + 15 * 128, 384 + 16 * 128, 384 + 16 * 128 + 512
N_CA = A_SL + 512
B_PERM, B_COS, B_SIN, B_RET, B_FM = 0, 128, 384, 640, 640 + 2048
N_CB = B_FM + 256
N_CU = max(N_CA, N_CB)
SW_AB, SW_FF, SW_WF = 0, 128, 256
N_SW = 768


def build_program(nc, io, layers=LAYERS):
    f32, f32r = mybir.dt.float32, mybir.dt.float32r
    ALU, ACT, AX = mybir.AluOpType, mybir.ActivationFunctionType, mybir.AxisListType.X
    total = N_LAYER + LAYER_CH * layers
    ADA_N = 24 * (1 + layers)
    ctx = ExitStack()
    with ctx:
        place = [16512]

        def room(nbytes):
            at = place[0]
            place[0] += nbytes
            assert place[0] <= 229344, place[0]
            return at

        def at(name, shape, offset, dt=f32):
            return nc.alloc_sbuf_tensor_at(name, shape, dt, offset=offset)

        def new(name, shape, dt=f32):
            n = 4
            for s in shape[1:]:
                n *= s
            return at(name, shape, room((n + 31) // 32 * 32), dt)

        raw = new("raw", [P, RAW, CH])
        w_hi = new("w_hi", [P, 2, CH], f32r)
        w_lo = new("w_lo", [P, 2, CH], f32r)
        x = new("x", [P, KT, T])
        F = [room(8192) for _ in range(4)]
        act_hi = [at(f"act_hi{i}", [P, KT, T], F[i], f32r) for i in range(2)]
        act_lo = [at(f"act_lo{i}", [P, KT, T], F[2 + i], f32r) for i in range(2)]
        ada_raw = new("ada_raw", [P, 2, CH])
        ada_acc = new("ada_acc", [P, 2, T])
        cc = new("consts_common", [P, N_COMMON])
        cu = new("consts_stage", [P, N_CU])
        vec = new("vectors", [P, NV])
        sw = new("small_weights", [P, N_SW])
        sw_hi = new("small_hi", [P, 256], f32r)
        sw_lo = new("small_lo", [P, 256], f32r)
        cs = new("silu_c", [P, 3, KT])
        cth = new("silu_c_tanh", [P, 3 * KT])
        mod = new("mod", [P, 48])
        mod_ctx = new("mod_ctx", [P, 16])
        gs = new("gain_scale", [P, 4, KT])
        eps = new("eps", [P, 1])
        std = new("std", [P, T])
        rstd = new("rstd", [P, T])
        sm = new("smalls", [P, 12, 32])
        A = [room(8192) for _ in range(7)]
        print_left = 229344 - place[0]
        ident, triu, ones, omean = (cc[:, o:o + P] for o in (C_ID, C_TRIU, C_ONES, C_OMEAN))

        ps = ctx.enter_context(nc.psum_tensor("ps", [P, 8, 512], f32))
        sems = {}

        def S(name):
            if name not in sems:
                sems[name] = ctx.enter_context(nc.semaphore(name))
            return sems[name]

        for s in range(RAW):
            S(f"raw_loaded{s}")
        block = ctx.enter_context(nc.Block())

        class Order:

            def __init__(self, eng, name):
                self.eng, self.sem, self.n = eng, S(name), 0

            def mark(self, ins):
                ins.then_inc(self.sem, 1)
                self.n = self.n + 1

            def __call__(self, ins):
                self.mark(ins)
                self.eng.wait_ge(self.sem, self.n)

        def bc(ap, n):
            ap = ap.unsqueeze(len(ap.shape))
            return ap.to_broadcast(list(ap.shape[:-1]) + [n])

        def bmid(ap, n):
            ap = ap.unsqueeze(1)
            return ap.to_broadcast([ap.shape[0], n, ap.shape[2]])

        def flat(ap):
            s = ap.shape
            return ap if len(s) == 2 else ap.rearrange("p a b -> p (a b)") if len(s) == 3 else ap.rearrange("p a b c -> p (a b c)")

        def V(name, n=1, i=0, layer=None):
            o = V1[name] if layer is None else VEC_FIRST + layer * VEC_LAYER + VL[name]
            return vec[:, o + i:o + i + n]

        pre_kv = at("pre_kv", [P, 8, 2, T + 2], A[0])
        pre_q = at("pre_q", [P, 4, T + 2], A[0] + 16512)
        assert 16512 + 4 * 258 * 4 <= 24576
        uz = at("uz", [P, 8, T], A[3])
        y_kv = at("y_kv", [P, 8, 2, T], A[4])
        y_q = at("y_q", [P, 4, T], A[6])
        th_kv = at("th_kv", [P, 8, 2, T], A[0])
        th_q = at("th_q", [P, 4, T], A[0] + 16384)
        k_tok = at("k_tok", [P, 4, 4, P], F[0])
        v_tok = at("v_tok", [P, 4, 4, P], F[1])
        q_tok = at("q_tok", [P, 2, 4, P], F[2])
        sq_kq = at("sq_kq", [P, 16, P], A[0])
        sq_q = at("sq_q", [P, 8, P], A[1])
        kT = at("kT", [P, 4, 4, P], A[1])
        qT = at("qT", [P, 2, 4, P], F[2] + 4096)
        attnT = at("attnT", [P, 2, 2, 4, P], A[2])
        U = at("U", [P, 2, 4, 4, P], A[4])
        Bm = at("Bm", [P, 4, 4, P], A[0])
        Tm = at("Tm", [P, 4, 4, P], A[6])
        X = at("X", [P, 4, 4, P], F[3])
        dec = at("dec", [P, 4, P], F[2])
        dem = at("dem", [P, 4, P], F[2] + 2048)
        St = at("state", [P, 2, 4, P], A[0])
        o_tok = at("o_tok", [P, 2, 4, P], A[0] + 4096)
        Rm = at("Rm", [P, 2, 4, P], A[6])
        vn = at("vn", [P, 2, 4, P], A[6] + 4096)
        v2 = at("v2", [P, 2, 4, P], F[3])
        tmp_s = at("tmp_s", [P, 2, 4, P], F[3] + 4096)
        o_sq = at("o_sq", [P, 8, P], A[6])
        th_z = at("th_z", [P, 4, T], F[2])
        yfd = at("yfd", [P, 8, T], A[6])
        m1 = at("m1", [P, 4, 2, P], A[2])
        Z = at("Z", [P, 2, 4, 2, P], A[1])
        norm_sq1, norm_h1 = at("norm_sq1", [P, KT, T], A[4]), at("norm_h1", [P, KT, T], A[5])
        xc = at("xc", [P, KT, T], A[3])
        ctx_acc = at("ctx_acc", [P, 8, T], A[0])
        ctx_prod = at("ctx_prod", [P, CH], A[1])
        ada_in1 = at("ada_in1", [P, 8, T], A[2])
        ada_in16 = at("ada_in16", [P, 16, T], A[0])
        ada_in = at("ada_in", [P, 24, T], A[0])
        y1 = at("y1", [P, KT, T], A[5])
        mid_hi1 = at("mid_hi1", [P, FB, T], A[0], f32r)
        mid_lo1 = at("mid_lo1", [P, FB, T], A[0] + FB * T * 4, f32r)
        ft = A[0] + 2 * FB * T * 4
        gpad = at("gpad", [P, 2, ROWS + 2, GRID_W + 2], ft)
        gacc = at("gacc", [P, 2, T], ft + 3168)
        gth = at("gth", [P, 2, T], ft + 3168 + 2048)
        gm = at("gm", [P, 2, T], ft + 3168 + 4096)
        assert ft + 3168 + 6144 <= A[6] + 8192
        y_down = at("y_down", [P, KT, T], F[0])
        sq_down = at("sq_down", [P, KT, T], F[2])
        a012 = at("a012", [P, 3 * KT, T], A[0])
        a0, a1, a2 = (a012[:, i * KT:(i + 1) * KT, :] for i in range(3))
        a3, a4, a5, a6 = (at(f"a{i}", [P, KT, T], A[i]) for i in range(3, 7))
        f0, f1 = at("f0", [P, KT, T], F[0]), at("f1", [P, KT, T], F[2])
        proj = a012[:, :, :].rearrange("p (a b) n -> p a (b n)", b=2)
        vtok = at("vtok", [P, 2, D], A[3])
        mlp_hi = at("mlp_hi", [P, 16, T], A[0], f32r)
        mlp_lo = at("mlp_lo", [P, 16, T], A[2], f32r)
        relu = at("relu", [P, 2, 512], A[6])
        rsq = at("rsq", [P, 2, 512], A[6] + 4096)
        fox_s = at("fox_s", [P, 8, 384], A[5])
        fox_pt = at("fox_pt", [P, 8, 384], A[0])

        J_OUT1, J_UP, J_DOWN = 10, 14, 36
        J_LAYER = 44
        def JL(o):
            return o if o <= L_LRU else o - 1
        LAYER_J = 92

        def loop_part(n0, count):
            k = count // 4 * 4 - (4 if n0 + count + 2 > total and count % 4 == 0 else 0)
            return k if k >= 8 else 0

        def source(e):
            return e if e < 4 else 4 + (e - 4) // 7 * 6 + ((e - 4) % 7 - ((e - 4) % 7 > 4))

        @block.sync
        def _(sp):
            sp.dma_start(vec[:, :], io["vecs"]).then_inc(S("vec_loaded"), 16)
            sp.dma_start(cc[:, :], io["consts_common"]).then_inc(S("small_loaded"), 16)
            sp.dma_start(xc[:, :, :], io["ctxT"]).then_inc(S("small_loaded"), 16)
            sp.dma_start(x[:, :, :], io["xT"]).then_inc(S("small_loaded"), 16)
            sp.dma_start(cu[:, 0:N_CA], io["consts_a"]).then_inc(S("small_loaded"), 16)
            sp.dma_start(sw[:, :], io["small_w"]).then_inc(S("small_loaded"), 16)

            def load(n, s):
                sp.dma_start(raw[:, s:s + 1, :], io["stream"][bass.ds(n, 1)].rearrange("a p n -> p a n"))\
                  .then_inc(S(f"raw_loaded{s}"), 16)

            for s in range(RAW):
                load(s, s)
            rounds = total // RAW
            with sp.Fori(1, rounds) as i:
                for s in range(RAW):
                    sp.wait_ge(S("lo_ready"), i * RAW + (s - RAW + 1))
                    load(i * RAW + s, s)
            for n in range(rounds * RAW, total):
                sp.wait_ge(S("lo_ready"), n - RAW + 1)
                load(n, n % RAW)
            sp.wait_ge(S("x_new"), 2 + 2 * layers)
            sp.dma_start(io["out"], x[:, :, :]).then_inc(S("stored"), 16)
            sp.wait_ge(S("stored"), 16)

        @block.gpsimd
        def _(pool):
            order = Order(pool, "pool_order")

            def load(m, s):
                pool.dma_start(ada_raw[:, s:s + 1, :], io["ada"][bass.ds(m, 1)].rearrange("a p n -> p a n"))\
                    .then_inc(S(f"ada_loaded{s}"), 16)

            def chunk(half, s, which, more, early=False):
                m = half * 2 + s
                order.n = m * 4
                pool.wait_ge(S(f"ada_loaded{s}"), half * 16 + 16)
                if early:
                    pool.wait_ge(S("ctx_read"), m + 1)
                r = ada_raw[:, s, :].rearrange("p (k n) -> p k n", k=KT)
                order(nc.gpsimd.tensor_tensor(r, r, bc(cs[:, which, :], T), ALU.mult))
                order(nc.gpsimd.tensor_tensor(r[:, 0:4, :], r[:, 0:4, :], r[:, 4:8, :], ALU.add))
                order(nc.gpsimd.tensor_tensor(r[:, 0:2, :], r[:, 0:2, :], r[:, 2:4, :], ALU.add))
                if not (isinstance(half, int) and half == 0):
                    pool.wait_ge(S(f"ada_stored{s}"), half * 16)
                order(nc.gpsimd.tensor_tensor(ada_acc[:, s, :], r[:, 0, :], r[:, 1, :], ALU.add))
                pool.dma_start(io["ada_part"][bass.ds(m, 1)].rearrange("a p n -> p a n"), ada_acc[:, s:s + 1, :])\
                    .then_inc(S(f"ada_stored{s}"), 16)
                if more:
                    load(m + 2, s)

            load(0, 0)
            load(1, 1)
            pool.wait_ge(S("cs_ready"), 1)
            for half in range(4):
                for s in range(2):
                    chunk(half, s, 0, True, early=True)
            with pool.Fori(4, 12 if layers else 11) as i:
                for s in range(2):
                    chunk(i, s, 0, True)
            if layers:
                with pool.Fori(12, ADA_N // 2 - 1) as i:
                    for s in range(2):
                        chunk(i, s, 2, True)
            for s in range(2):
                chunk(ADA_N // 2 - 1, s, 2 if layers else 0, False)
            for s in range(2):
                pool.wait_ge(S(f"ada_stored{s}"), ADA_N // 2 * 16)

        @block.tensor
        def _(pe):
            mm, tr = nc.tensor.matmul, nc.tensor.transpose

            def mm3(out, ah, al, bh, bl, first, last):
                mm(out, ah, bh, start=first, stop=False)
                mm(out, ah, bl, start=False, stop=False)
                return mm(out, al, bh, start=False, stop=last)

            def begin(n, j, strict=False):
                pe.wait_ge(S("lo_ready"), n + 1)
                if j is None:
                    return
                if strict:
                    pe.wait_ge(S("evicted"), j)
                elif not isinstance(j, int) or j >= 2:
                    pe.wait_ge(S("evicted"), j - 1)

            def feat_chunk(wp, bank, s):
                for b in range(2):
                    for k in range(KT):
                        o = (b * KT + k) * P
                        last = mm3(ps[:, bank, b * T:(b + 1) * T], w_hi[:, wp, o:o + P], w_lo[:, wp, o:o + P],
                                   act_hi[s][:, k, :], act_lo[s][:, k, :], k == 0, k == KT - 1)
                return last

            def tok_chunk(wp, bank, s):
                for t in range(TT):
                    for k in range(KT):
                        last = mm3(ps[:, bank, t * T:(t + 1) * T], act_hi[s][:, k, t * P:(t + 1) * P],
                                   act_lo[s][:, k, t * P:(t + 1) * P], w_hi[:, wp, k * T:(k + 1) * T],
                                   w_lo[:, wp, k * T:(k + 1) * T], k == 0, k == KT - 1)
                return last

            def job(fn, n0, j0, count, s, strict=False):
                def four(i, m):
                    for c in range(m):
                        begin(i + (n0 + c), i + (j0 + c), strict and isinstance(i, int) and i + c == 0)
                        fn((n0 + c) % 2, (j0 + c) % 2, s).then_inc(S("chunk_done"), 1)
                if count >= 8:
                    if strict:
                        four(0, 4)
                        with pe.Fori(1, count // 4) as i:
                            four(i * 4, 4)
                    else:
                        with pe.Fori(0, count // 4) as i:
                            four(i * 4, 4)
                    if count % 4:
                        four(count // 4 * 4, count % 4)
                else:
                    four(0, count)

            def deep_chunk(wp, bank, s):
                for k in range(16):
                    last = mm3(ps[:, bank, 0:T], w_hi[:, wp, k * P:(k + 1) * P], w_lo[:, wp, k * P:(k + 1) * P],
                               mlp_hi[:, k, :], mlp_lo[:, k, :], k == 0, k == 15)
                return last

            def norm(k, sq):
                pe.wait_ge(S("norm_sq"), k + 1)
                for b in range(KT):
                    last = mm(ps[:, 7, 0:T], omean, sq[:, b, :], start=b == 0, stop=b == KT - 1)
                last.then_inc(S("norm_ms"), 1)

            def mods(k, src, cols, col0):
                pe.wait_ge(S("ada_in"), 16 * (k + 1))
                for c in range(cols):
                    o = c % 2 * P
                    last = mm(ps[:, 7, col0 + c:col0 + c + 1], src[:, c // 2, o:o + P], ones[:, 0:1],
                              start=True, stop=True)
                last.then_inc(S("mod_mm"), 1)

            pe.wait_ge(S("small_loaded"), 5 * 16)
            pe.wait_ge(S("ctx_acc_done"), 1)
            for c in range(16):
                last = mm(ps[:, 6, c:c + 1], ctx_acc[:, c // 2, c % 2 * P:c % 2 * P + P], ones[:, 0:1], start=True, stop=True)
            last.then_inc(S("modctx_mm"), 1)
            mods(0, ada_in1, 16, 0)
            pe.wait_ge(S("mods_done"), 1)
            norm(0, norm_sq1)
            pe.wait_ge(S("norm_std"), 1)
            norm(1, norm_sq1)
            pe.wait_ge(S("act_ready"), 4)
            job(feat_chunk, N_Q, 0, 2, 1)
            for c in range(4):
                n = N_KV + c
                begin(n, n)
                bank = n % 2 * 2
                if c == 0:
                    pe.wait_ge(S("evicted"), 2)
                feat_chunk(n % 2, bank, 0)
                feat_chunk(n % 2, bank + 1, 1).then_inc(S("chunk_done"), 1)
            job(feat_chunk, N_UZ, N_UZ, 4, 1, strict=True)
            pe.wait_ge(S("sw_lo"), 1)
            for t in range(4):
                s, tt = t // 2, t % 2
                for k in range(KT):
                    last = mm3(ps[:, 7, t * 16:t * 16 + 16], act_hi[s][:, k, tt * P:tt * P + P],
                               act_lo[s][:, k, tt * P:tt * P + P], sw_hi[:, k * 16:k * 16 + 16],
                               sw_lo[:, k * 16:k * 16 + 16], k == 0, k == KT - 1)
            last.then_inc(S("ab_mm"), 1)
            pe.wait_ge(S("y_ready"), 1)
            groups = [("k", t) for t in range(4)] + [("v", t) for t in range(4)] + [("q", t) for t in range(2)]
            for g, (kind, t) in enumerate(groups):
                if g >= 3:
                    pe.wait_ge(S("tr_ev"), g - 2)
                for h in range(HEADS):
                    src = y_q[:, h, t * P:(t + 1) * P] if kind == "q" else \
                        y_kv[:, h + (4 if kind == "v" else 0), t // 2, t % 2 * P:t % 2 * P + P]
                    last = tr(ps[:, 4 + g % 3, h * P:(h + 1) * P], src, ident)
                last.then_inc(S("tr_mm"), 1)
            pe.wait_ge(S("kq_norm"), 1)
            pe.wait_ge(S("tr_ev"), 10)
            for g in range(6):
                if g >= 3:
                    pe.wait_ge(S("trb_ev"), g - 2)
                for h in range(HEADS):
                    src = k_tok[:, g, h, :] if g < 4 else q_tok[:, g - 4, h, :]
                    last = tr(ps[:, 4 + g % 3, h * P:(h + 1) * P], src, ident)
                last.then_inc(S("trb_mm"), 1)
            pe.wait_ge(S("g_ready"), 1)
            g_ = sm[:, 1, :].rearrange("p (t c) -> p t c", t=4)
            tril = cu[:, A_TRIL:A_TRIL + P]
            for t in range(4):
                mm(ps[:, 7, t * 8:t * 8 + 4], triu, g_[:, t, 0:4], start=True, stop=True)
                mm(ps[:, 7, t * 8 + 4:t * 8 + 8], tril, g_[:, t, 4:8], start=True, stop=True)
                last = mm(ps[:, 7, 32 + t * 8:32 + t * 8 + 8], ones, g_[:, t, :], start=True, stop=True)
            last.then_inc(S("gc_mm"), 1)
            pe.wait_ge(S("trb_ev"), 6)
            pe.wait_ge(S("gc_ev"), 1)
            inv = 0
            seen_ev = 0
            for d in range(2):
                for t in range(4):
                    e = d * 4 + t
                    if e > 0:
                        pe.wait_ge(S("mat_ev"), e)
                    for h in range(HEADS):
                        mm(ps[:, 4, h * P:(h + 1) * P], kT[:, t, h, :], kT[:, t, h, :], start=True, stop=True)
                    if t >= 2:
                        for h in range(HEADS):
                            mm(ps[:, 5, h * P:(h + 1) * P], kT[:, t, h, :], qT[:, t - 2, h, :], start=True, stop=True)
                    for h in range(HEADS):
                        col = d * 4 + h
                        last = mm(ps[:, 6, h * P:(h + 1) * P], g_[:, t, col:col + 1].to_broadcast([P, P]),
                                  triu if d == 0 else tril, start=True, stop=True)
                    last.then_inc(S("mat_mm"), 1)
                pe.wait_ge(S("mat_ev"), 4 * (d + 1))
                pe.wait_ge(S("inv_init"), d + 1)
                for lvl in range(7):
                    size = 1 << lvl
                    pcol, rcol = (0, 1) if d == 0 else (1, 0)
                    def half(ap, which):
                        return ap.rearrange("p (g two s) -> p g two s", two=2, s=size)[:, :, which, :]
                    for g in range(4):
                        if lvl > 0:
                            pe.wait_ge(S("inv_u"), d * 28 + (lvl - 1) * 4 + g + 1)
                        for h in range(HEADS):
                            last = mm(ps[:, 4 + g, h * P:(h + 1) * P], Bm[:, g, h, :], Tm[:, g, h, :], start=True, stop=True)
                        last.then_inc(S("inv_x_mm"), 1)
                    for g in range(4):
                        pe.wait_ge(S("inv_x"), d * 28 + lvl * 4 + g + 1)
                        for h in range(HEADS):
                            if lvl < 6:
                                mm(ps[:, 4 + g, h * 64:(h + 1) * 64], U[:, d, g, h, :], half(X[:, g, h, :], pcol),
                                   start=True, stop=True)
                            last = mm(ps[:, 4 + g, 256 + h * 64:256 + (h + 1) * 64], X[:, g, h, :],
                                      half(U[:, d, g, h, :], rcol), start=True, stop=True)
                        last.then_inc(S("inv_u_mm"), 1)
                pe.wait_ge(S("inv_u"), d * 28 + 28)
            pe.wait_ge(S("scan_init"), 1)
            for st in range(4):
                for d in range(2):
                    e = st * 2 + d
                    t = (st if d == 0 else [1, 0, 3, 2][st])
                    if st > 0:
                        pe.wait_ge(S("scan_s"), e - 1)
                    for h in range(HEADS):
                        last = mm(ps[:, 4 + d, h * P:(h + 1) * P], kT[:, t, h, :], St[:, d, h, :], start=True, stop=True)
                    if t >= 2:
                        if st == 3:
                            pe.wait_ge(S("scan_o"), 2 * (d + 1))
                        for h in range(HEADS):
                            last = mm(ps[:, 6 + d, h * P:(h + 1) * P], qT[:, t - 2, h, :], St[:, d, h, :], start=True, stop=True)
                    last.then_inc(S("scan_p_mm"), 1)
                for d in range(2):
                    e = st * 2 + d
                    t = (st if d == 0 else [1, 0, 3, 2][st])
                    pe.wait_ge(S("scan_r"), e + 1)
                    for h in range(HEADS):
                        last = mm(ps[:, 4 + d, h * P:(h + 1) * P], U[:, d, t, h, :], Rm[:, d, h, :], start=True, stop=True)
                    last.then_inc(S("scan_w_mm"), 1)
                for d in range(2):
                    e = st * 2 + d
                    t = (st if d == 0 else [1, 0, 3, 2][st])
                    pe.wait_ge(S("scan_v"), e + 1)
                    for h in range(HEADS):
                        last = mm(ps[:, 4 + d, h * P:(h + 1) * P], k_tok[:, t, h, :], v2[:, d, h, :], start=True, stop=True)
                    if st >= 2:
                        pe.wait_ge(S("scan_o"), (st - 2) * 4 + d * 1 + 1)
                        for h in range(HEADS):
                            last = mm(ps[:, 6 + d, h * P:(h + 1) * P], attnT[:, d, t - 2, h, :], vn[:, d, h, :], start=True, stop=True)
                    last.then_inc(S("scan_s_mm"), 1)
            pe.wait_ge(S("scan_s"), 8)
            CC, SC = cu[:, A_CC:A_CC + P], cu[:, A_SC:A_SC + P]
            pe.wait_ge(S("scan_o"), 8)
            for g in range(4):
                wf = sw[:, SW_WF + g * P:SW_WF + (g + 1) * P]
                o = g % 2 * T
                mm(ps[:, 4 + g // 2, o:o + P], CC, wf, start=True, stop=True)
                last = mm(ps[:, 4 + g // 2, o + P:o + T], SC, wf, start=True, stop=True)
            last.then_inc(S("four_mm"), 1)
            pe.wait_ge(S("four_ev"), 1)
            for t in range(2):
                for g in range(4):
                    last = mm(ps[:, 4 + t * 2 + g // 2, g % 2 * T:g % 2 * T + T], uz[:, g, t * P:(t + 1) * P],
                              flat(m1[:, g, :, :]), start=True, stop=True)
            last.then_inc(S("four_mm"), 1)
            pe.wait_ge(S("four_ev"), 2)
            for g in range(4):
                for t in range(2):
                    for m, base in enumerate((A_CL, A_SL)):
                        last = mm(ps[:, 4 + g // 2, g % 2 * T:g % 2 * T + T], Z[:, t, g, m, :],
                                  cu[:, base + t * T:base + (t + 1) * T], start=(t + m == 0), stop=(t + m == 2))
            last.then_inc(S("four_mm"), 1)
            pe.wait_ge(S("o_norm"), 1)
            for h in range(HEADS):
                for t in range(2):
                    last = tr(ps[:, 6 + h // 2, h % 2 * T + t * P:h % 2 * T + t * P + P], o_tok[:, t, h, :], ident)
            last.then_inc(S("o_tr"), 1)
            pe.wait_ge(S("act_ready"), 6)
            mods(1, ada_in16, 32, 0)
            pe.wait_ge(S("mods_done"), 2)
            job(feat_chunk, N_OUT1, J_OUT1, 4, 1, strict=True)
            norm(2, norm_sq1)
            norm(3, norm_sq1)
            pe.wait_ge(S("act_ready"), 8)
            job(feat_chunk, N_UP, J_UP, FB, 1)
            pe.wait_ge(S("mid_ready"), FB)
            for o in range(KT):
                for k in range(FB):
                    i = o * FB + k
                    n, b = N_DOWN + i // 16, i % 16
                    if b == 0:
                        pe.wait_ge(S("lo_ready"), n + 1)
                    if k == 0:
                        pe.wait_ge(S("evicted"), J_DOWN + (o - 1 if o >= 1 else 0))
                    last = mm3(ps[:, o % 2, 0:T], w_hi[:, n % 2, b * P:(b + 1) * P], w_lo[:, n % 2, b * P:(b + 1) * P],
                               mid_hi1[:, k, :], mid_lo1[:, k, :], k == 0, k == FB - 1)
                    if b == 15:
                        last.then_inc(S("chunk_done"), 1)
            norm(4, sq_down)

            for L in range(layers):
                n0, j0 = N_LAYER + L * LAYER_CH, J_LAYER + L * LAYER_J
                ns, ar = 5 + 4 * L, 8 + 14 * L
                mods(2 + L, ada_in, 48, 0)
                pe.wait_ge(S("mods_done"), 3 + L)
                norm(ns, a6)
                pe.wait_ge(S("act_ready"), ar + 2)
                job(tok_chunk, n0 + L_RV, j0 + L_RV, 4, 1)
                job(feat_chunk, n0 + L_RQK, j0 + L_RQK, 12, 1)
                perm = cu[:, B_PERM:B_PERM + P]
                pe.wait_ge(S("consts_b"), 16)
                pe.wait_ge(S("evicted"), j0 + L_RETO)
                for b in range(8):
                    last = mm(ps[:, 4 + b // 2, b % 2 * T:b % 2 * T + T], perm, a0[:, b, :], start=True, stop=True)
                last.then_inc(S("rope_mm"), 1)
                pe.wait_ge(S("rope_done"), L + 1)
                for h in range(HEADS):
                    for m in range(2):
                        last = mm(ps[:, 4 + h, m * T:(m + 1) * T], a0[:, 4 + h, m * P:(m + 1) * P], a0[:, h, :],
                                  start=True, stop=True)
                last.then_inc(S("ret_s_mm"), 1)
                pe.wait_ge(S("ret_p"), L + 1)
                pt = a5[:, :, :]
                for t in range(2):
                    for h in range(HEADS):
                        out = ps[:, 4 + t * 2 + h // 2, h % 2 * T:h % 2 * T + T]
                        for m in range(t + 1):
                            last = mm(out, pt[:, h * 2 + m, t * P:(t + 1) * P], vtok[:, m, h * T:(h + 1) * T],
                                      start=m == 0, stop=m == t)
                last.then_inc(S("ret_o_mm"), 1)
                pe.wait_ge(S("ret_norm"), L + 1)
                o_ = a6[:, :, :].rearrange("p (t h) n -> p t h n", t=2)
                for b in range(8):
                    for t in range(2):
                        last = tr(ps[:, 4 + b // 2, b % 2 * T + t * P:b % 2 * T + t * P + P],
                                  o_[:, t, b // 2, b % 2 * P:b % 2 * P + P], ident)
                last.then_inc(S("ret_tr"), 1)
                pe.wait_ge(S("act_ready"), ar + 4)
                job(feat_chunk, n0 + L_RETO, j0 + L_RETO, 4, 0)
                job(feat_chunk, n0 + L_LX, j0 + L_LX, 12, 1)
                pe.wait_ge(S("act_ready"), ar + 6)
                n = n0 + L_LRU
                begin(n, j0 + JL(L_LRU), strict=True)
                for b in range(16):
                    bank = (4 if b < 8 else 0) + b % 8 // 2
                    last = mm3(ps[:, bank, b % 2 * T:b % 2 * T + T], w_hi[:, n % 2, b * P:(b + 1) * P],
                               w_lo[:, n % 2, b * P:(b + 1) * P], act_hi[0][:, b % 8, :], act_lo[0][:, b % 8, :], True, True)
                last.then_inc(S("chunk_done"), 1)
                pe.wait_ge(S("lru_ev"), 16 * (L + 1))
                pe.wait_ge(S("act_ready"), ar + 8)
                job(feat_chunk, n0 + L_LRUO, j0 + JL(L_LRUO), 4, 0)
                job(tok_chunk, n0 + L_FV, j0 + JL(L_FV), 4, 1)
                job(feat_chunk, n0 + L_FQK, j0 + JL(L_FQK), 12, 1)
                for t in range(2):
                    for k in range(KT):
                        o = SW_FF + L * 64 + k * 8
                        last = mm3(ps[:, 7, t * 8:t * 8 + 8], act_hi[1][:, k, t * P:(t + 1) * P],
                                   act_lo[1][:, k, t * P:(t + 1) * P], sw_hi[:, o:o + 8], sw_lo[:, o:o + 8],
                                   k == 0, k == KT - 1)
                last.then_inc(S("ff_mm"), 1)
                nlf = sm[:, 1, 0:16].rearrange("p (t h) -> p t h", t=2)
                pe.wait_ge(S("nlf_ready"), L + 1)
                mm(ps[:, 7, 16:24], triu, nlf[:, 0, :], start=True, stop=True)
                mm(ps[:, 7, 24:32], ones, nlf[:, 0, :], start=True, stop=False)
                mm(ps[:, 7, 24:32], triu, nlf[:, 1, :], start=False, stop=True).then_inc(S("cum_mm"), 1)
                pe.wait_ge(S("cum_ev"), L + 1)
                pe.wait_ge(S("evicted"), j0 + JL(L_FOXO))
                for h in range(8):
                    e = L * 8 + h
                    if h >= 4:
                        pe.wait_ge(S("fox_s_ev"), e - 3)
                    q, k, bank = a0[:, h, :], a1[:, h, :], 4 + h % 4
                    t0, t1 = ps[:, bank, 0:P], ps[:, bank, P:P + T]
                    mm(t0, q[:, 0:P], k[:, 0:P], start=True, stop=False)
                    mm(t0, nlf[:, 0, h:h + 1].to_broadcast([P, P]), triu, start=False, stop=True)
                    mm(t1, q[:, P:T], k, start=True, stop=False)
                    mm(t1, nlf[:, 0, h:h + 1].to_broadcast([P, P]), cc[:, C_TRIU:C_TRIU + T], start=False, stop=False)
                    mm(ps[:, bank, T:T + P], nlf[:, 1, h:h + 1].to_broadcast([P, P]), triu, start=False, stop=True)\
                        .then_inc(S("fox_s_mm"), 1)
                pe.wait_ge(S("fox_p"), L + 1)
                for h in range(8):
                    e = L * 8 + h
                    if h >= 4:
                        pe.wait_ge(S("fox_t_ev"), e - 3)
                    bank = 4 + h % 4
                    tr(ps[:, bank, 0:P], fox_s[:, h, 0:P], ident)
                    tr(ps[:, bank, P:2 * P], fox_s[:, h, P:2 * P], ident)
                    tr(ps[:, bank, 2 * P:3 * P], fox_s[:, h, 2 * P:3 * P], ident).then_inc(S("fox_t_mm"), 1)
                pe.wait_ge(S("fox_t_ev"), L * 8 + 8)
                for h in range(8):
                    o = h % 2 * T
                    v_ = vtok[:, :, h * P:(h + 1) * P]
                    mm(ps[:, 4 + h // 2, o:o + T], v_[:, 0, :], fox_pt[:, h, 0:T], start=True, stop=False)
                    last = mm(ps[:, 4 + h // 2, o + P:o + T], v_[:, 1, :], fox_pt[:, h, T:T + P], start=False, stop=True)
                last.then_inc(S("fox_o_mm"), 1)
                pe.wait_ge(S("act_ready"), ar + 10)
                job(feat_chunk, n0 + L_FOXO, j0 + JL(L_FOXO), 4, 0)
                pe.wait_ge(S("act_ready"), ar + 12)
                job(feat_chunk, n0 + L_WOUT, j0 + JL(L_WOUT), 4, 0)
                norm(ns + 1, a6)
                norm(ns + 2, a6)
                pe.wait_ge(S("act_ready"), ar + 14)
                for hf in range(2):
                    n = n0 + L_MLP + 16 * hf
                    j = j0 + JL(L_MLP) + 16 * hf
                    job(feat_chunk, n, j, 8, 1)
                    pe.wait_ge(S("mlp_ready"), 8 * (2 * L + hf + 1))
                    job(deep_chunk, n + 8, j + 8, 8, 1)
                norm(ns + 3, a6)

        @block.scalar
        def _(act):
            act_ = nc.scalar.activation

            def prep(n, s4, s2):
                if isinstance(n, int):
                    if n >= total:
                        return
                    rnd = n // RAW * 16 + 16
                    act.wait_ge(S(f"raw_loaded{s4}"), rnd)
                    if n >= 2:
                        act.wait_ge(S("chunk_done"), n - 1)
                else:
                    act.wait_ge(S(f"raw_loaded{s4}"), n[1])
                    act.wait_ge(S("chunk_done"), n[0] - 1)
                act_(w_hi[:, s2, :], raw[:, s4, :], ACT.Copy).then_inc(S("hi_ready"), 1)

            def evict(dst, bank, n_done, func=ACT.Copy, scale=1.0, src=None):
                act.wait_ge(S("chunk_done"), n_done + 1)
                act_(dst, ps[:, bank, :] if src is None else src, func, scale=scale).then_inc(S("evicted"), 1)

            def job(n0, j0, count, dst, func=ACT.Copy, scale=1.0, sl=slice(0, 512), hook=None):
                def four(i, m):
                    for c in range(m):
                        n = n0 + c + 2
                        if isinstance(i, int):
                            prep(i + n, (i + n) % RAW, (i + n) % 2)
                        else:
                            prep((i + n, i * (16 // RAW) + (n // RAW * 16 + 16)), n % RAW, n % 2)
                        if hook:
                            hook(i, c)
                        else:
                            evict(dst(i + c), (j0 + c) % 2, i + (n0 + c), func, scale, ps[:, (j0 + c) % 2, sl])
                looped = loop_part(n0, count)
                if looped:
                    with act.Fori(0, looped // 4) as i:
                        four(i * 4, 4)
                for r in range(looped, count, 4):
                    four(r, min(4, count - r))

            def norm(k, src, sq):
                act_(sq[:, :, :], src[:, :, :], ACT.Square).then_inc(S("norm_sq"), 1)
                act.wait_ge(S("norm_ms"), k + 1)
                act_(std[:, :], ps[:, 7, 0:T], ACT.Sqrt, bias=eps[:, :]).then_inc(S("norm_std"), 1)

            def split(e, src, hi):
                for hf in range(2):
                    act.wait_ge(S("split_src"), 2 * source(e) + hf + 1)
                    act_(hi[:, 4 * hf:4 * hf + 4, :], src[:, 4 * hf:4 * hf + 4, :], ACT.Copy).then_inc(S("split_hi"), 1)

            def load_ada(k, dst, first, count):
                last = first + count
                for s in range(2):
                    act.wait_ge(S(f"ada_stored{s}"), (last + 1 - s) // 2 * 16)
                act.dma_start(dst[:, :, :], io["ada_part"][first:last].rearrange("c p n -> p c n")).then_inc(S("ada_in"), 16)

            act.wait_ge(S("vec_loaded"), 16)
            act_(cth[:, :], vec[:, 0:3 * KT], ACT.Tanh, scale=0.5).then_inc(S("c_tanh"), 1)
            prep(0, 0, 0)
            prep(1, 1, 1)
            act.wait_ge(S("small_loaded"), 5 * 16)
            act_(sw_hi[:, :], sw[:, 0:256], ACT.Copy).then_inc(S("sw_hi"), 1)
            act.wait_ge(S("eps_set"), 1)
            load_ada(0, ada_in1, 0, 8)
            norm(0, xc, norm_sq1)
            act.wait_ge(S("norm_rstd"), 1)
            norm(1, x, norm_sq1)
            split(0, norm_h1, act_hi[0])
            split(1, norm_h1, act_hi[1])
            for c in range(2):
                n = N_Q + c
                prep(n + 2, (n + 2) % RAW, n % 2)
                act.wait_ge(S("chunk_done"), n + 1)
                if c == 0:
                    act.wait_ge(S("pads"), 3)
                act_(pre_q[:, 2 * c:2 * c + 2, 1:T + 1], ps[:, n % 2, :].rearrange("p (b t) -> p b t", b=2), ACT.Copy)\
                    .then_inc(S("evicted"), 1)
            for c in range(4):
                n = N_KV + c
                prep(n + 2, (n + 2) % RAW, n % 2)
                act.wait_ge(S("chunk_done"), n + 1)
                bank = n % 2 * 2
                act_(pre_kv[:, 2 * c:2 * c + 2, :, 1:T + 1],
                     ps[:, bank:bank + 2, :].rearrange("p s (b t) -> p b s t", b=2), ACT.Copy).then_inc(S("evicted"), 1)
            job(N_UZ, N_UZ, 4, lambda i: flat(uz[:, 2 * i:2 * i + 2, :]))
            act.wait_ge(S("conv"), 1)
            act_(th_kv[:, :, :, :], y_kv[:, :, :, :], ACT.Tanh, scale=0.5)
            act_(th_q[:, :, :], y_q[:, :, :], ACT.Tanh, scale=0.5).then_inc(S("conv_tanh"), 1)
            ab = sm[:, 0, :]
            act.wait_ge(S("ab_abs"), 1)
            act_(sm[:, 2, :], sm[:, 2, :], ACT.Tanh, scale=0.5)
            act_(sm[:, 3, :], sm[:, 3, :], ACT.Exp, scale=-1.0)
            act_(sm[:, 4, 0:8], V("a_log", 8), ACT.Exp).then_inc(S("ab_act"), 1)
            act.wait_ge(S("tr_ev"), 10)
            act_(sq_kq[:, :, :], k_tok[:, :, :, :].rearrange("p t h n -> p (t h) n"), ACT.Square)
            act_(sq_q[:, :, :], q_tok[:, :, :, :].rearrange("p t h n -> p (t h) n"), ACT.Square).then_inc(S("kq_sq"), 1)
            act.wait_ge(S("kq_ss"), 1)
            act_(sm[:, 5, 0:24], sm[:, 5, 0:24], ACT.Sqrt, scale=0.25, bias=eps[:, :]).then_inc(S("kq_std"), 1)
            for g in range(6):
                act.wait_ge(S("trb_mm"), g + 1)
                dst = kT[:, g, :, :] if g < 4 else qT[:, g - 4, :, :]
                act_(flat(dst), ps[:, 4 + g % 3, :], ACT.Copy).then_inc(S("trb_ev"), 1)
            act.wait_ge(S("gc_diff"), 1)
            act_(sm[:, 8:11, :], sm[:, 8:11, :], ACT.Exp).then_inc(S("gc_exp"), 1)
            for e in range(8):
                act.wait_ge(S("dec_min"), e + 1)
                act_(dec[:, :, :], dec[:, :, :], ACT.Exp).then_inc(S("dec_exp"), 1)
            act.wait_ge(S("scan_o"), 8)
            act_(th_z[:, :, :], uz[:, 4:8, :], ACT.Tanh, scale=0.5).then_inc(S("z_tanh"), 1)
            act_(o_sq[:, :, :], o_tok[:, :, :, :].rearrange("p t h n -> p (t h) n"), ACT.Square).then_inc(S("o_sq"), 1)
            act.wait_ge(S("o_ss"), 1)
            act_(sm[:, 5, 0:8], sm[:, 5, 0:8], ACT.Sqrt, scale=1.0 / P, bias=eps[:, :]).then_inc(S("o_std"), 1)
            act.wait_ge(S("four_mm"), 1)
            act_(m1[:, :, :, :].rearrange("p (a g) m n -> p a (g m n)", a=2), ps[:, 4:6, :], ACT.Copy).then_inc(S("four_ev"), 1)
            act.wait_ge(S("four_mm"), 2)
            act_(Z[:, :, :, :, :].rearrange("p t (a g) m n -> p (t a) (g m n)", a=2), ps[:, 4:8, :], ACT.Copy)\
                .then_inc(S("four_ev"), 1)
            act.wait_ge(S("four_mm"), 3)
            act.wait_ge(S("o_ss"), 1)
            act_(yfd[:, 0:4, :].rearrange("p (a b) t -> p a (b t)", a=2), ps[:, 4:6, :], ACT.Copy).then_inc(S("split_src"), 1)
            split(2, yfd, act_hi[1])
            load_ada(1, ada_in16, 8, 16)
            job(N_OUT1, J_OUT1, 4, lambda i: flat(y1[:, 2 * i:2 * i + 2, :]))
            act.wait_ge(S("evicted"), J_OUT1 + 4)
            norm(2, y1, norm_sq1)
            act.wait_ge(S("x_new"), 1)
            norm(3, x, norm_sq1)
            split(3, norm_h1, act_hi[1])
            def ffn_steps(i, c):
                n = N_UP + c
                s = n % 2
                e = i + c
                act.wait_ge(S("chunk_done"), i + (n + 1))
                act_(gpad[:, s, 1:ROWS + 1, 1:GRID_W + 1],
                     ps[:, (J_UP + c) % 2, T:2 * T].rearrange("p (r w) -> p r w", r=ROWS), ACT.Copy).then_inc(S("gate_in"), 1)
                act.wait_ge(S("gconv"), e + 1)
                act_(gth[:, s, :], gacc[:, s, :], ACT.Tanh, scale=0.5).then_inc(S("gate_tanh"), 1)
                act.wait_ge(S("evicted"), e + (J_UP + 1))
                act_(mid_hi1[:, bass.ds(e, 1), :], gm[:, s:s + 1, :], ACT.Copy).then_inc(S("mid_hi"), 1)
            act.wait_ge(S("gpad_zero"), 1)
            job(N_UP, J_UP, FB, None, hook=ffn_steps)
            outs = 0
            for c in range(11):
                n = N_DOWN + c
                prep(n + 2, (n + 2) % RAW, n % 2)
                while outs < KT and (outs * FB + FB - 1) // 16 == c:
                    evict(y_down[:, outs, :], outs % 2, n, src=ps[:, outs % 2, 0:T])
                    outs += 1
            act.wait_ge(S("evicted"), J_DOWN + 8)
            norm(4, y_down, sq_down)

            for L in range(layers):
                n0, j0 = N_LAYER + L * LAYER_CH, J_LAYER + L * LAYER_J
                ns, sp_ = 5 + 4 * L, 4 + 7 * L
                act.wait_ge(S("x_new"), 2 + 2 * L)
                if L == 0:
                    act.dma_start(cu[:, 0:N_CB], io["consts_b"]).then_inc(S("consts_b"), 16)
                load_ada(2 + L, ada_in, 24 * (L + 1), 24)
                norm(ns, x, a6)
                split(sp_, a5, act_hi[1])
                act.wait_ge(S("lam_abs"), L + 1)
                act_(sm[:, 3, 0:8], sm[:, 3, 0:8], ACT.Exp, scale=-1.0).then_inc(S("lam_exp"), 1)
                vdst = vtok[:, :, :]
                act.wait_ge(S("mods_done"), 3 + L)
                job(n0 + L_RV, j0 + L_RV, 4, lambda i: vdst[:, :, i * T:(i + 1) * T])
                job(n0 + L_RQK, j0 + L_RQK, 12, lambda i: proj[:, bass.ds(i, 1), :])
                act.wait_ge(S("ret_o_mm"), L + 1)
                act_(a6[:, :, :].rearrange("p (a b) n -> p a (b n)", a=4), ps[:, 4:8, :], ACT.Copy).then_inc(S("ret_o"), 1)
                act.wait_ge(S("ret_mean"), L + 1)
                act_(a0[:, :, :], a6[:, :, :], ACT.Square).then_inc(S("ret_sq"), 1)
                act.wait_ge(S("ret_ss"), L + 1)
                act_(sm[:, 5, 0:8], sm[:, 5, 0:8], ACT.Sqrt, scale=1.0 / T, bias=eps[:, :]).then_inc(S("ret_std"), 1)
                act_(a0[:, :, :], a1[:, :, :], ACT.Tanh, scale=0.5).then_inc(S("ret_gtanh"), 1)
                act_(a2[:, :, :], a2[:, :, :], ACT.Tanh, scale=0.5)
                split(sp_ + 1, a1, act_hi[0])
                job(n0 + L_RETO, j0 + L_RETO, 4, lambda i: flat(a5[:, 2 * i:2 * i + 2, :]))
                act.wait_ge(S("merge"), 2 * L + 1)
                job(n0 + L_LX, j0 + L_LX, 12, lambda i: proj[:, bass.ds(i, 1), :])
                split(sp_ + 2, a3, act_hi[0])
                n = n0 + L_LRU
                prep(n + 2, (n + 2) % RAW, n % 2)
                act.wait_ge(S("chunk_done"), n + 1)
                for b in range(16):
                    bank = (4 if b < 8 else 0) + b % 8 // 2
                    dst = a5 if b < 8 else a6
                    act_(dst[:, b % 8, :], ps[:, bank, b % 2 * T:b % 2 * T + T], ACT.Tanh, scale=0.5,
                         bias=gs[:, 3, b:b + 1] if b < 8 else sm[:, 4, b - 8:b - 7]).then_inc(S("lru_ev"), 1)
                act.wait_ge(S("lru_ev"), 16 * (L + 1))
                for b in range(8):
                    act_(a0[:, b, :], a5[:, b, :], ACT.Tanh, scale=sm[:, 6, 16 + b:17 + b], bias=sm[:, 6, 16 + b:17 + b])\
                        .then_inc(S("lru_th"), 1)
                act.wait_ge(S("lru_th"), 8 * (L + 1))
                for b in range(8):
                    act_(a5[:, b, :], a5[:, b, :], ACT.Exp, scale=sm[:, 6, 24 + b:25 + b], bias=sm[:, 6, 24 + b:25 + b])\
                        .then_inc(S("lru_a"), 1)
                act.wait_ge(S("lru_v"), L + 1)
                act_(a0[:, :, :], a0[:, :, :], ACT.Sqrt).then_inc(S("lru_sqrt"), 1)
                act.wait_ge(S("gelu_in"), L + 1)
                act_(f0[:, :, :], f0[:, :, :], ACT.Tanh, scale=math.sqrt(2.0 / math.pi)).then_inc(S("gelu_tanh"), 1)
                act_(a2[:, :, :], a2[:, :, :], ACT.Tanh, scale=0.5)
                split(sp_ + 3, a1, act_hi[0])
                job(n0 + L_LRUO, j0 + JL(L_LRUO), 4, lambda i: flat(a5[:, 2 * i:2 * i + 2, :]))
                act.wait_ge(S("merge"), 2 * L + 2)
                job(n0 + L_FV, j0 + JL(L_FV), 4, lambda i: vdst[:, :, i * T:(i + 1) * T])
                job(n0 + L_FQK, j0 + JL(L_FQK), 12, lambda i: proj[:, bass.ds(i, 1), :])
                act.wait_ge(S("ff_abs"), L + 1)
                act_(sm[:, 3, 0:16], sm[:, 3, 0:16], ACT.Exp, scale=-1.0).then_inc(S("ff_exp"), 1)
                act.wait_ge(S("fox_max"), L + 1)
                for h in range(8):
                    for t in range(2):
                        s_ = fox_s[:, h, 0:P] if t == 0 else fox_s[:, h, P:3 * P]
                        c = t * 8 + h
                        act_(s_, s_, ACT.Exp, scale=P ** -0.5, bias=sm[:, 7, c:c + 1], accum_out=sm[:, 7, 16 + c:17 + c]).then_inc(S("fox_e"), 1)
                for h in range(8):
                    act.wait_ge(S("fox_t_mm"), L * 8 + h + 1)
                    act_(fox_pt[:, h, :], ps[:, 4 + h % 4, 0:384], ACT.Copy).then_inc(S("fox_t_ev"), 1)
                act_(a2[:, :, :], a2[:, :, :], ACT.Tanh, scale=0.5)
                act.wait_ge(S("fox_o_mm"), L + 1)
                act_(a5[:, :, :].rearrange("p (a b) n -> p a (b n)", a=4), ps[:, 4:8, :], ACT.Copy).then_inc(S("fox_o"), 1)
                act.wait_ge(S("fox_o"), L + 1)
                for hf in range(2):
                    act_(act_hi[0][:, 4 * hf:4 * hf + 4, :], a5[:, 4 * hf:4 * hf + 4, :], ACT.Copy).then_inc(S("split_hi"), 1)
                job(n0 + L_FOXO, j0 + JL(L_FOXO), 4, lambda i: flat(a6[:, 2 * i:2 * i + 2, :]))
                split(sp_ + 5, a4, act_hi[0])
                job(n0 + L_WOUT, j0 + JL(L_WOUT), 4, lambda i: flat(a5[:, 2 * i:2 * i + 2, :]))
                act.wait_ge(S("evicted"), j0 + JL(L_MLP))
                norm(ns + 1, a5, a6)
                act.wait_ge(S("x_new"), 3 + 2 * L)
                norm(ns + 2, x, a6)
                split(sp_ + 6, a5, act_hi[1])
                act.wait_ge(S("mods_done"), 3 + L)
                for hf in range(2):
                    n = n0 + L_MLP + 16 * hf
                    j = j0 + JL(L_MLP) + 16 * hf

                    def mlp_steps(i, c, n=n, j=j, hf=hf):
                        s = (j + c) % 2
                        e = 8 * (2 * L + hf) + i + c
                        evict(relu[:, s, :], s, i + (n + c), ACT.Relu)
                        act.wait_ge(S("mlp_sq"), e + 1)
                        act_(mlp_hi[:, bass.ds((i + c) * 2, 2), :], rsq[:, s, :].rearrange("p (b t) -> p b t", b=2), ACT.Copy)\
                            .then_inc(S("mlp_hi"), 1)
                    job(n, j, 8, None, hook=mlp_steps)
                    dst = a4 if hf == 0 else a5
                    job(n + 8, j + 8, 8, lambda i: dst[:, bass.ds(i, 1), :], sl=slice(0, T))
                act.wait_ge(S("y_sum"), L + 1)
                norm(ns + 3, a5, a6)

        @block.vector
        def _(dve):
            order = Order(dve, "dve_order")
            tt, ts, stt = nc.vector.tensor_tensor, nc.vector.tensor_scalar, nc.vector.scalar_tensor_tensor
            red = nc.vector.tensor_reduce

            def prep(n, s4, s2):
                if isinstance(n, int) and n >= total:
                    return
                dve.wait_ge(S("hi_ready"), n + 1)
                tt(w_lo[:, s2, :], raw[:, s4, :], w_hi[:, s2, :].bitcast(f32), ALU.subtract).then_inc(S("lo_ready"), 1)

            def job(n0, count, hook=None):
                def four(i, m):
                    for c in range(m):
                        n = n0 + c + 2
                        prep(i + n, n % RAW, n % 2)
                        if hook:
                            hook(i, c)
                looped = loop_part(n0, count)
                if looped:
                    with dve.Fori(0, looped // 4) as i:
                        four(i * 4, 4)
                for r in range(looped, count, 4):
                    four(r, min(4, count - r))

            def rs(k, src, dst):
                dve.wait_ge(S("norm_std"), k + 1)
                nc.vector.reciprocal(rstd[:, :], std[:, :]).then_inc(S("norm_rstd"), 1)
                dve.wait_ge(S("norm_rstd"), k + 1)
                order(tt(dst[:, :, :], src[:, :, :], bmid(rstd[:, :], KT), ALU.mult))

            def split_lo(e, src, hi, lo):
                for hf in range(2):
                    o = slice(4 * hf, 4 * hf + 4)
                    dve.wait_ge(S("split_hi"), 2 * e + hf + 1)
                    tt(lo[:, o, :], src[:, o, :], hi[:, o, :].bitcast(f32), ALU.subtract).then_inc(S("act_ready"), 1)

            def modulate(k, e, src, dst, g, sh, hi, lo):
                rs(k, src, dst)
                for b in range(KT):
                    ins = ts(dst[:, b, :], dst[:, b, :], g[:, b:b + 1], sh[:, b:b + 1], ALU.mult, ALU.add)
                    if b % 4 == 3:
                        ins.then_inc(S("split_src"), 1)
                    else:
                        order.mark(ins)
                dve.wait_ge(S("split_src"), 2 * source(e) + 2)
                split_lo(e, dst, hi, lo)

            def residual(k, y, g):
                rs(k, y, y)
                for b in range(KT):
                    ins = stt(x[:, b, :], y[:, b, :], g[:, b:b + 1], x[:, b, :], ALU.mult, ALU.add)
                    if b == KT - 1:
                        ins.then_inc(S("x_new"), 1)
                    else:
                        order.mark(ins)

            def softplus(dst, z, e, m, n):
                t1, t2 = sm[:, 11, 0:n], z
                order(ts(t1, e, 2.0, None, ALU.add))
                order(nc.vector.reciprocal(t1, t1))
                order(tt(t2, e, t1, ALU.mult))
                order(tt(t1, t2, t2, ALU.mult))
                order(ts(e, t1, 1.0 / 17, 1.0 / 15, ALU.mult, ALU.add))
                for odd in (13, 11, 9, 7, 5, 3, 1):
                    order(tt(e, e, t1, ALU.mult))
                    order(ts(e, e, 1.0 / odd, None, ALU.add))
                order(tt(e, e, t2, ALU.mult))
                order(stt(dst, e, 2.0, m, ALU.mult, ALU.add))

            nc.vector.memset(eps[:, :], EPS).then_inc(S("eps_set"), 1)
            dve.wait_ge(S("c_tanh"), 1)
            c3 = cs[:, :, :].rearrange("p a k -> p (a k)")
            order(ts(cth[:, :], cth[:, :], 0.5, 0.5, ALU.mult, ALU.add))
            tt(c3, cth[:, :], vec[:, 0:3 * KT], ALU.mult).then_inc(S("cs_ready"), 1)
            dve.wait_ge(S("cs_ready"), 1)
            for m in range(8):
                s = m % 2
                dve.wait_ge(S(f"ada_loaded{s}"), (m // 2 + 1) * 16)
                r = ctx_prod[:, :].rearrange("p (k n) -> p k n", k=KT)
                tt(r, ada_raw[:, s, :].rearrange("p (k n) -> p k n", k=KT), bc(cs[:, 1, :], T), ALU.mult)\
                    .then_inc(S("ctx_read"), 1)
                dve.wait_ge(S("ctx_read"), m + 1)
                order(tt(r[:, 0:4, :], r[:, 0:4, :], r[:, 4:8, :], ALU.add))
                order(tt(r[:, 0:2, :], r[:, 0:2, :], r[:, 2:4, :], ALU.add))
                ins = tt(ctx_acc[:, m, :], r[:, 0, :], r[:, 1, :], ALU.add)
                if m < 7:
                    order(ins)
                else:
                    ins.then_inc(S("ctx_acc_done"), 1)
            prep(0, 0, 0)
            prep(1, 1, 1)
            dve.wait_ge(S("sw_hi"), 1)
            tt(sw_lo[:, :], sw[:, 0:256], sw_hi[:, :].bitcast(f32), ALU.subtract).then_inc(S("sw_lo"), 1)
            dve.wait_ge(S("modctx_mm"), 1)
            order(tt(mod_ctx[:, :], ps[:, 6, 0:16], V("b_ada", 16), ALU.add))
            dve.wait_ge(S("mod_mm"), 1)
            tt(mod[:, 0:16], ps[:, 7, 0:16], V("b_ada", 16), ALU.add).then_inc(S("mods_done"), 1)
            dve.wait_ge(S("mods_done"), 1)
            order(stt(gs[:, 0, :], mod_ctx[:, 8:16], 1.0, V("g_pre_mix", KT), ALU.add, ALU.mult))
            order(stt(gs[:, 1, :], mod[:, 8:16], 1.0, V("g_pre_mix", KT), ALU.add, ALU.mult))
            dve.wait_ge(S("norm_sq"), 1)
            modulate(0, 0, xc, norm_h1, gs[:, 0, :], mod_ctx[:, 0:8], act_hi[0], act_lo[0])
            dve.wait_ge(S("act_ready"), 2)
            modulate(1, 1, x, norm_h1, gs[:, 1, :], mod[:, 0:8], act_hi[1], act_lo[1])
            nc.vector.memset(pre_kv[:, :, :, 0:T + 2:T + 1], 0.0).then_inc(S("pads"), 1)
            nc.vector.memset(pre_q[:, :, 0:1], 0.0).then_inc(S("pads"), 1)
            nc.vector.memset(pre_q[:, :, T + 1:T + 2], 0.0).then_inc(S("pads"), 1)
            job(N_Q, 2)
            job(N_KV, 4)
            job(N_UZ, 4)
            dve.wait_ge(S("evicted"), 10)
            for b in range(4):
                w = lambda i: V("conv", 1, i * 12 + b)
                order(ts(y_q[:, b, :], pre_q[:, b, 0:T], w(0), None, ALU.mult))
                order(stt(y_q[:, b, :], pre_q[:, b, 1:T + 1], w(1), y_q[:, b, :], ALU.mult, ALU.add))
                order(stt(y_q[:, b, :], pre_q[:, b, 2:T + 2], w(2), y_q[:, b, :], ALU.mult, ALU.add))
            for b in range(8):
                w = lambda i: V("conv", 1, i * 12 + 4 + b)
                order(ts(y_kv[:, b, :, :], pre_kv[:, b, :, 0:T], w(0), None, ALU.mult))
                order(stt(y_kv[:, b, :, :], pre_kv[:, b, :, 1:T + 1], w(1), y_kv[:, b, :, :], ALU.mult, ALU.add))
                ins = stt(y_kv[:, b, :, :], pre_kv[:, b, :, 2:T + 2], w(2), y_kv[:, b, :, :], ALU.mult, ALU.add)
                if b < 7:
                    order.mark(ins)
                else:
                    ins.then_inc(S("conv"), 1)
            dve.wait_ge(S("ab_mm"), 1)
            abp = ps[:, 7, 0:64].rearrange("p (t c) -> p t c", t=4)
            s32 = lambda i: sm[:, i, :].rearrange("p (t c) -> p t c", t=4)
            order(nc.vector.tensor_copy(s32(2), abp[:, :, 0:8]))
            order(tt(s32(1), abp[:, :, 8:16], bmid(V("dt_bias", 8), 4), ALU.add))
            order(ts(s32(0), s32(1), 0.0, None, ALU.max))
            order(ts(sm[:, 3, :], sm[:, 1, :], -1.0, None, ALU.mult))
            tt(sm[:, 3, :], sm[:, 3, :], sm[:, 1, :], ALU.max).then_inc(S("ab_abs"), 1)
            dve.wait_ge(S("conv_tanh"), 1)
            order(stt(flat(y_q[:, :, :]), flat(th_q[:, :, :]), 1.0, flat(y_q[:, :, :]), ALU.add, ALU.mult))
            stt(flat(y_kv[:, :, :, :]), flat(th_kv[:, :, :, :]), 1.0, flat(y_kv[:, :, :, :]), ALU.add, ALU.mult).then_inc(S("y_ready"), 1)
            dve.wait_ge(S("ab_act"), 1)
            order(ts(sm[:, 2, :], sm[:, 2, :], 0.5, 0.5, ALU.mult, ALU.add))
            softplus(sm[:, 0, :], sm[:, 1, :], sm[:, 3, :], sm[:, 0, :], 32)
            tneg = sm[:, 4, 0:8]
            order(ts(tneg, tneg, -1.0, None, ALU.mult))
            tt(s32(1), s32(0), bmid(tneg, 4), ALU.mult).then_inc(S("g_ready"), 1)
            for g in range(10):
                dve.wait_ge(S("tr_mm"), g + 1)
                src = ps[:, 4 + g % 3, :]
                if g < 4:
                    ins = nc.vector.tensor_copy(flat(k_tok[:, g, :, :]), src)
                elif g < 8:
                    ins = ts(flat(v_tok[:, g - 4, :, :]), src, 0.5, None, ALU.mult)
                else:
                    ins = nc.vector.tensor_copy(flat(q_tok[:, g - 8, :, :]), src)
                ins.then_inc(S("tr_ev"), 1)
            dve.wait_ge(S("kq_sq"), 1)
            order(red(sm[:, 5, 0:16], sq_kq[:, :, :], AX, ALU.add))
            red(sm[:, 5, 16:24], sq_q[:, :, :], AX, ALU.add).then_inc(S("kq_ss"), 1)
            dve.wait_ge(S("kq_std"), 1)
            order(nc.vector.reciprocal(sm[:, 5, 0:24], sm[:, 5, 0:24]))
            order(ts(sm[:, 5, 0:16], sm[:, 5, 0:16], 0.5, None, ALU.mult))
            order(ts(sm[:, 5, 16:24], sm[:, 5, 16:24], 0.5 * P ** -0.5, None, ALU.mult))
            k3 = k_tok[:, :, :, :].rearrange("p t h n -> p (t h) n")
            q3 = q_tok[:, :, :, :].rearrange("p t h n -> p (t h) n")
            order(tt(k3, k3, bc(sm[:, 5, 0:16], P), ALU.mult))
            tt(q3, q3, bc(sm[:, 5, 16:24], P), ALU.mult).then_inc(S("kq_norm"), 1)
            dve.wait_ge(S("gc_mm"), 1)
            order(nc.vector.tensor_copy(sm[:, 6:8, :], ps[:, 7, 0:64].rearrange("p (a c) -> p a c", a=2)))
            order(nc.vector.tensor_copy(sm[:, 8:10, :], sm[:, 6:8, :]))
            tt(sm[:, 10, :], sm[:, 7, :], sm[:, 6, :], ALU.subtract).then_inc(S("gc_diff"), 1)
            dve.wait_ge(S("gc_exp"), 1)
            order(tt(sm[:, 10, :], sm[:, 10, :], sm[:, 2, :], ALU.mult))
            ts(sm[:, 7, :], sm[:, 8, :], -1.0, None, ALU.mult).then_inc(S("gc_ev"), 1)
            dve.wait_ge(S("gc_ev"), 1)
            tril = cu[:, A_TRIL:A_TRIL + P]
            for d in range(2):
                for t in range(4):
                    e = d * 4 + t
                    cols = slice(t * 8 + d * 4, t * 8 + d * 4 + 4)
                    dve.wait_ge(S("mat_mm"), e + 1)
                    if e > 0:
                        dve.wait_ge(S("mat_ev"), e)
                    b4, b5, b6 = (ps[:, i, :].rearrange("p (h n) -> p h n", h=4) for i in (4, 5, 6))
                    order(tt(dec[:, :, :], b6, bc(sm[:, 6, cols], P), ALU.subtract))
                    ts(dec[:, :, :], dec[:, :, :], 0.0, None, ALU.min).then_inc(S("dec_min"), 1)
                    dve.wait_ge(S("dec_exp"), e + 1)
                    order(tt(dem[:, :, :], dec[:, :, :], bmid(triu if d == 0 else tril, 4), ALU.mult))
                    order(tt(Bm[:, t, :, :], b4, dem[:, :, :], ALU.mult))
                    order(tt(Bm[:, t, :, :], Bm[:, t, :, :], bc(sm[:, 2, cols], P), ALU.mult))
                    if t >= 2:
                        order(tt(attnT[:, d, t - 2, :, :], b5, dem[:, :, :], ALU.mult))
                    strict = cu[:, A_STR + d * P:A_STR + (d + 1) * P]
                    tt(Bm[:, t, :, :], Bm[:, t, :, :], bmid(strict, 4), ALU.mult).then_inc(S("mat_ev"), 1)
                idb = bmid(ident, 16)
                order(nc.vector.tensor_copy(Tm[:, :, :, :].rearrange("p t h n -> p (t h) n"), idb))
                nc.vector.tensor_copy(U[:, d, :, :, :].rearrange("p t h n -> p (t h) n"), idb).then_inc(S("inv_init"), 1)
                dve.wait_ge(S("inv_init"), d + 1)
                for lvl in range(7):
                    size = 1 << lvl
                    pcol, rcol = (0, 1) if d == 0 else (1, 0)
                    mask = cu[:, A_LVL + (d * 7 + lvl) * P:A_LVL + (d * 7 + lvl + 1) * P]

                    def half(ap, which):
                        return ap.rearrange("p h (g two s) -> p h g two s", two=2, s=size)[:, :, :, which, :]
                    for g in range(4):
                        dve.wait_ge(S("inv_x_mm"), d * 28 + lvl * 4 + g + 1)
                        tt(X[:, g, :, :], ps[:, 4 + g, :].rearrange("p (h n) -> p h n", h=4), bmid(mask, 4), ALU.mult)\
                            .then_inc(S("inv_x"), 1)
                    for g in range(4):
                        dve.wait_ge(S("inv_u_mm"), d * 28 + lvl * 4 + g + 1)
                        b = ps[:, 4 + g, :].rearrange("p (w h g s) -> p w h g s", w=2, h=4, s=size)
                        if lvl < 6:
                            Tg = half(Tm[:, g, :, :], pcol)
                            order(tt(Tg, Tg, b[:, 0], ALU.subtract))
                        Ug = half(U[:, d, g, :, :], rcol)
                        tt(Ug, Ug, b[:, 1], ALU.subtract).then_inc(S("inv_u"), 1)
                dve.wait_ge(S("inv_u"), d * 28 + 28)
            order(nc.vector.memset(St[:, :, :, :], 0.0))
            nc.vector.memset(o_tok[:, :, :, :], 0.0).then_inc(S("scan_init"), 1)
            dve.wait_ge(S("scan_init"), 1)
            oc = 0
            for st in range(4):
                tile = lambda d: (st if d == 0 else [1, 0, 3, 2][st])
                cols = lambda d: slice(tile(d) * 8 + d * 4, tile(d) * 8 + d * 4 + 4)
                b4 = lambda i: ps[:, i, :].rearrange("p (h n) -> p h n", h=4)
                for d in range(2):
                    dve.wait_ge(S("scan_p_mm"), st * 2 + d + 1)
                    order(tt(Rm[:, d, :, :], b4(4 + d), bc(sm[:, 7, cols(d)], P), ALU.mult))
                    tt(Rm[:, d, :, :], Rm[:, d, :, :], v_tok[:, tile(d), :, :], ALU.add).then_inc(S("scan_r"), 1)
                if st >= 2:
                    for d in range(2):
                        order(tt(tmp_s[:, d, :, :], b4(6 + d), bc(sm[:, 8, cols(d)], P), ALU.mult))
                        o_ = o_tok[:, tile(d) - 2, :, :]
                        tt(o_, o_, tmp_s[:, d, :, :], ALU.add).then_inc(S("scan_o"), 1)
                        oc += 1
                        dve.wait_ge(S("scan_o"), oc)
                for d in range(2):
                    dve.wait_ge(S("scan_w_mm"), st * 2 + d + 1)
                    order(tt(vn[:, d, :, :], b4(4 + d), bc(sm[:, 2, cols(d)], P), ALU.mult))
                    tt(v2[:, d, :, :], b4(4 + d), bc(sm[:, 10, cols(d)], P), ALU.mult).then_inc(S("scan_v"), 1)
                for d in range(2):
                    dve.wait_ge(S("scan_s_mm"), st * 2 + d + 1)
                    if st >= 2:
                        o_ = o_tok[:, tile(d) - 2, :, :]
                        tt(o_, o_, b4(6 + d), ALU.add).then_inc(S("scan_o"), 1)
                        oc += 1
                        dve.wait_ge(S("scan_o"), oc)
                    order(tt(St[:, d, :, :], St[:, d, :, :], bc(sm[:, 9, cols(d)], P), ALU.mult))
                    tt(St[:, d, :, :], St[:, d, :, :], b4(4 + d), ALU.add).then_inc(S("scan_s"), 1)
                    dve.wait_ge(S("scan_s"), st * 2 + d + 1)
            dve.wait_ge(S("o_sq"), 1)
            red(sm[:, 5, 0:8], o_sq[:, :, :], AX, ALU.add).then_inc(S("o_ss"), 1)
            dve.wait_ge(S("z_tanh"), 1)
            order(stt(th_z[:, :, :], th_z[:, :, :], 1.0, uz[:, 4:8, :], ALU.add, ALU.mult))
            order(ts(th_z[:, :, :], th_z[:, :, :], 0.5, None, ALU.mult))
            dve.wait_ge(S("o_std"), 1)
            order(nc.vector.reciprocal(sm[:, 5, 0:8], sm[:, 5, 0:8]))
            o3 = o_tok[:, :, :, :].rearrange("p t h n -> p (t h) n")
            tt(o3, o3, bc(sm[:, 5, 0:8], P), ALU.mult).then_inc(S("o_norm"), 1)
            dve.wait_ge(S("o_tr"), 1)
            dve.wait_ge(S("split_src"), 5)
            stt(yfd[:, 4:8, :], ps[:, 6:8, :].rearrange("p a (b t) -> p (a b) t", b=2), V("g_gdn"), th_z[:, :, :],
                ALU.mult, ALU.mult).then_inc(S("split_src"), 1)
            dve.wait_ge(S("split_src"), 6)
            split_lo(2, yfd, act_hi[1], act_lo[1])
            dve.wait_ge(S("mod_mm"), 2)
            tt(mod[:, 16:48], ps[:, 7, 0:32], V("b_ada", 32, 16), ALU.add).then_inc(S("mods_done"), 1)
            dve.wait_ge(S("mods_done"), 2)
            order(tt(gs[:, 0, :], mod[:, 16:24], V("g_post_mix", KT), ALU.mult))
            order(stt(gs[:, 1, :], mod[:, 32:40], 1.0, V("g_pre_ffn", KT), ALU.add, ALU.mult))
            order(tt(gs[:, 2, :], mod[:, 40:48], V("g_post_ffn", KT), ALU.mult))
            job(N_OUT1, 4)
            residual(2, y1, gs[:, 0, :])
            dve.wait_ge(S("x_new"), 1)
            modulate(3, 3, x, norm_h1, gs[:, 1, :], mod[:, 24:32], act_hi[1], act_lo[1])
            dve.wait_ge(S("act_ready"), 8)
            nc.vector.memset(gpad[:, :, :, :], 0.0).then_inc(S("gpad_zero"), 1)
            FFN_MARKS = 9
            base = order.n

            def ffn_steps(i, c):
                s = (N_UP + c) % 2
                e = i + c
                order.n = base + e * FFN_MARKS
                dve.wait_ge(S("gate_in"), e + 1)
                acc = gacc[:, s, :].rearrange("p (r w) -> p r w", r=ROWS)
                for tap in range(9):
                    src = gpad[:, s, tap // 3:tap // 3 + ROWS, tap % 3:tap % 3 + GRID_W]
                    w = vec[:, bass.ds(e + (V1["dwc"] + tap * FB), 1)]
                    if tap == 0:
                        order(ts(acc, src, w, None, ALU.mult))
                    elif tap < 8:
                        order(stt(acc, src, w, acc, ALU.mult, ALU.add))
                    else:
                        stt(acc, src, w, acc, ALU.mult, ALU.add).then_inc(S("gconv"), 1)
                dve.wait_ge(S("gate_tanh"), e + 1)
                order(stt(gth[:, s, :], gth[:, s, :], 1.0, gacc[:, s, :], ALU.add, ALU.mult))
                stt(gm[:, s, :], gth[:, s, :], 0.5, ps[:, (J_UP + c) % 2, 0:T], ALU.mult, ALU.mult)\
                    .then_inc(S("evicted"), 1)
                dve.wait_ge(S("mid_hi"), e + 1)
                tt(mid_lo1[:, bass.ds(e, 1), :], gm[:, s:s + 1, :], mid_hi1[:, bass.ds(e, 1), :].bitcast(f32), ALU.subtract)\
                    .then_inc(S("mid_ready"), 1)
            job(N_UP, FB, hook=ffn_steps)
            order.n = base + FB * FFN_MARKS
            job(N_DOWN, 11)
            residual(4, y_down, gs[:, 2, :])
            dve.wait_ge(S("x_new"), 2)

            for L in range(layers):
                n0 = N_LAYER + L * LAYER_CH
                j0 = J_LAYER + L * LAYER_J
                ns, sp_ = 5 + 4 * L, 4 + 7 * L
                v = lambda name, n=1, i=0: V(name, n, i, L)
                order(ts(sm[:, 6, 8:16], v("lam", 8), -1.0, None, ALU.mult))
                order(ts(sm[:, 6, 0:8], sm[:, 6, 8:16], 0.0, None, ALU.max))
                tt(sm[:, 3, 0:8], sm[:, 6, 8:16], v("lam", 8), ALU.max).then_inc(S("lam_abs"), 1)
                order(ts(gs[:, 3, :], v("b_a", 8), 0.5, None, ALU.mult))
                order(ts(sm[:, 4, 0:8], v("b_x", 8), 0.5, None, ALU.mult))
                dve.wait_ge(S("mod_mm"), 3 + L)
                tt(mod[:, :], ps[:, 7, 0:48], v("b_ada", 48), ALU.add).then_inc(S("mods_done"), 1)
                dve.wait_ge(S("mods_done"), 3 + L)
                order(stt(gs[:, 0, :], mod[:, 8:16], 1.0, v("g_pre_mix", KT), ALU.add, ALU.mult))
                modulate(ns, sp_, x, a5, gs[:, 0, :], mod[:, 0:8], act_hi[1], act_lo[1])
                order(tt(gs[:, 0, :], mod[:, 16:24], v("g_post_mix", KT), ALU.mult))
                order(stt(gs[:, 1, :], mod[:, 32:40], 1.0, v("g_pre_mlp", KT), ALU.add, ALU.mult))
                order(tt(gs[:, 2, :], mod[:, 40:48], v("g_post_mlp", KT), ALU.mult))
                dve.wait_ge(S("lam_exp"), L + 1)
                softplus(sm[:, 6, 0:8], sm[:, 6, 8:16], sm[:, 3, 0:8], sm[:, 6, 0:8], 8)
                order(ts(sm[:, 6, 16:24], sm[:, 6, 0:8], LRU_C / 2, None, ALU.mult))
                order(ts(sm[:, 6, 24:32], sm[:, 6, 0:8], -LRU_C / 2, None, ALU.mult))
                job(n0 + L_RV, 4)
                job(n0 + L_RQK, 12)
                dve.wait_ge(S("consts_b"), 16)
                dve.wait_ge(S("evicted"), j0 + L_RETO)
                dve.wait_ge(S("rope_mm"), L + 1)
                cos, sin = cu[:, B_COS:B_COS + T], cu[:, B_SIN:B_SIN + T]
                order(tt(a5[:, :, :], ps[:, 4:8, :].rearrange("p a (b t) -> p (a b) t", b=2), bmid(sin, 8), ALU.mult))
                order(tt(a0[:, :, :], a0[:, :, :], bmid(cos, 8), ALU.mult))
                tt(a0[:, :, :], a0[:, :, :], a5[:, :, :], ALU.add).then_inc(S("rope_done"), 1)
                dve.wait_ge(S("ret_s_mm"), L + 1)
                tt(flat(a5[:, :, :]), ps[:, 4:8, :].rearrange("p a b -> p (a b)"), cu[:, B_RET:B_RET + 2048], ALU.mult)\
                    .then_inc(S("ret_p"), 1)
                dve.wait_ge(S("ret_o"), L + 1)
                order(red(sm[:, 5, 0:8], a6[:, :, :], AX, ALU.add))
                order(ts(sm[:, 5, 0:8], sm[:, 5, 0:8], 1.0 / T, None, ALU.mult))
                tt(a6[:, :, :], a6[:, :, :], bc(sm[:, 5, 0:8], T), ALU.subtract).then_inc(S("ret_mean"), 1)
                dve.wait_ge(S("ret_sq"), L + 1)
                red(sm[:, 5, 0:8], a0[:, :, :], AX, ALU.add).then_inc(S("ret_ss"), 1)
                dve.wait_ge(S("ret_std"), L + 1)
                order(nc.vector.reciprocal(sm[:, 5, 0:8], sm[:, 5, 0:8]))
                tt(a6[:, :, :], a6[:, :, :], bc(sm[:, 5, 0:8], T), ALU.mult).then_inc(S("ret_norm"), 1)
                dve.wait_ge(S("ret_gtanh"), L + 1)
                order(stt(a1[:, :, :], a0[:, :, :], 1.0, a1[:, :, :], ALU.add, ALU.mult))
                dve.wait_ge(S("ret_tr"), L + 1)
                for hf in range(2):
                    o = slice(4 * hf, 4 * hf + 4)
                    stt(flat(a1[:, o, :]), ps[:, 4 + 2 * hf:6 + 2 * hf, :].rearrange("p a b -> p (a b)"), 0.5, flat(a1[:, o, :]),
                        ALU.mult, ALU.mult).then_inc(S("split_src"), 1)
                split_lo(sp_ + 1, a1, act_hi[0], act_lo[0])
                job(n0 + L_RETO, 4)
                dve.wait_ge(S("evicted"), j0 + L_LX)
                stt(a4[:, :, :], a2[:, :, :], 1.0, a5[:, :, :], ALU.add, ALU.mult).then_inc(S("merge"), 1)
                dve.wait_ge(S("merge"), 2 * L + 1)
                job(n0 + L_LX, 12)
                dve.wait_ge(S("evicted"), j0 + JL(L_LRU))
                for tap in range(3, -1, -1):
                    back = 3 - tap
                    for b in range(8):
                        w = v("conv_w", 1, tap * 8 + b)
                        if tap == 0:
                            ins = stt(a3[:, b, back:T], a0[:, b, 0:T - back], w, a3[:, b, back:T], ALU.mult, ALU.add)
                            if b % 4 == 3:
                                ins.then_inc(S("split_src"), 1)
                            else:
                                order.mark(ins)
                        elif tap == 3:
                            order.mark(ts(a3[:, b, :], a0[:, b, :], w, v("conv_b", 1, b), ALU.mult, ALU.add))
                        else:
                            order.mark(stt(a3[:, b, back:T], a0[:, b, 0:T - back], w, a3[:, b, back:T], ALU.mult, ALU.add))
                    dve.wait_ge(S("dve_order"), order.n)
                split_lo(sp_ + 2, a3, act_hi[0], act_lo[0])
                prep(n0 + L_LRU + 2, (n0 + L_LRU + 2) % RAW, (n0 + L_LRU) % 2)
                dve.wait_ge(S("lru_ev"), 16 * (L + 1))
                order(stt(a6[:, :, :], a6[:, :, :], 1.0, a3[:, :, :], ALU.add, ALU.mult))
                dve.wait_ge(S("lru_a"), 8 * (L + 1))
                order(tt(f0[:, :, :], a5[:, :, :], a5[:, :, :], ALU.mult))
                order(stt(a0[:, :, :], f0[:, :, :], 1.0, a0[:, :, :], ALU.add, ALU.mult))
                ts(a0[:, :, :], a0[:, :, :], 0.0, None, ALU.max).then_inc(S("lru_v"), 1)
                order(tt(f0[:, :, :], a1[:, :, :], a1[:, :, :], ALU.mult))
                order(ts(f0[:, :, :], f0[:, :, :], 0.044715, 1.0, ALU.mult, ALU.add))
                tt(f0[:, :, :], f0[:, :, :], a1[:, :, :], ALU.mult).then_inc(S("gelu_in"), 1)
                dve.wait_ge(S("lru_sqrt"), L + 1)
                order(stt(a6[:, :, :], a6[:, :, :], 0.5, a0[:, :, :], ALU.mult, ALU.mult))
                for b in range(8):
                    order.mark(nc.vector.tensor_tensor_scan(a0[:, b, :], a5[:, b, :], a6[:, b, :], 0.0, ALU.mult, ALU.add))
                dve.wait_ge(S("dve_order"), order.n)
                dve.wait_ge(S("gelu_tanh"), L + 1)
                order(stt(f0[:, :, :], f0[:, :, :], 1.0, a1[:, :, :], ALU.add, ALU.mult))
                for hf in range(2):
                    o = slice(4 * hf, 4 * hf + 4)
                    stt(a1[:, o, :], f0[:, o, :], 0.5, a0[:, o, :], ALU.mult, ALU.mult).then_inc(S("split_src"), 1)
                split_lo(sp_ + 3, a1, act_hi[0], act_lo[0])
                job(n0 + L_LRUO, 4)
                dve.wait_ge(S("evicted"), j0 + JL(L_FV))
                order(stt(a5[:, :, :], a2[:, :, :], 1.0, a5[:, :, :], ALU.add, ALU.mult))
                tt(a4[:, :, :], a4[:, :, :], a5[:, :, :], ALU.add).then_inc(S("merge"), 1)
                dve.wait_ge(S("merge"), 2 * L + 2)
                job(n0 + L_FV, 4)
                job(n0 + L_FQK, 12)
                dve.wait_ge(S("ff_mm"), L + 1)
                y16 = sm[:, 1, 0:16].rearrange("p (t h) -> p t h", t=2)
                order(tt(y16, ps[:, 7, 0:16].rearrange("p (t h) -> p t h", t=2), bmid(v("b_f", 8), 2), ALU.add))
                order(ts(sm[:, 2, 0:16], sm[:, 1, 0:16], -1.0, None, ALU.mult))
                order(ts(sm[:, 0, 0:16], sm[:, 2, 0:16], 0.0, None, ALU.max))
                tt(sm[:, 3, 0:16], sm[:, 2, 0:16], sm[:, 1, 0:16], ALU.max).then_inc(S("ff_abs"), 1)
                dve.wait_ge(S("ff_exp"), L + 1)
                softplus(sm[:, 0, 0:16], sm[:, 2, 0:16], sm[:, 3, 0:16], sm[:, 0, 0:16], 16)
                ts(sm[:, 1, 0:16], sm[:, 0, 0:16], math.sqrt(P), None, ALU.mult).then_inc(S("nlf_ready"), 1)
                dve.wait_ge(S("cum_mm"), L + 1)
                ts(sm[:, 5, 0:16], ps[:, 7, 16:32], -1.0, None, ALU.mult).then_inc(S("cum_ev"), 1)
                dve.wait_ge(S("cum_ev"), L + 1)
                fm = cu[:, B_FM:B_FM + T]
                dve.wait_ge(S("evicted"), j0 + JL(L_FOXO))
                for h in range(8):
                    e = L * 8 + h
                    bank = 4 + h % 4
                    dve.wait_ge(S("fox_s_mm"), e + 1)
                    order.mark(stt(fox_s[:, h, 0:P], ps[:, bank, 0:P], sm[:, 5, h:h + 1], fm[:, P:T], ALU.add, ALU.add))
                    stt(fox_s[:, h, P:3 * P], ps[:, bank, P:3 * P], sm[:, 5, 8 + h:9 + h], fm, ALU.add, ALU.add)\
                        .then_inc(S("fox_s_ev"), 1)
                dve.wait_ge(S("fox_s_ev"), L * 8 + 8)
                dve.wait_ge(S("dve_order"), order.n)
                order(red(sm[:, 7, 0:8], fox_s[:, :, 0:P], AX, ALU.max, negate=True))
                order(red(sm[:, 7, 8:16], fox_s[:, :, P:3 * P], AX, ALU.max, negate=True))
                ts(sm[:, 7, 0:16], sm[:, 7, 0:16], P ** -0.5, None, ALU.mult).then_inc(S("fox_max"), 1)
                dve.wait_ge(S("fox_e"), 16 * (L + 1))
                order(nc.vector.reciprocal(sm[:, 7, 16:32], sm[:, 7, 16:32]))
                order.mark(tt(fox_s[:, :, 0:P], fox_s[:, :, 0:P], bc(sm[:, 7, 16:24], P), ALU.mult))
                dve.wait_ge(S("dve_order"), order.n)
                tt(fox_s[:, :, P:3 * P], fox_s[:, :, P:3 * P], bc(sm[:, 7, 24:32], T), ALU.mult).then_inc(S("fox_p"), 1)
                dve.wait_ge(S("fox_o"), L + 1)
                split_lo(sp_ + 4, a5, act_hi[0], act_lo[0])
                job(n0 + L_FOXO, 4)
                dve.wait_ge(S("evicted"), j0 + JL(L_WOUT))
                order(stt(a6[:, :, :], a2[:, :, :], 1.0, a6[:, :, :], ALU.add, ALU.mult))
                order(tt(a4[:, :, :], a4[:, :, :], a6[:, :, :], ALU.add))
                for hf in range(2):
                    o = slice(4 * hf, 4 * hf + 4)
                    ts(a4[:, o, :], a4[:, o, :], 0.5, None, ALU.mult).then_inc(S("split_src"), 1)
                split_lo(sp_ + 5, a4, act_hi[0], act_lo[0])
                job(n0 + L_WOUT, 4)
                residual(ns + 1, a5, gs[:, 0, :])
                dve.wait_ge(S("x_new"), 3 + 2 * L)
                modulate(ns + 2, sp_ + 6, x, a5, gs[:, 1, :], mod[:, 24:32], act_hi[1], act_lo[1])
                for hf in range(2):
                    n = n0 + L_MLP + 16 * hf
                    j = j0 + JL(L_MLP) + 16 * hf

                    def mlp_steps(i, c, j=j, hf=hf):
                        s = (j + c) % 2
                        e = 8 * (2 * L + hf) + i + c
                        dve.wait_ge(S("evicted"), i + (j + c + 1))
                        tt(rsq[:, s, :], relu[:, s, :], relu[:, s, :], ALU.mult).then_inc(S("mlp_sq"), 1)
                        dve.wait_ge(S("mlp_hi"), e + 1)
                        b = bass.ds((i + c) * 2, 2)
                        tt(mlp_lo[:, b, :], rsq[:, s, :].rearrange("p (b t) -> p b t", b=2), mlp_hi[:, b, :].bitcast(f32),
                           ALU.subtract).then_inc(S("mlp_ready"), 1)
                    job(n, 8, hook=mlp_steps)
                    job(n + 8, 8)
                dve.wait_ge(S("evicted"), j0 + LAYER_J)
                tt(a5[:, :, :], a5[:, :, :], a4[:, :, :], ALU.add).then_inc(S("y_sum"), 1)
                dve.wait_ge(S("y_sum"), L + 1)
                residual(ns + 3, a5, gs[:, 2, :])
                dve.wait_ge(S("x_new"), 4 + 2 * L)
        return print_left


def _constants():
    i = np.arange(P)
    triu = (i[:, None] <= i[None, :]).astype(np.float64)
    common = np.zeros((P, N_COMMON))
    common[:, C_ID:C_ID + P] = np.eye(P)
    common[:, C_TRIU:C_TRIU + P] = triu
    common[:, C_ONES:C_ONES + P] = 1.0
    common[:, C_OMEAN:C_OMEAN + P] = 1.0 / D
    a = np.zeros((P, N_CU))
    a[:, A_TRIL:A_TRIL + P] = triu.T
    a[:, A_STR:A_STR + P] = triu - np.eye(P)
    a[:, A_STR + P:A_STR + 2 * P] = triu.T - np.eye(P)
    for lvl in range(7):
        size = 1 << lvl
        group, second = i // (2 * size), i % (2 * size) >= size
        m = (group[:, None] == group[None, :]) & second[:, None] & ~second[None, :]
        a[:, A_LVL + lvl * P:A_LVL + (lvl + 1) * P] = m
        a[:, A_LVL + (7 + lvl) * P:A_LVL + (8 + lvl) * P] = m.T
    ang = 2 * np.pi * (i[:, None] * i[None, :] % P) / P
    a[:, A_CC:A_CC + P], a[:, A_SC:A_SC + P] = np.cos(ang), np.sin(ang)
    t = np.arange(T)
    ang = 2 * np.pi * (t[:, None] * t[None, :] % T) / T
    norm = 1.0 / math.sqrt(T * P)
    for tile in range(TT):
        a[:, A_CL + tile * T:A_CL + (tile + 1) * T] = np.cos(ang[tile * P:(tile + 1) * P]) * norm
        a[:, A_SL + tile * T:A_SL + (tile + 1) * T] = -np.sin(ang[tile * P:(tile + 1) * P]) * norm
    b = np.zeros((P, N_CU))
    b[:, B_PERM:B_PERM + P] = np.roll(np.eye(P), P // 2, axis=0)
    half = P // 2
    inv = np.float32(10000.0) ** (-np.arange(half, dtype=np.float32) / np.float32(half))
    ang = (inv[:, None] * t[None, :].astype(np.float32)).astype(np.float64)
    b[:, B_COS:B_COS + T] = np.concatenate([np.cos(ang)] * 2)
    b[:, B_SIN:B_SIN + T] = np.concatenate([-np.sin(ang), np.sin(ang)])
    for h in range(HEADS):
        gamma = 1.0 - 2.0 ** (-5.0 - h)
        w = gamma ** np.abs(t[:, None] - t[None, :]) * P ** -0.5
        w = np.where(t[:, None] // 64 <= t[None, :] // 64, w, 0.0)
        for m in range(TT):
            o = B_RET + (h * 2 + m) * T
            b[:, o:o + T] = w[m * P:(m + 1) * P]
    b[:, B_FM + P:B_FM + T] = np.where(i[None, :] <= i[:, None], 0.0, -1e30)
    return common.astype(np.float32), a.astype(np.float32), b.astype(np.float32)


def _columns_of(v):
    return np.asarray(v).reshape(-1, P).T


def _feat(w):
    k, n = w.shape
    c = w.reshape(k // P, P, n // P, P).transpose(2, 1, 0, 3)
    per = CH // (k // P * P)
    return c.reshape(-1, per, P, k // P * P).transpose(0, 2, 1, 3).reshape(-1, P, CH)


def _tok(w):
    n = w.shape[1]
    return w.reshape(KT, P, n // T, T).transpose(2, 1, 0, 3).reshape(-1, P, CH)


def _stream(a):
    w = np.asarray(a["w_in"])[0]
    u, q, k, v, z = w[:, 0:512], w[:, 512:1024], w[:, 1024:1536], w[:, 1536:2048], w[:, 2048:2560]
    parts = [_feat(q), _feat(k), _feat(v), _feat(u), _feat(z), _feat(np.asarray(a["w_out"])[0])]
    up = np.asarray(a["w_up"])[0].reshape(D, 2, FB, P).transpose(0, 2, 1, 3).reshape(D, 2 * D_FF)
    parts.append(_feat(up))
    down = np.asarray(a["w_down"])[0].reshape(FB, P, KT, P).transpose(2, 0, 1, 3).reshape(-1, 16, P, P)
    parts.append(down.transpose(0, 2, 1, 3).reshape(-1, P, CH))
    for L in range(LAYERS):
        g = lambda name: np.asarray(a[name])[L]
        w = g("w_in_2")
        cut = np.cumsum([0, 512, 512, 1024, 1024, 1024, 1024, 1024, 1024, 1024, 8, 3072])
        rq, rk, rv, rg, lx, ly, fq, fk, fv, ff, gates = (w[:, cut[i]:cut[i + 1]] for i in range(11))
        g0, g1, g2 = gates[:, 0:D], gates[:, D:2 * D], gates[:, 2 * D:]
        lru = np.concatenate([g("lru_w_a_2"), g("lru_w_x_2")]).transpose(1, 0, 2).reshape(1, P, CH)
        parts += [_tok(rv), _feat(rq), _feat(rk), _feat(rg), _feat(g0), _feat(g("ret_w_o_2")),
                  _feat(lx), _feat(ly), _feat(g1), lru, _feat(g("lru_w_o_2")),
                  _tok(fv), _feat(fq), _feat(fk), _feat(g2), _feat(g("fox_w_o_2")), _feat(g("w_out_2"))]
        w1, w2 = g("mlp_w1_2"), g("mlp_w2_2")
        for hf in range(2):
            parts += [_feat(w1[:, hf * 2048:(hf + 1) * 2048]), _feat(w2[hf * 2048:(hf + 1) * 2048])]
    return np.concatenate(parts)


def _vectors(a):
    out = np.zeros((P, NV), np.float32)

    def put(at, v):
        out[:, at:at + v.shape[1]] = v
    rows = lambda v: np.broadcast_to(np.asarray(v).reshape(1, -1), (P, np.asarray(v).size))
    for name in ("c", "c_ctx", "c_2", "b_ada", "g_pre_mix", "g_post_mix", "g_pre_ffn", "g_post_ffn", "g_gdn"):
        put(V1[name], _columns_of(a[name]))
    put(V1["conv"], _columns_of(a["w_qkv_conv"]))
    put(V1["dwc"], _columns_of(a["w_dwc"]))
    put(V1["dt_bias"], rows(a["dt_bias"]))
    put(V1["a_log"], rows(a["a_log"]))
    for L in range(LAYERS):
        at = VEC_FIRST + L * VEC_LAYER
        for name, key in (("b_ada", "ada_b_2"), ("g_pre_mix", "norm_pre_mix_2"), ("g_post_mix", "norm_post_mix_2"),
                          ("g_pre_mlp", "norm_pre_mlp_2"), ("g_post_mlp", "norm_post_mlp_2"), ("conv_w", "conv_w_2"),
                          ("conv_b", "conv_b_2"), ("b_a", "lru_b_a_2"), ("b_x", "lru_b_x_2"), ("lam", "lru_lambda_2")):
            put(at + VL[name], _columns_of(np.asarray(a[key])[L]))
        put(at + VL["b_f"], rows(np.asarray(a["fox_b_f_2"])[L]))
    return out


def arrays_of(inputs):
    a = {k: np.asarray(v) for k, v in inputs.items()}
    common, ca, cb = _constants()
    small = np.zeros((P, N_SW), np.float32)
    small[:, SW_AB:SW_AB + 128] = a["w_in"][0][:, 2560:2576].reshape(KT, P, 16).transpose(1, 0, 2).reshape(P, 128)
    for L in range(LAYERS):
        ff = a["w_in_2"][L][:, 8192:8200]
        small[:, SW_FF + L * 64:SW_FF + (L + 1) * 64] = ff.reshape(KT, P, 8).transpose(1, 0, 2).reshape(P, 64)
    small[:, SW_WF:] = a["w_fourier"][0].transpose(1, 0, 2).reshape(P, 512)
    ada = np.concatenate([_tok(a["w_ada"][0])] + [_tok(a["ada_w_2"][L]) for L in range(LAYERS)])
    feat = lambda t: np.ascontiguousarray(t[0].reshape(T, KT, P).transpose(2, 1, 0))
    return {"xT": feat(a["x"]), "ctxT": feat(a["ctx"]), "stream": _stream(a), "ada": ada, "small_w": small,
            "vecs": _vectors(a), "consts_common": common, "consts_a": ca[:, :N_CA], "consts_b": cb[:, :N_CB]}


def kernel(**inputs):
    import concourse.bacc as bacc
    from concourse.bass_utils import run_bass_kernel_spmd

    nc = bacc.Bacc("TRN2", target_bir_lowering=False, num_devices=1)
    arrays = {k: np.ascontiguousarray(v) for k, v in arrays_of(inputs).items()}
    io = {k: nc.dram_tensor(k, v.shape, mybir.dt.float32, kind="ExternalInput").ap() for k, v in arrays.items()}
    io["out"] = nc.dram_tensor("out", [P, KT, T], mybir.dt.float32, kind="ExternalOutput").ap()
    io["ada_part"] = nc.dram_tensor("ada_part", [24 * (1 + LAYERS), P, T], mybir.dt.float32).ap()
    build_program(nc, io)
    got = run_bass_kernel_spmd(nc, [arrays], core_ids=[0]).results[0]["out"]
    return np.ascontiguousarray(np.asarray(got).reshape(P, KT, T).transpose(2, 1, 0)).reshape(1, T, D)
```

```python
import math
from contextlib import ExitStack

import numpy as np

import concourse.bass as bass
from concourse import mybir

P = 128
D = 1024
KT = D // P
T = 256
TT = T // P
EPS = 1e-6
CH = 2048
RAW = 4
D_FF = 2816
FB = D_FF // P
GRID_W = 64
ROWS = T // GRID_W
HEADS = 4
MLP_B = 4096 // P
LRU_C = 8.0

N_Q, N_KV, N_UZ = 0, 2, 6
N_OUT1, N_UP, N_DOWN = 10, 14, 36
N_LAYER = 47
(L_FQK, L_FV, L_G2, L_RQK, L_RV, L_LX, L_FOXO, L_LY, L_LRU, L_RG, L_G1, L_G0, L_RETO, L_LRUO, L_WOUT, L_MLP) = (
    0, 8, 12, 16, 20, 24, 28, 32, 36, 37, 41, 45, 49, 53, 57, 61)
LAYER_CH = 93
LAYERS = 2

V1 = {}
VL = {}


def _columns():
    at = 0
    for name, n in (("c", KT), ("c_ctx", KT), ("c_2", KT), ("b_ada", 48), ("g_pre_mix", KT), ("g_post_mix", KT),
                    ("g_pre_ffn", KT), ("g_post_ffn", KT), ("conv", 36), ("g_gdn", 1), ("dwc", 9 * FB),
                    ("dt_bias", 8), ("a_log", 8)):
        V1[name] = at
        at += n
    first = at
    at = 0
    for name, n in (("b_ada", 48), ("g_pre_mix", KT), ("g_post_mix", KT), ("g_pre_mlp", KT), ("g_post_mlp", KT),
                    ("conv_w", 32), ("conv_b", 8), ("b_a", 8), ("b_x", 8), ("lam", 8), ("b_f", 8)):
        VL[name] = at
        at += n
    return first, at


VEC_FIRST, VEC_LAYER = _columns()
NV = VEC_FIRST + LAYERS * VEC_LAYER

C_ID, C_TRIU, C_ONES, C_OMEAN = 0, 128, 256, 384
N_COMMON = 512
A_TRIL, A_STR, A_LVL, A_CC, A_SC, A_CL, A_SL = 0, 128, 384, 384 + 14 * 128, 384 + 15 * 128, 384 + 16 * 128, 384 + 16 * 128 + 512
N_CA = A_SL + 512
B_PERM, B_COS, B_SIN, B_RET, B_FM = 0, 128, 384, 640, 640 + 2048
N_CB = B_FM + 256
N_CU = max(N_CA, N_CB)
SW_AB, SW_FF, SW_WF = 0, 128, 256
N_SW = 768


def build_program(nc, io, layers=LAYERS):
    f32, f32r = mybir.dt.float32, mybir.dt.float32r
    ALU, ACT, AX = mybir.AluOpType, mybir.ActivationFunctionType, mybir.AxisListType.X
    total = N_LAYER + LAYER_CH * layers
    ADA_N = 24 * (1 + layers)
    ctx = ExitStack()
    with ctx:
        place = [16512]

        def room(nbytes):
            at = place[0]
            place[0] += nbytes
            assert place[0] <= 229344, place[0]
            return at

        def at(name, shape, offset, dt=f32):
            return nc.alloc_sbuf_tensor_at(name, shape, dt, offset=offset)

        def new(name, shape, dt=f32):
            n = 4
            for s in shape[1:]:
                n *= s
            return at(name, shape, room((n + 31) // 32 * 32), dt)

        raw = new("raw", [P, RAW, CH])
        w_hi = new("w_hi", [P, 2, CH], f32r)
        w_lo = new("w_lo", [P, 2, CH], f32r)
        x = new("x", [P, KT, T])
        F = [room(8192) for _ in range(4)]
        act_hi = [at(f"act_hi{i}", [P, KT, T], F[i], f32r) for i in range(2)]
        act_lo = [at(f"act_lo{i}", [P, KT, T], F[2 + i], f32r) for i in range(2)]
        R = [room(8192), room(8192)]
        ada_raw = at("ada_raw", [P, 2, CH], R[0])
        ada_acc = new("ada_acc", [P, 2, T])
        cc = new("consts_common", [P, N_COMMON])
        cu = new("consts_stage", [P, N_CU])
        vec = new("vectors", [P, NV])
        sw = new("small_weights", [P, N_SW])
        sw_hi = new("small_hi", [P, 256], f32r)
        sw_lo = new("small_lo", [P, 256], f32r)
        cs = new("silu_c", [P, 3, KT])
        cth = new("silu_c_tanh", [P, 3 * KT])
        mod = new("mod", [P, 48])
        mod_ctx = new("mod_ctx", [P, 16])
        gs = new("gain_scale", [P, 4, KT])
        eps = new("eps", [P, 1])
        std = new("std", [P, T])
        rstd = new("rstd", [P, T])
        sm = new("smalls", [P, 12, 32])
        A = [room(8192) for _ in range(7)]
        print_left = 229344 - place[0]
        ident, triu, ones, omean = (cc[:, o:o + P] for o in (C_ID, C_TRIU, C_ONES, C_OMEAN))

        ps = ctx.enter_context(nc.psum_tensor("ps", [P, 8, 512], f32))
        sems = {}

        def S(name):
            if name not in sems:
                sems[name] = ctx.enter_context(nc.semaphore(name))
            return sems[name]

        for s in range(RAW):
            S(f"raw_loaded{s}")
        block = ctx.enter_context(nc.Block())

        class Order:

            def __init__(self, eng, name):
                self.eng, self.sem, self.n = eng, S(name), 0

            def mark(self, ins):
                ins.then_inc(self.sem, 1)
                self.n = self.n + 1

            def __call__(self, ins):
                self.mark(ins)
                self.eng.wait_ge(self.sem, self.n)

        def bc(ap, n):
            ap = ap.unsqueeze(len(ap.shape))
            return ap.to_broadcast(list(ap.shape[:-1]) + [n])

        def bmid(ap, n):
            ap = ap.unsqueeze(1)
            return ap.to_broadcast([ap.shape[0], n, ap.shape[2]])

        def flat(ap):
            s = ap.shape
            return ap if len(s) == 2 else ap.rearrange("p a b -> p (a b)") if len(s) == 3 else ap.rearrange("p a b c -> p (a b c)")

        def V(name, n=1, i=0, layer=None):
            o = V1[name] if layer is None else VEC_FIRST + layer * VEC_LAYER + VL[name]
            return vec[:, o + i:o + i + n]

        pre_kv = at("pre_kv", [P, 8, 2, T + 2], A[0])
        pre_q = at("pre_q", [P, 4, T + 2], A[0] + 16512)
        assert 16512 + 4 * 258 * 4 <= 24576
        uz = at("uz", [P, 8, T], A[3])
        y_kv = at("y_kv", [P, 8, 2, T], A[4])
        y_q = at("y_q", [P, 4, T], A[6])
        th_kv = at("th_kv", [P, 8, 2, T], A[0])
        th_q = at("th_q", [P, 4, T], A[0] + 16384)
        k_tok = at("k_tok", [P, 4, 4, P], F[0])
        v_tok = at("v_tok", [P, 4, 4, P], F[1])
        q_tok = at("q_tok", [P, 2, 4, P], F[2])
        sq_kq = at("sq_kq", [P, 16, P], A[0])
        sq_q = at("sq_q", [P, 8, P], A[1])
        kT = at("kT", [P, 4, 4, P], A[1])
        qT = at("qT", [P, 2, 4, P], F[2] + 4096)
        attnT = at("attnT", [P, 2, 2, 4, P], A[2])
        U = at("U", [P, 2, 4, 4, P], A[4])
        Bm = at("Bm", [P, 4, 4, P], A[0])
        Tm = at("Tm", [P, 4, 4, P], A[6])
        X = at("X", [P, 4, 4, P], F[3])
        dec = at("dec", [P, 4, P], F[2])
        dem = at("dem", [P, 4, P], F[2] + 2048)
        St = at("state", [P, 2, 4, P], A[0])
        o_tok = at("o_tok", [P, 2, 4, P], A[0] + 4096)
        Rm = at("Rm", [P, 2, 4, P], A[6])
        vn = at("vn", [P, 2, 4, P], A[6] + 4096)
        v2 = at("v2", [P, 2, 4, P], F[3])
        tmp_s = at("tmp_s", [P, 2, 4, P], F[3] + 4096)
        o_sq = at("o_sq", [P, 8, P], A[6])
        th_z = at("th_z", [P, 4, T], F[2])
        yfd = at("yfd", [P, 8, T], A[6])
        m1 = at("m1", [P, 4, 2, P], A[2])
        Z = at("Z", [P, 2, 4, 2, P], A[1])
        norm_sq1, norm_h1 = at("norm_sq1", [P, KT, T], A[4]), at("norm_h1", [P, KT, T], A[5])
        xc = at("xc", [P, KT, T], A[3])
        ctx_acc = at("ctx_acc", [P, 8, T], A[0])
        ctx_prod = at("ctx_prod", [P, CH], A[1])
        ada_in1 = at("ada_in1", [P, 8, T], A[2])
        ada_in16 = at("ada_in16", [P, 16, T], A[0])
        ada_in = at("ada_in", [P, 16, T], R[0])
        y1 = at("y1", [P, KT, T], A[5])
        mid_hi1 = at("mid_hi1", [P, FB, T], A[0], f32r)
        mid_lo1 = at("mid_lo1", [P, FB, T], A[0] + FB * T * 4, f32r)
        ft = A[0] + 2 * FB * T * 4
        gpad = at("gpad", [P, 2, ROWS + 2, GRID_W + 2], ft)
        gacc = at("gacc", [P, 2, T], ft + 3168)
        gth = at("gth", [P, 2, T], ft + 3168 + 2048)
        gm = at("gm", [P, 2, T], ft + 3168 + 4096)
        assert ft + 3168 + 6144 <= A[6] + 8192
        y_down = at("y_down", [P, KT, T], F[0])
        sq_down = at("sq_down", [P, KT, T], F[2])
        s01 = at("s01", [P, 2 * KT, T], A[0])
        s0, s1 = s01[:, 0:KT, :], s01[:, KT:2 * KT, :]
        s2, s3, s4, s5, s6 = (at(f"s{i}", [P, KT, T], A[i]) for i in range(2, 7))
        s7, s8 = at("s7", [P, KT, T], R[0]), at("s8", [P, KT, T], R[1])
        a4, a5, a6 = s4, s5, s6
        vtok_f, vtok_r = at("vtok_f", [P, 2, D], A[2]), at("vtok_r", [P, 2, D], R[0])
        mlp_hi = at("mlp_hi", [P, 16, T], A[0], f32r)
        mlp_lo = at("mlp_lo", [P, 16, T], A[2], f32r)
        relu = at("relu", [P, 2, 512], A[6])
        rsq = at("rsq", [P, 2, 512], A[6] + 4096)
        fox_s = at("fox_s", [P, 8, 384], A[4])
        fox_pt = at("fox_pt", [P, 8, 384], A[0])

        J_OUT1, J_UP, J_DOWN = 10, 14, 36
        J_LAYER = 44
        def JL(o):
            return o if o <= L_LRU else o - 1
        LAYER_J = 92

        def loop_part(n0, count):
            k = count // 4 * 4 - (4 if n0 + count + 2 > total and count % 4 == 0 else 0)
            return k if k >= 8 else 0

        def source(e):
            return e if e < 4 else 4 + (e - 4) // 7 * 6 + ((e - 4) % 7 - ((e - 4) % 7 > 1))

        @block.sync
        def _(sp):
            sp.dma_start(vec[:, :], io["vecs"]).then_inc(S("vec_loaded"), 16)
            sp.dma_start(cc[:, :], io["consts_common"]).then_inc(S("small_loaded"), 16)
            sp.dma_start(xc[:, :, :], io["ctxT"]).then_inc(S("small_loaded"), 16)
            sp.dma_start(x[:, :, :], io["xT"]).then_inc(S("small_loaded"), 16)
            sp.dma_start(cu[:, 0:N_CA], io["consts_a"]).then_inc(S("small_loaded"), 16)
            sp.dma_start(sw[:, :], io["small_w"]).then_inc(S("small_loaded"), 16)

            def load(n, s):
                sp.dma_start(raw[:, s:s + 1, :], io["stream"][bass.ds(n, 1)].rearrange("a p n -> p a n"))\
                  .then_inc(S(f"raw_loaded{s}"), 16)

            for s in range(RAW):
                load(s, s)
            rounds = total // RAW
            with sp.Fori(1, rounds) as i:
                for s in range(RAW):
                    sp.wait_ge(S("lo_ready"), i * RAW + (s - RAW + 1))
                    load(i * RAW + s, s)
            for n in range(rounds * RAW, total):
                sp.wait_ge(S("lo_ready"), n - RAW + 1)
                load(n, n % RAW)
            sp.wait_ge(S("x_new"), 2 + 2 * layers)
            sp.dma_start(io["out"], x[:, :, :]).then_inc(S("stored"), 16)
            sp.wait_ge(S("stored"), 16)

        @block.gpsimd
        def _(pool):
            order = Order(pool, "pool_order")

            def load(m, s):
                pool.dma_start(ada_raw[:, s:s + 1, :], io["ada"][bass.ds(m, 1)].rearrange("a p n -> p a n"))\
                    .then_inc(S(f"ada_loaded{s}"), 16)

            def chunk(half, s, which, more, early=False):
                m = half * 2 + s
                order.n = m * 4
                pool.wait_ge(S(f"ada_loaded{s}"), half * 16 + 16)
                if early:
                    pool.wait_ge(S("ctx_read"), m + 1)
                r = ada_raw[:, s, :].rearrange("p (k n) -> p k n", k=KT)
                order(nc.gpsimd.tensor_tensor(r, r, bc(cs[:, which, :], T), ALU.mult))
                order(nc.gpsimd.tensor_tensor(r[:, 0:4, :], r[:, 0:4, :], r[:, 4:8, :], ALU.add))
                order(nc.gpsimd.tensor_tensor(r[:, 0:2, :], r[:, 0:2, :], r[:, 2:4, :], ALU.add))
                if not (isinstance(half, int) and half == 0):
                    pool.wait_ge(S(f"ada_stored{s}"), half * 16)
                order(nc.gpsimd.tensor_tensor(ada_acc[:, s, :], r[:, 0, :], r[:, 1, :], ALU.add))
                pool.dma_start(io["ada_part"][bass.ds(m, 1)].rearrange("a p n -> p a n"), ada_acc[:, s:s + 1, :])\
                    .then_inc(S(f"ada_stored{s}"), 16)
                if more:
                    load(m + 2, s)

            load(0, 0)
            load(1, 1)
            pool.wait_ge(S("cs_ready"), 1)
            for half in range(4):
                for s in range(2):
                    chunk(half, s, 0, True, early=True)
            with pool.Fori(4, 12 if layers else 11) as i:
                for s in range(2):
                    chunk(i, s, 0, True)
            if layers:
                with pool.Fori(12, ADA_N // 2 - 1) as i:
                    for s in range(2):
                        chunk(i, s, 2, True)
            for s in range(2):
                chunk(ADA_N // 2 - 1, s, 2 if layers else 0, False)
            for s in range(2):
                pool.wait_ge(S(f"ada_stored{s}"), ADA_N // 2 * 16)
            for L in range(layers):
                if L > 0:
                    pool.wait_ge(S("split_src"), 2 * source(4 + 7 * (L - 1) + 5) + 2)
                first = 24 * (L + 1)
                pool.dma_start(ada_in[:, :, :], io["ada_part"][first:first + 16].rearrange("c p n -> p c n"))\
                    .then_inc(S("ada_layer"), 16)
                pool.wait_ge(S("mod_mm"), 4 + 2 * L)
                pool.dma_start(ada_in[:, 0:8, :], io["ada_part"][first + 16:first + 24].rearrange("c p n -> p c n"))\
                    .then_inc(S("ada_layer"), 16)

        @block.tensor
        def _(pe):
            mm, tr = nc.tensor.matmul, nc.tensor.transpose

            def mm3(out, ah, al, bh, bl, first, last):
                mm(out, ah, bh, start=first, stop=False)
                mm(out, ah, bl, start=False, stop=False)
                return mm(out, al, bh, start=False, stop=last)

            def begin(n, j, strict=False):
                pe.wait_ge(S("lo_ready"), n + 1)
                if j is None:
                    return
                if strict:
                    pe.wait_ge(S("evicted"), j)
                elif not isinstance(j, int) or j >= 2:
                    pe.wait_ge(S("evicted"), j - 1)

            def feat_chunk(wp, bank, s):
                for b in range(2):
                    for k in range(KT):
                        o = (b * KT + k) * P
                        last = mm3(ps[:, bank, b * T:(b + 1) * T], w_hi[:, wp, o:o + P], w_lo[:, wp, o:o + P],
                                   act_hi[s][:, k, :], act_lo[s][:, k, :], k == 0, k == KT - 1)
                return last

            def tok_chunk(wp, bank, s):
                for t in range(TT):
                    for k in range(KT):
                        last = mm3(ps[:, bank, t * T:(t + 1) * T], act_hi[s][:, k, t * P:(t + 1) * P],
                                   act_lo[s][:, k, t * P:(t + 1) * P], w_hi[:, wp, k * T:(k + 1) * T],
                                   w_lo[:, wp, k * T:(k + 1) * T], k == 0, k == KT - 1)
                return last

            def job(fn, n0, j0, count, s, strict=False):
                def four(i, m):
                    for c in range(m):
                        begin(i + (n0 + c), i + (j0 + c), strict and isinstance(i, int) and i + c == 0)
                        fn((n0 + c) % 2, (j0 + c) % 2, s).then_inc(S("chunk_done"), 1)
                if count >= 8:
                    if strict:
                        four(0, 4)
                        with pe.Fori(1, count // 4) as i:
                            four(i * 4, 4)
                    else:
                        with pe.Fori(0, count // 4) as i:
                            four(i * 4, 4)
                    if count % 4:
                        four(count // 4 * 4, count % 4)
                else:
                    four(0, count)

            def deep_chunk(wp, bank, s):
                for k in range(16):
                    last = mm3(ps[:, bank, 0:T], w_hi[:, wp, k * P:(k + 1) * P], w_lo[:, wp, k * P:(k + 1) * P],
                               mlp_hi[:, k, :], mlp_lo[:, k, :], k == 0, k == 15)
                return last

            def norm(k, sq):
                pe.wait_ge(S("norm_sq"), k + 1)
                for b in range(KT):
                    last = mm(ps[:, 7, 0:T], omean, sq[:, b, :], start=b == 0, stop=b == KT - 1)
                last.then_inc(S("norm_ms"), 1)

            def mods(loads, src, first, count, col0, loaded="ada_in"):
                pe.wait_ge(S(loaded), 16 * loads)
                for c in range(first, first + count):
                    o = c % 2 * P
                    last = mm(ps[:, 5, col0 + c:col0 + c + 1], src[:, c // 2, o:o + P], ones[:, 0:1],
                              start=True, stop=True)
                last.then_inc(S("mod_mm"), 1)

            pe.wait_ge(S("small_loaded"), 5 * 16)
            pe.wait_ge(S("ctx_acc_done"), 1)
            for c in range(16):
                last = mm(ps[:, 6, c:c + 1], ctx_acc[:, c // 2, c % 2 * P:c % 2 * P + P], ones[:, 0:1], start=True, stop=True)
            last.then_inc(S("modctx_mm"), 1)
            mods(1, ada_in1, 0, 16, 0)
            pe.wait_ge(S("mods_done"), 1)
            norm(0, norm_sq1)
            pe.wait_ge(S("norm_std"), 1)
            norm(1, norm_sq1)
            pe.wait_ge(S("act_ready"), 4)
            job(feat_chunk, N_Q, 0, 2, 1)
            for c in range(4):
                n = N_KV + c
                begin(n, n)
                bank = n % 2 * 2
                if c == 0:
                    pe.wait_ge(S("evicted"), 2)
                feat_chunk(n % 2, bank, 0)
                feat_chunk(n % 2, bank + 1, 1).then_inc(S("chunk_done"), 1)
            job(feat_chunk, N_UZ, N_UZ, 4, 1, strict=True)
            pe.wait_ge(S("sw_lo"), 1)
            for t in range(4):
                s, tt = t // 2, t % 2
                for k in range(KT):
                    last = mm3(ps[:, 7, t * 16:t * 16 + 16], act_hi[s][:, k, tt * P:tt * P + P],
                               act_lo[s][:, k, tt * P:tt * P + P], sw_hi[:, k * 16:k * 16 + 16],
                               sw_lo[:, k * 16:k * 16 + 16], k == 0, k == KT - 1)
            last.then_inc(S("ab_mm"), 1)
            pe.wait_ge(S("y_ready"), 1)
            groups = [("k", t) for t in range(4)] + [("v", t) for t in range(4)] + [("q", t) for t in range(2)]
            for g, (kind, t) in enumerate(groups):
                if g >= 3:
                    pe.wait_ge(S("tr_ev"), g - 2)
                for h in range(HEADS):
                    src = y_q[:, h, t * P:(t + 1) * P] if kind == "q" else \
                        y_kv[:, h + (4 if kind == "v" else 0), t // 2, t % 2 * P:t % 2 * P + P]
                    last = tr(ps[:, 4 + g % 3, h * P:(h + 1) * P], src, ident)
                last.then_inc(S("tr_mm"), 1)
            pe.wait_ge(S("kq_norm"), 1)
            pe.wait_ge(S("tr_ev"), 10)
            for g in range(6):
                if g >= 3:
                    pe.wait_ge(S("trb_ev"), g - 2)
                for h in range(HEADS):
                    src = k_tok[:, g, h, :] if g < 4 else q_tok[:, g - 4, h, :]
                    last = tr(ps[:, 4 + g % 3, h * P:(h + 1) * P], src, ident)
                last.then_inc(S("trb_mm"), 1)
            pe.wait_ge(S("g_ready"), 1)
            g_ = sm[:, 1, :].rearrange("p (t c) -> p t c", t=4)
            tril = cu[:, A_TRIL:A_TRIL + P]
            for t in range(4):
                mm(ps[:, 7, t * 8:t * 8 + 4], triu, g_[:, t, 0:4], start=True, stop=True)
                mm(ps[:, 7, t * 8 + 4:t * 8 + 8], tril, g_[:, t, 4:8], start=True, stop=True)
                last = mm(ps[:, 7, 32 + t * 8:32 + t * 8 + 8], ones, g_[:, t, :], start=True, stop=True)
            last.then_inc(S("gc_mm"), 1)
            pe.wait_ge(S("trb_ev"), 6)
            pe.wait_ge(S("gc_ev"), 1)
            inv = 0
            seen_ev = 0
            for d in range(2):
                for t in range(4):
                    e = d * 4 + t
                    if e > 0:
                        pe.wait_ge(S("mat_ev"), e)
                    for h in range(HEADS):
                        mm(ps[:, 4, h * P:(h + 1) * P], kT[:, t, h, :], kT[:, t, h, :], start=True, stop=True)
                    if t >= 2:
                        for h in range(HEADS):
                            mm(ps[:, 5, h * P:(h + 1) * P], kT[:, t, h, :], qT[:, t - 2, h, :], start=True, stop=True)
                    for h in range(HEADS):
                        col = d * 4 + h
                        last = mm(ps[:, 6, h * P:(h + 1) * P], g_[:, t, col:col + 1].to_broadcast([P, P]),
                                  triu if d == 0 else tril, start=True, stop=True)
                    last.then_inc(S("mat_mm"), 1)
                pe.wait_ge(S("mat_ev"), 4 * (d + 1))
                pe.wait_ge(S("inv_init"), d + 1)
                for lvl in range(7):
                    size = 1 << lvl
                    pcol, rcol = (0, 1) if d == 0 else (1, 0)
                    def half(ap, which):
                        return ap.rearrange("p (g two s) -> p g two s", two=2, s=size)[:, :, which, :]
                    for g in range(4):
                        if lvl > 0:
                            pe.wait_ge(S("inv_u"), d * 28 + (lvl - 1) * 4 + g + 1)
                        for h in range(HEADS):
                            last = mm(ps[:, 4 + g, h * P:(h + 1) * P], Bm[:, g, h, :], Tm[:, g, h, :], start=True, stop=True)
                        last.then_inc(S("inv_x_mm"), 1)
                    for g in range(4):
                        pe.wait_ge(S("inv_x"), d * 28 + lvl * 4 + g + 1)
                        for h in range(HEADS):
                            if lvl < 6:
                                mm(ps[:, 4 + g, h * 64:(h + 1) * 64], U[:, d, g, h, :], half(X[:, g, h, :], pcol),
                                   start=True, stop=True)
                            last = mm(ps[:, 4 + g, 256 + h * 64:256 + (h + 1) * 64], X[:, g, h, :],
                                      half(U[:, d, g, h, :], rcol), start=True, stop=True)
                        last.then_inc(S("inv_u_mm"), 1)
                pe.wait_ge(S("inv_u"), d * 28 + 28)
            pe.wait_ge(S("scan_init"), 1)
            for st in range(4):
                for d in range(2):
                    e = st * 2 + d
                    t = (st if d == 0 else [1, 0, 3, 2][st])
                    if st > 0:
                        pe.wait_ge(S("scan_s"), e - 1)
                    for h in range(HEADS):
                        last = mm(ps[:, 4 + d, h * P:(h + 1) * P], kT[:, t, h, :], St[:, d, h, :], start=True, stop=True)
                    if t >= 2:
                        if st == 3:
                            pe.wait_ge(S("scan_o"), 2 * (d + 1))
                        for h in range(HEADS):
                            last = mm(ps[:, 6 + d, h * P:(h + 1) * P], qT[:, t - 2, h, :], St[:, d, h, :], start=True, stop=True)
                    last.then_inc(S("scan_p_mm"), 1)
                for d in range(2):
                    e = st * 2 + d
                    t = (st if d == 0 else [1, 0, 3, 2][st])
                    pe.wait_ge(S("scan_r"), e + 1)
                    for h in range(HEADS):
                        last = mm(ps[:, 4 + d, h * P:(h + 1) * P], U[:, d, t, h, :], Rm[:, d, h, :], start=True, stop=True)
                    last.then_inc(S("scan_w_mm"), 1)
                for d in range(2):
                    e = st * 2 + d
                    t = (st if d == 0 else [1, 0, 3, 2][st])
                    pe.wait_ge(S("scan_v"), e + 1)
                    for h in range(HEADS):
                        last = mm(ps[:, 4 + d, h * P:(h + 1) * P], k_tok[:, t, h, :], v2[:, d, h, :], start=True, stop=True)
                    if st >= 2:
                        pe.wait_ge(S("scan_o"), (st - 2) * 4 + d * 1 + 1)
                        for h in range(HEADS):
                            last = mm(ps[:, 6 + d, h * P:(h + 1) * P], attnT[:, d, t - 2, h, :], vn[:, d, h, :], start=True, stop=True)
                    last.then_inc(S("scan_s_mm"), 1)
            pe.wait_ge(S("scan_s"), 8)
            CC, SC = cu[:, A_CC:A_CC + P], cu[:, A_SC:A_SC + P]
            pe.wait_ge(S("scan_o"), 8)
            for g in range(4):
                wf = sw[:, SW_WF + g * P:SW_WF + (g + 1) * P]
                o = g % 2 * T
                mm(ps[:, 4 + g // 2, o:o + P], CC, wf, start=True, stop=True)
                last = mm(ps[:, 4 + g // 2, o + P:o + T], SC, wf, start=True, stop=True)
            last.then_inc(S("four_mm"), 1)
            pe.wait_ge(S("four_ev"), 1)
            for t in range(2):
                for g in range(4):
                    last = mm(ps[:, 4 + t * 2 + g // 2, g % 2 * T:g % 2 * T + T], uz[:, g, t * P:(t + 1) * P],
                              flat(m1[:, g, :, :]), start=True, stop=True)
            last.then_inc(S("four_mm"), 1)
            pe.wait_ge(S("four_ev"), 2)
            for g in range(4):
                for t in range(2):
                    for m, base in enumerate((A_CL, A_SL)):
                        last = mm(ps[:, 4 + g // 2, g % 2 * T:g % 2 * T + T], Z[:, t, g, m, :],
                                  cu[:, base + t * T:base + (t + 1) * T], start=(t + m == 0), stop=(t + m == 2))
            last.then_inc(S("four_mm"), 1)
            pe.wait_ge(S("o_norm"), 1)
            for h in range(HEADS):
                for t in range(2):
                    last = tr(ps[:, 6 + h // 2, h % 2 * T + t * P:h % 2 * T + t * P + P], o_tok[:, t, h, :], ident)
            last.then_inc(S("o_tr"), 1)
            pe.wait_ge(S("act_ready"), 6)
            mods(2, ada_in16, 0, 8, 0)
            job(feat_chunk, N_OUT1, J_OUT1, 4, 1, strict=True)
            norm(2, norm_sq1)
            mods(2, ada_in16, 8, 24, 0)
            norm(3, norm_sq1)
            pe.wait_ge(S("act_ready"), 8)
            def up(i, m):
                for c in range(m):
                    pe.wait_ge(S("lo_ready"), i + (N_UP + c + 1))
                    pe.wait_ge(S("evicted"), i + (J_UP + c - 3) if not isinstance(i, int) or i > 0 else J_UP)
                    feat_chunk((N_UP + c) % 2, c % 4, 1).then_inc(S("chunk_done"), 1)
            up(0, 4)
            with pe.Fori(1, FB // 4) as i:
                up(i * 4, 4)
            up(FB // 4 * 4, FB % 4)
            if layers:
                pe.wait_ge(S("mods_done"), 3)
                mods(1, ada_in, 0, 32, 0, "ada_layer")
            pe.wait_ge(S("mid_ready"), FB)
            for o in range(KT):
                for k in range(FB):
                    i = o * FB + k
                    n, b = N_DOWN + i // 16, i % 16
                    if b == 0:
                        pe.wait_ge(S("lo_ready"), n + 1)
                    if k == 0:
                        pe.wait_ge(S("evicted"), J_DOWN + (o - 1 if o >= 1 else 0))
                    last = mm3(ps[:, o % 2, 0:T], w_hi[:, n % 2, b * P:(b + 1) * P], w_lo[:, n % 2, b * P:(b + 1) * P],
                               mid_hi1[:, k, :], mid_lo1[:, k, :], k == 0, k == FB - 1)
                    if b == 15:
                        last.then_inc(S("chunk_done"), 1)
            if layers:
                mods(2, ada_in, 0, 16, 32, "ada_layer")
            norm(4, sq_down)

            for L in range(layers):
                n0, j0 = N_LAYER + L * LAYER_CH, J_LAYER + L * LAYER_J
                ns, ar = 5 + 4 * L, 8 + 14 * L
                norm(ns, a6)
                pe.wait_ge(S("act_ready"), ar + 2)
                def group(fn, off, src, after=(), n0=n0, j0=j0):
                    for c in range(4):
                        begin(n0 + off + c, j0 + JL(off) + c)
                        fn((n0 + off + c) % 2, (j0 + JL(off) + c) % 2, src).then_inc(S("chunk_done"), 1)
                        if c < len(after) and after[c]:
                            after[c]()

                nlf = sm[:, 1, 0:16].rearrange("p (t h) -> p t h", t=2)

                def ff():
                    for t in range(2):
                        for k in range(KT):
                            o = SW_FF + L * 64 + k * 8
                            last = mm3(ps[:, 7, t * 8:t * 8 + 8], act_hi[1][:, k, t * P:(t + 1) * P],
                                       act_lo[1][:, k, t * P:(t + 1) * P], sw_hi[:, o:o + 8], sw_lo[:, o:o + 8],
                                       k == 0, k == KT - 1)
                    last.then_inc(S("ff_mm"), 1)

                def cum():
                    pe.wait_ge(S("nlf_ready"), L + 1)
                    mm(ps[:, 7, 16:24], triu, nlf[:, 0, :], start=True, stop=True)
                    mm(ps[:, 7, 24:32], ones, nlf[:, 0, :], start=True, stop=False)
                    mm(ps[:, 7, 24:32], triu, nlf[:, 1, :], start=False, stop=True).then_inc(S("cum_mm"), 1)

                def fox_scores(h0):
                    if h0 == 0:
                        pe.wait_ge(S("evicted"), j0 + L_FV)
                        pe.wait_ge(S("cum_ev"), L + 1)
                    for h in range(h0, h0 + 4):
                        if h >= 4:
                            pe.wait_ge(S("fox_s_ev"), L * 8 + h - 3)
                        q, k, bank = s0[:, h, :], s1[:, h, :], 4 + h % 4
                        t0, t1 = ps[:, bank, 0:P], ps[:, bank, P:P + T]
                        mm(t0, q[:, 0:P], k[:, 0:P], start=True, stop=False)
                        mm(t0, nlf[:, 0, h:h + 1].to_broadcast([P, P]), triu, start=False, stop=True)
                        mm(t1, q[:, P:T], k, start=True, stop=False)
                        mm(t1, nlf[:, 0, h:h + 1].to_broadcast([P, P]), cc[:, C_TRIU:C_TRIU + T], start=False, stop=False)
                        mm(ps[:, bank, T:T + P], nlf[:, 1, h:h + 1].to_broadcast([P, P]), triu, start=False, stop=True)\
                            .then_inc(S("fox_s_mm"), 1)

                def fox_tr(h0):
                    if h0 == 0:
                        pe.wait_ge(S("fox_p"), L + 1)
                    for h in range(h0, h0 + 4):
                        if h >= 4:
                            pe.wait_ge(S("fox_t_ev"), L * 8 + h - 3)
                        bank = 4 + h % 4
                        tr(ps[:, bank, 0:P], fox_s[:, h, 0:P], ident)
                        tr(ps[:, bank, P:2 * P], fox_s[:, h, P:2 * P], ident)
                        tr(ps[:, bank, 2 * P:3 * P], fox_s[:, h, 2 * P:3 * P], ident).then_inc(S("fox_t_mm"), 1)

                def fox_out():
                    pe.wait_ge(S("fox_t_ev"), L * 8 + 8)
                    for h in range(8):
                        o = h % 2 * T
                        v_ = vtok_f[:, :, h * P:(h + 1) * P]
                        mm(ps[:, 4 + h // 2, o:o + T], v_[:, 0, :], fox_pt[:, h, 0:T], start=True, stop=False)
                        last = mm(ps[:, 4 + h // 2, o + P:o + T], v_[:, 1, :], fox_pt[:, h, T:T + P], start=False, stop=True)
                    last.then_inc(S("fox_o_mm"), 1)

                def rope():
                    pe.wait_ge(S("fox_o"), L + 1)
                    for b in range(8):
                        last = mm(ps[:, 4 + b // 2, b % 2 * T:b % 2 * T + T], cu[:, B_PERM:B_PERM + P], s6[:, b, :],
                                  start=True, stop=True)
                    last.then_inc(S("rope_mm"), 1)

                def ret_scores():
                    pe.wait_ge(S("rope_done"), L + 1)
                    for h in range(HEADS):
                        for m in range(2):
                            last = mm(ps[:, 4 + h, m * T:(m + 1) * T], s6[:, 4 + h, m * P:(m + 1) * P], s6[:, h, :],
                                      start=True, stop=True)
                    last.then_inc(S("ret_s_mm"), 1)

                def ret_out():
                    pe.wait_ge(S("ret_p"), L + 1)
                    for t in range(2):
                        for h in range(HEADS):
                            out = ps[:, 4 + t * 2 + h // 2, h % 2 * T:h % 2 * T + T]
                            for m in range(t + 1):
                                last = mm(out, s1[:, h * 2 + m, t * P:(t + 1) * P], vtok_r[:, m, h * T:(h + 1) * T],
                                          start=m == 0, stop=m == t)
                    last.then_inc(S("ret_o_mm"), 1)

                def ret_tr():
                    pe.wait_ge(S("ret_norm"), L + 1)
                    pe.wait_ge(S("lru_ev"), 16 * (L + 1))
                    o_ = s4[:, :, :].rearrange("p (t h) n -> p t h n", t=2)
                    for b in range(8):
                        for t in range(2):
                            last = tr(ps[:, 4 + b // 2, b % 2 * T + t * P:b % 2 * T + t * P + P],
                                      o_[:, t, b // 2, b % 2 * P:b % 2 * P + P], ident)
                    last.then_inc(S("ret_tr"), 1)

                job(feat_chunk, n0 + L_FQK, j0 + L_FQK, 8, 1)
                group(tok_chunk, L_FV, 1, [None, None, None, ff])
                group(feat_chunk, L_G2, 1, [None, None, cum, lambda: fox_scores(0)])
                group(feat_chunk, L_RQK, 1, [lambda: fox_scores(4)])
                group(tok_chunk, L_RV, 1, [None, None, lambda: fox_tr(0), lambda: fox_tr(4)])
                group(feat_chunk, L_LX, 1, [fox_out, rope])
                pe.wait_ge(S("act_ready"), ar + 4)
                group(feat_chunk, L_FOXO, 0, [None, ret_scores, ret_out])
                group(feat_chunk, L_LY, 1)
                pe.wait_ge(S("act_ready"), ar + 6)
                n = n0 + L_LRU
                begin(n, j0 + JL(L_LRU), strict=True)
                pe.wait_ge(S("ret_o"), L + 1)
                for b in list(range(8, 16)) + list(range(8)):
                    bank = (4 if b < 8 else 0) + b % 8 // 2
                    last = mm3(ps[:, bank, b % 2 * T:b % 2 * T + T], w_hi[:, n % 2, b * P:(b + 1) * P],
                               w_lo[:, n % 2, b * P:(b + 1) * P], act_hi[0][:, b % 8, :], act_lo[0][:, b % 8, :], True, True)
                    if b == 15:
                        last.then_inc(S("lru_x_mm"), 1)
                last.then_inc(S("chunk_done"), 1)
                pe.wait_ge(S("lru_ev"), 16 * L + 4)
                group(feat_chunk, L_RG, 1)
                group(feat_chunk, L_G1, 1, [None, None, ret_tr])
                group(feat_chunk, L_G0, 1)
                pe.wait_ge(S("act_ready"), ar + 8)
                group(feat_chunk, L_RETO, 0)
                pe.wait_ge(S("act_ready"), ar + 10)
                group(feat_chunk, L_LRUO, 0)
                pe.wait_ge(S("act_ready"), ar + 12)
                group(feat_chunk, L_WOUT, 1)
                norm(ns + 1, a6)
                norm(ns + 2, a6)
                pe.wait_ge(S("act_ready"), ar + 14)
                for hf in range(2):
                    n = n0 + L_MLP + 16 * hf
                    j = j0 + JL(L_MLP) + 16 * hf
                    job(feat_chunk, n, j, 8, 1)
                    if L + 1 < layers:
                        pe.wait_ge(S("mods_done"), 4 + L)
                        mods(3 + 2 * L + hf, ada_in, 0, 32 - 16 * hf, 32 * hf, "ada_layer")
                    pe.wait_ge(S("mlp_ready"), 8 * (2 * L + hf + 1))
                    job(deep_chunk, n + 8, j + 8, 8, 1)
                norm(ns + 3, a6)

        @block.scalar
        def _(act):
            act_ = nc.scalar.activation

            def prep(n, s4, s2):
                if isinstance(n, int):
                    if n >= total:
                        return
                    rnd = n // RAW * 16 + 16
                    act.wait_ge(S(f"raw_loaded{s4}"), rnd)
                    if n >= 2:
                        act.wait_ge(S("chunk_done"), n - 1)
                else:
                    act.wait_ge(S(f"raw_loaded{s4}"), n[1])
                    act.wait_ge(S("chunk_done"), n[0] - 1)
                act_(w_hi[:, s2, :], raw[:, s4, :], ACT.Copy).then_inc(S("hi_ready"), 1)

            def evict(dst, bank, n_done, func=ACT.Copy, scale=1.0, src=None):
                act.wait_ge(S("chunk_done"), n_done + 1)
                act_(dst, ps[:, bank, :] if src is None else src, func, scale=scale).then_inc(S("evicted"), 1)

            def job(n0, j0, count, dst, func=ACT.Copy, scale=1.0, sl=slice(0, 512), hook=None):
                def four(i, m):
                    for c in range(m):
                        n = n0 + c + 2
                        if isinstance(i, int):
                            prep(i + n, (i + n) % RAW, (i + n) % 2)
                        else:
                            prep((i + n, i * (16 // RAW) + (n // RAW * 16 + 16)), n % RAW, n % 2)
                        if hook:
                            hook(i, c)
                        else:
                            evict(dst(i + c), (j0 + c) % 2, i + (n0 + c), func, scale, ps[:, (j0 + c) % 2, sl])
                looped = loop_part(n0, count)
                if looped:
                    with act.Fori(0, looped // 4) as i:
                        four(i * 4, 4)
                for r in range(looped, count, 4):
                    four(r, min(4, count - r))

            def norm(k, src, sq):
                act_(sq[:, :, :], src[:, :, :], ACT.Square).then_inc(S("norm_sq"), 1)
                act.wait_ge(S("norm_ms"), k + 1)
                act_(std[:, :], ps[:, 7, 0:T], ACT.Sqrt, bias=eps[:, :]).then_inc(S("norm_std"), 1)

            def split(e, src, hi):
                for hf in range(2):
                    act.wait_ge(S("split_src"), 2 * source(e) + hf + 1)
                    act_(hi[:, 4 * hf:4 * hf + 4, :], src[:, 4 * hf:4 * hf + 4, :], ACT.Copy).then_inc(S("split_hi"), 1)

            def load_ada(k, dst, first, count):
                last = first + count
                for s in range(2):
                    act.wait_ge(S(f"ada_stored{s}"), (last + 1 - s) // 2 * 16)
                act.dma_start(dst[:, :, :], io["ada_part"][first:last].rearrange("c p n -> p c n")).then_inc(S("ada_in"), 16)

            act.wait_ge(S("vec_loaded"), 16)
            act_(cth[:, :], vec[:, 0:3 * KT], ACT.Tanh, scale=0.5).then_inc(S("c_tanh"), 1)
            prep(0, 0, 0)
            prep(1, 1, 1)
            act.wait_ge(S("small_loaded"), 5 * 16)
            act_(sw_hi[:, :], sw[:, 0:256], ACT.Copy).then_inc(S("sw_hi"), 1)
            act.wait_ge(S("eps_set"), 1)
            load_ada(0, ada_in1, 0, 8)
            norm(0, xc, norm_sq1)
            act.wait_ge(S("norm_rstd"), 1)
            norm(1, x, norm_sq1)
            split(0, norm_h1, act_hi[0])
            split(1, norm_h1, act_hi[1])
            for c in range(2):
                n = N_Q + c
                prep(n + 2, (n + 2) % RAW, n % 2)
                act.wait_ge(S("chunk_done"), n + 1)
                if c == 0:
                    act.wait_ge(S("pads"), 3)
                act_(pre_q[:, 2 * c:2 * c + 2, 1:T + 1], ps[:, n % 2, :].rearrange("p (b t) -> p b t", b=2), ACT.Copy)\
                    .then_inc(S("evicted"), 1)
            for c in range(4):
                n = N_KV + c
                prep(n + 2, (n + 2) % RAW, n % 2)
                act.wait_ge(S("chunk_done"), n + 1)
                bank = n % 2 * 2
                act_(pre_kv[:, 2 * c:2 * c + 2, :, 1:T + 1],
                     ps[:, bank:bank + 2, :].rearrange("p s (b t) -> p b s t", b=2), ACT.Copy).then_inc(S("evicted"), 1)
            job(N_UZ, N_UZ, 4, lambda i: flat(uz[:, 2 * i:2 * i + 2, :]))
            act.wait_ge(S("conv"), 1)
            act_(th_kv[:, :, :, :], y_kv[:, :, :, :], ACT.Tanh, scale=0.5)
            act_(th_q[:, :, :], y_q[:, :, :], ACT.Tanh, scale=0.5).then_inc(S("conv_tanh"), 1)
            ab = sm[:, 0, :]
            act.wait_ge(S("ab_abs"), 1)
            act_(sm[:, 2, :], sm[:, 2, :], ACT.Tanh, scale=0.5)
            act_(sm[:, 3, :], sm[:, 3, :], ACT.Exp, scale=-1.0)
            act_(sm[:, 4, 0:8], V("a_log", 8), ACT.Exp).then_inc(S("ab_act"), 1)
            act.wait_ge(S("tr_ev"), 10)
            act_(sq_kq[:, :, :], k_tok[:, :, :, :].rearrange("p t h n -> p (t h) n"), ACT.Square)
            act_(sq_q[:, :, :], q_tok[:, :, :, :].rearrange("p t h n -> p (t h) n"), ACT.Square).then_inc(S("kq_sq"), 1)
            act.wait_ge(S("kq_ss"), 1)
            act_(sm[:, 5, 0:24], sm[:, 5, 0:24], ACT.Sqrt, scale=0.25, bias=eps[:, :]).then_inc(S("kq_std"), 1)
            for g in range(6):
                act.wait_ge(S("trb_mm"), g + 1)
                dst = kT[:, g, :, :] if g < 4 else qT[:, g - 4, :, :]
                act_(flat(dst), ps[:, 4 + g % 3, :], ACT.Copy).then_inc(S("trb_ev"), 1)
            act.wait_ge(S("gc_diff"), 1)
            act_(sm[:, 8:11, :], sm[:, 8:11, :], ACT.Exp).then_inc(S("gc_exp"), 1)
            for e in range(8):
                act.wait_ge(S("dec_min"), e + 1)
                act_(dec[:, :, :], dec[:, :, :], ACT.Exp).then_inc(S("dec_exp"), 1)
            act.wait_ge(S("scan_o"), 8)
            act_(th_z[:, :, :], uz[:, 4:8, :], ACT.Tanh, scale=0.5).then_inc(S("z_tanh"), 1)
            act_(o_sq[:, :, :], o_tok[:, :, :, :].rearrange("p t h n -> p (t h) n"), ACT.Square).then_inc(S("o_sq"), 1)
            act.wait_ge(S("o_ss"), 1)
            act_(sm[:, 5, 0:8], sm[:, 5, 0:8], ACT.Sqrt, scale=1.0 / P, bias=eps[:, :]).then_inc(S("o_std"), 1)
            act.wait_ge(S("four_mm"), 1)
            act_(m1[:, :, :, :].rearrange("p (a g) m n -> p a (g m n)", a=2), ps[:, 4:6, :], ACT.Copy).then_inc(S("four_ev"), 1)
            act.wait_ge(S("four_mm"), 2)
            act_(Z[:, :, :, :, :].rearrange("p t (a g) m n -> p (t a) (g m n)", a=2), ps[:, 4:8, :], ACT.Copy)\
                .then_inc(S("four_ev"), 1)
            act.wait_ge(S("four_mm"), 3)
            act.wait_ge(S("o_ss"), 1)
            act_(yfd[:, 0:4, :].rearrange("p (a b) t -> p a (b t)", a=2), ps[:, 4:6, :], ACT.Copy).then_inc(S("split_src"), 1)
            split(2, yfd, act_hi[1])
            load_ada(1, ada_in16, 8, 16)
            job(N_OUT1, J_OUT1, 4, lambda i: flat(y1[:, 2 * i:2 * i + 2, :]))
            act.wait_ge(S("evicted"), J_OUT1 + 4)
            norm(2, y1, norm_sq1)
            act.wait_ge(S("x_new"), 1)
            norm(3, x, norm_sq1)
            split(3, norm_h1, act_hi[1])
            def up_steps(i, c):
                n, s, e, first = N_UP + c, c % 2, i + c, isinstance(i, int) and i == 0
                act.wait_ge(S("chunk_done"), i + (n + 1))
                if not (first and c < 2):
                    act.wait_ge(S("evicted"), i + (J_UP + c - 1))
                act_(gpad[:, s, 1:ROWS + 1, 1:GRID_W + 1],
                     ps[:, c % 4, T:2 * T].rearrange("p (r w) -> p r w", r=ROWS), ACT.Copy)
                act_(gacc[:, s, :], ps[:, c % 4, T:2 * T], ACT.Copy, scale=vec[:, bass.ds(e + (V1["dwc"] + 4 * FB), 1)])\
                    .then_inc(S("gate_in"), 1)
                if isinstance(i, int):
                    prep(i + n + 2, (i + n + 2) % RAW, (i + n) % 2)
                else:
                    prep((i + (n + 2), i * (16 // RAW) + ((n + 2) // RAW * 16 + 16)), (n + 2) % RAW, n % 2)
                if not (first and c == 0):
                    up_silu(i, c)

            def up_silu(i, c):
                s = (c + 1) % 2
                act.wait_ge(S("gconv"), i + c)
                act_(gth[:, s, :], gacc[:, s, :], ACT.Tanh, scale=0.5).then_inc(S("gate_tanh"), 1)
                act.wait_ge(S("evicted"), i + (J_UP + c))
                act_(mid_hi1[:, bass.ds(i + (c - 1), 1), :], gm[:, s:s + 1, :], ACT.Copy).then_inc(S("mid_hi"), 1)
            act.wait_ge(S("gpad_zero"), 1)
            for c in range(4):
                up_steps(0, c)
            with act.Fori(1, FB // 4) as i:
                for c in range(4):
                    up_steps(i * 4, c)
            for c in range(FB % 4):
                up_steps(FB // 4 * 4, c)
            up_silu(FB // 4 * 4, FB % 4)
            outs = 0
            for c in range(11):
                n = N_DOWN + c
                prep(n + 2, (n + 2) % RAW, n % 2)
                while outs < KT and (outs * FB + FB - 1) // 16 == c:
                    evict(y_down[:, outs, :], outs % 2, n, src=ps[:, outs % 2, 0:T])
                    outs += 1
            act.wait_ge(S("evicted"), J_DOWN + 8)
            norm(4, y_down, sq_down)

            for L in range(layers):
                n0, j0 = N_LAYER + L * LAYER_CH, J_LAYER + L * LAYER_J
                ns, sp_ = 5 + 4 * L, 4 + 7 * L
                act.wait_ge(S("x_new"), 2 + 2 * L)
                if L == 0:
                    act.dma_start(cu[:, 0:N_CB], io["consts_b"]).then_inc(S("consts_b"), 16)
                norm(ns, x, a6)
                split(sp_, a5, act_hi[1])
                act.wait_ge(S("lam_abs"), L + 1)
                act_(sm[:, 3, 0:8], sm[:, 3, 0:8], ACT.Exp, scale=-1.0).then_inc(S("lam_exp"), 1)
                def group(off, dst, after=(), n0=n0, j0=j0):
                    for c in range(4):
                        n = n0 + off + c
                        prep(n + 2, (n + 2) % RAW, n % 2)
                        evict(dst(c), (j0 + JL(off) + c) % 2, n)
                        if c < len(after) and after[c]:
                            after[c]()

                def to(t):
                    return lambda c: flat(t[:, 2 * c:2 * c + 2, :])

                def hi_of(e, src, hi):
                    return lambda: split(e, src, hi)

                def ff_exp():
                    act.wait_ge(S("ff_abs"), L + 1)
                    act_(sm[:, 3, 0:16], sm[:, 3, 0:16], ACT.Exp, scale=-1.0).then_inc(S("ff_exp"), 1)

                def fox_exp(h0):
                    act.wait_ge(S("fox_max"), L + 1)
                    for h in range(h0, h0 + 4):
                        for t in range(2):
                            s_ = fox_s[:, h, 0:P] if t == 0 else fox_s[:, h, P:3 * P]
                            c = t * 8 + h
                            act_(s_, s_, ACT.Exp, scale=P ** -0.5, bias=sm[:, 7, c:c + 1],
                                 accum_out=sm[:, 7, 16 + c:17 + c]).then_inc(S("fox_e"), 1)

                def fox_tr(h0):
                    for h in range(h0, h0 + 4):
                        act.wait_ge(S("fox_t_mm"), L * 8 + h + 1)
                        act_(fox_pt[:, h, :], ps[:, 4 + h % 4, 0:384], ACT.Copy).then_inc(S("fox_t_ev"), 1)

                def fox_out():
                    act.wait_ge(S("fox_o_mm"), L + 1)
                    act_(s4[:, :, :].rearrange("p (a b) n -> p a (b n)", a=4), ps[:, 4:8, :], ACT.Copy).then_inc(S("fox_o"), 1)

                def fox_split():
                    act.wait_ge(S("fox_o"), L + 1)
                    for hf in range(2):
                        act_(act_hi[0][:, 4 * hf:4 * hf + 4, :], s4[:, 4 * hf:4 * hf + 4, :], ACT.Copy).then_inc(S("split_hi"), 1)

                def tanh_gate(t, name, n_done):
                    def f():
                        act.wait_ge(S("evicted"), n_done)
                        act_(t[:, :, :], t[:, :, :], ACT.Tanh, scale=0.5).then_inc(S(name), 1)
                    return f

                def ret_out():
                    act.wait_ge(S("ret_o_mm"), L + 1)
                    act_(s4[:, :, :].rearrange("p (a b) n -> p a (b n)", a=4), ps[:, 4:8, :], ACT.Copy).then_inc(S("ret_o"), 1)

                def ret_sq():
                    act.wait_ge(S("ret_mean"), L + 1)
                    act_(s1[:, :, :], s4[:, :, :], ACT.Square).then_inc(S("ret_sq"), 1)

                def ret_std():
                    act.wait_ge(S("ret_ss"), L + 1)
                    act_(sm[:, 5, 0:8], sm[:, 5, 0:8], ACT.Sqrt, scale=1.0 / T, bias=eps[:, :]).then_inc(S("ret_std"), 1)

                def ret_gate():
                    act.wait_ge(S("lru_v"), L + 1)
                    act.wait_ge(S("evicted"), j0 + JL(L_G1))
                    act_(s1[:, :, :], s3[:, :, :], ACT.Tanh, scale=0.5).then_inc(S("ret_gtanh"), 1)

                def lru_gates(bs):
                    for b in bs:
                        bank = (4 if b < 8 else 0) + b % 8 // 2
                        dst = s7 if b < 8 else s8
                        act_(dst[:, b % 8, :], ps[:, bank, b % 2 * T:b % 2 * T + T], ACT.Tanh, scale=0.5,
                             bias=gs[:, 3, b:b + 1] if b < 8 else sm[:, 4, b - 8:b - 7]).then_inc(S("lru_ev"), 1)

                def lru_th():
                    act.wait_ge(S("lru_ev"), 16 * (L + 1))
                    for b in range(8):
                        act_(s6[:, b, :], s7[:, b, :], ACT.Tanh, scale=sm[:, 6, 16 + b:17 + b], bias=sm[:, 6, 16 + b:17 + b])\
                            .then_inc(S("lru_th"), 1)

                def lru_a():
                    act.wait_ge(S("lru_th"), 8 * (L + 1))
                    for b in range(8):
                        act_(s7[:, b, :], s7[:, b, :], ACT.Exp, scale=sm[:, 6, 24 + b:25 + b], bias=sm[:, 6, 24 + b:25 + b])\
                            .then_inc(S("lru_a"), 1)

                def lru_sqrt():
                    act.wait_ge(S("lru_v"), L + 1)
                    act_(s6[:, :, :], s6[:, :, :], ACT.Sqrt).then_inc(S("lru_sqrt"), 1)

                def gelu():
                    act.wait_ge(S("gelu_in"), L + 1)
                    act_(s1[:, :, :], s1[:, :, :], ACT.Tanh, scale=math.sqrt(2.0 / math.pi)).then_inc(S("gelu_tanh"), 1)

                job(n0 + L_FQK, j0 + L_FQK, 8, lambda i: s01[:, :, :].rearrange("p (a b) n -> p a (b n)", b=2)[:, bass.ds(i, 1), :])
                group(L_FV, lambda c: vtok_f[:, :, c * T:(c + 1) * T], [None, None, None, ff_exp])
                group(L_G2, to(s3))
                group(L_RQK, to(s6), [None, None, lambda: fox_exp(0), lambda: fox_exp(4)])
                act.wait_ge(S("mods_done"), 4 + L)
                group(L_RV, lambda c: vtok_r[:, :, c * T:(c + 1) * T], [None, None, lambda: fox_tr(0), lambda: fox_tr(4)])
                group(L_LX, to(s8), [fox_out, fox_split])
                group(L_FOXO, to(s0), [tanh_gate(s3, "g2_tanh", j0 + L_RQK), None, ret_out])
                group(L_LY, to(s2), [None, None, None, hi_of(sp_ + 2, s5, act_hi[0])])
                n = n0 + L_LRU
                act.wait_ge(S("lru_x_mm"), L + 1)
                lru_gates(range(8, 16))
                prep(n + 2, (n + 2) % RAW, n % 2)
                act.wait_ge(S("chunk_done"), n + 1)
                lru_gates(range(0, 4))
                act.wait_ge(S("merge"), 2 * L + 1)

                def rest():
                    lru_gates(range(4, 8))

                def ret_gates():
                    ret_gate()
                    lru_sqrt()
                group(L_RG, to(s3), [rest, lru_th, lru_a, ret_sq])
                group(L_G1, to(s5), [ret_std])
                act.wait_ge(S("ret_tr"), L + 1)
                group(L_G0, to(s4), [ret_gates, hi_of(sp_ + 3, s3, act_hi[0])])
                group(L_RETO, to(s3), [gelu, tanh_gate(s5, "g1_tanh", j0 + JL(L_G1) + 4), tanh_gate(s4, "g0_tanh", j0 + JL(L_RETO)),
                                       hi_of(sp_ + 4, s2, act_hi[0])])
                group(L_LRUO, to(s7))
                split(sp_ + 5, s0, act_hi[1])
                group(L_WOUT, to(s5))
                act.wait_ge(S("evicted"), j0 + JL(L_MLP))
                norm(ns + 1, a5, a6)
                act.wait_ge(S("x_new"), 3 + 2 * L)
                norm(ns + 2, x, a6)
                split(sp_ + 6, a5, act_hi[1])
                for hf in range(2):
                    n = n0 + L_MLP + 16 * hf
                    j = j0 + JL(L_MLP) + 16 * hf

                    def mlp_steps(i, c, n=n, j=j, hf=hf):
                        s = (j + c) % 2
                        e = 8 * (2 * L + hf) + i + c
                        evict(relu[:, s, :], s, i + (n + c), ACT.Relu)
                        act.wait_ge(S("mlp_sq"), e + 1)
                        act_(mlp_hi[:, bass.ds((i + c) * 2, 2), :], rsq[:, s, :].rearrange("p (b t) -> p b t", b=2), ACT.Copy)\
                            .then_inc(S("mlp_hi"), 1)
                    job(n, j, 8, None, hook=mlp_steps)
                    dst = a4 if hf == 0 else a5
                    job(n + 8, j + 8, 8, lambda i: dst[:, bass.ds(i, 1), :], sl=slice(0, T))
                act.wait_ge(S("y_sum"), L + 1)
                norm(ns + 3, a5, a6)

        @block.vector
        def _(dve):
            order = Order(dve, "dve_order")
            tt, ts, stt = nc.vector.tensor_tensor, nc.vector.tensor_scalar, nc.vector.scalar_tensor_tensor
            red = nc.vector.tensor_reduce

            def prep(n, s4, s2):
                if isinstance(n, int) and n >= total:
                    return
                dve.wait_ge(S("hi_ready"), n + 1)
                tt(w_lo[:, s2, :], raw[:, s4, :], w_hi[:, s2, :].bitcast(f32), ALU.subtract).then_inc(S("lo_ready"), 1)

            def job(n0, count, hook=None):
                def four(i, m):
                    for c in range(m):
                        n = n0 + c + 2
                        prep(i + n, n % RAW, n % 2)
                        if hook:
                            hook(i, c)
                looped = loop_part(n0, count)
                if looped:
                    with dve.Fori(0, looped // 4) as i:
                        four(i * 4, 4)
                for r in range(looped, count, 4):
                    four(r, min(4, count - r))

            def rs(k, src, dst):
                dve.wait_ge(S("norm_std"), k + 1)
                nc.vector.reciprocal(rstd[:, :], std[:, :]).then_inc(S("norm_rstd"), 1)
                dve.wait_ge(S("norm_rstd"), k + 1)
                order(tt(dst[:, :, :], src[:, :, :], bmid(rstd[:, :], KT), ALU.mult))

            def split_lo(e, src, hi, lo):
                for hf in range(2):
                    o = slice(4 * hf, 4 * hf + 4)
                    dve.wait_ge(S("split_hi"), 2 * e + hf + 1)
                    tt(lo[:, o, :], src[:, o, :], hi[:, o, :].bitcast(f32), ALU.subtract).then_inc(S("act_ready"), 1)

            def modulate(k, e, src, dst, g, sh, hi, lo):
                rs(k, src, dst)
                for b in range(KT):
                    ins = ts(dst[:, b, :], dst[:, b, :], g[:, b:b + 1], sh[:, b:b + 1], ALU.mult, ALU.add)
                    if b % 4 == 3:
                        ins.then_inc(S("split_src"), 1)
                    else:
                        order.mark(ins)
                dve.wait_ge(S("split_src"), 2 * source(e) + 2)
                split_lo(e, dst, hi, lo)

            def residual(k, y, g):
                rs(k, y, y)
                for b in range(KT):
                    ins = stt(x[:, b, :], y[:, b, :], g[:, b:b + 1], x[:, b, :], ALU.mult, ALU.add)
                    if b == KT - 1:
                        ins.then_inc(S("x_new"), 1)
                    else:
                        order.mark(ins)

            def softplus(dst, z, e, m, n):
                t1, t2 = sm[:, 11, 0:n], z
                order(ts(t1, e, 2.0, None, ALU.add))
                order(nc.vector.reciprocal(t1, t1))
                order(tt(t2, e, t1, ALU.mult))
                order(tt(t1, t2, t2, ALU.mult))
                order(ts(e, t1, 1.0 / 17, 1.0 / 15, ALU.mult, ALU.add))
                for odd in (13, 11, 9, 7, 5, 3, 1):
                    order(tt(e, e, t1, ALU.mult))
                    order(ts(e, e, 1.0 / odd, None, ALU.add))
                order(tt(e, e, t2, ALU.mult))
                order(stt(dst, e, 2.0, m, ALU.mult, ALU.add))

            nc.vector.memset(eps[:, :], EPS).then_inc(S("eps_set"), 1)
            dve.wait_ge(S("c_tanh"), 1)
            c3 = cs[:, :, :].rearrange("p a k -> p (a k)")
            order(ts(cth[:, :], cth[:, :], 0.5, 0.5, ALU.mult, ALU.add))
            tt(c3, cth[:, :], vec[:, 0:3 * KT], ALU.mult).then_inc(S("cs_ready"), 1)
            dve.wait_ge(S("cs_ready"), 1)
            for m in range(8):
                s = m % 2
                dve.wait_ge(S(f"ada_loaded{s}"), (m // 2 + 1) * 16)
                r = ctx_prod[:, :].rearrange("p (k n) -> p k n", k=KT)
                tt(r, ada_raw[:, s, :].rearrange("p (k n) -> p k n", k=KT), bc(cs[:, 1, :], T), ALU.mult)\
                    .then_inc(S("ctx_read"), 1)
                dve.wait_ge(S("ctx_read"), m + 1)
                order(tt(r[:, 0:4, :], r[:, 0:4, :], r[:, 4:8, :], ALU.add))
                order(tt(r[:, 0:2, :], r[:, 0:2, :], r[:, 2:4, :], ALU.add))
                ins = tt(ctx_acc[:, m, :], r[:, 0, :], r[:, 1, :], ALU.add)
                if m < 7:
                    order(ins)
                else:
                    ins.then_inc(S("ctx_acc_done"), 1)
            prep(0, 0, 0)
            prep(1, 1, 1)
            dve.wait_ge(S("sw_hi"), 1)
            tt(sw_lo[:, :], sw[:, 0:256], sw_hi[:, :].bitcast(f32), ALU.subtract).then_inc(S("sw_lo"), 1)
            dve.wait_ge(S("modctx_mm"), 1)
            order(tt(mod_ctx[:, :], ps[:, 6, 0:16], V("b_ada", 16), ALU.add))
            dve.wait_ge(S("mod_mm"), 1)
            tt(mod[:, 0:16], ps[:, 5, 0:16], V("b_ada", 16), ALU.add).then_inc(S("mods_done"), 1)
            dve.wait_ge(S("mods_done"), 1)
            order(stt(gs[:, 0, :], mod_ctx[:, 8:16], 1.0, V("g_pre_mix", KT), ALU.add, ALU.mult))
            order(stt(gs[:, 1, :], mod[:, 8:16], 1.0, V("g_pre_mix", KT), ALU.add, ALU.mult))
            dve.wait_ge(S("norm_sq"), 1)
            modulate(0, 0, xc, norm_h1, gs[:, 0, :], mod_ctx[:, 0:8], act_hi[0], act_lo[0])
            dve.wait_ge(S("act_ready"), 2)
            modulate(1, 1, x, norm_h1, gs[:, 1, :], mod[:, 0:8], act_hi[1], act_lo[1])
            nc.vector.memset(pre_kv[:, :, :, 0:T + 2:T + 1], 0.0).then_inc(S("pads"), 1)
            nc.vector.memset(pre_q[:, :, 0:1], 0.0).then_inc(S("pads"), 1)
            nc.vector.memset(pre_q[:, :, T + 1:T + 2], 0.0).then_inc(S("pads"), 1)
            job(N_Q, 2)
            job(N_KV, 4)
            job(N_UZ, 4)
            dve.wait_ge(S("evicted"), 10)
            for b in range(4):
                w = lambda i: V("conv", 1, i * 12 + b)
                order(ts(y_q[:, b, :], pre_q[:, b, 0:T], w(0), None, ALU.mult))
                order(stt(y_q[:, b, :], pre_q[:, b, 1:T + 1], w(1), y_q[:, b, :], ALU.mult, ALU.add))
                order(stt(y_q[:, b, :], pre_q[:, b, 2:T + 2], w(2), y_q[:, b, :], ALU.mult, ALU.add))
            for b in range(8):
                w = lambda i: V("conv", 1, i * 12 + 4 + b)
                order(ts(y_kv[:, b, :, :], pre_kv[:, b, :, 0:T], w(0), None, ALU.mult))
                order(stt(y_kv[:, b, :, :], pre_kv[:, b, :, 1:T + 1], w(1), y_kv[:, b, :, :], ALU.mult, ALU.add))
                ins = stt(y_kv[:, b, :, :], pre_kv[:, b, :, 2:T + 2], w(2), y_kv[:, b, :, :], ALU.mult, ALU.add)
                if b < 7:
                    order.mark(ins)
                else:
                    ins.then_inc(S("conv"), 1)
            dve.wait_ge(S("ab_mm"), 1)
            abp = ps[:, 7, 0:64].rearrange("p (t c) -> p t c", t=4)
            s32 = lambda i: sm[:, i, :].rearrange("p (t c) -> p t c", t=4)
            order(nc.vector.tensor_copy(s32(2), abp[:, :, 0:8]))
            order(tt(s32(1), abp[:, :, 8:16], bmid(V("dt_bias", 8), 4), ALU.add))
            order(ts(s32(0), s32(1), 0.0, None, ALU.max))
            order(ts(sm[:, 3, :], sm[:, 1, :], -1.0, None, ALU.mult))
            tt(sm[:, 3, :], sm[:, 3, :], sm[:, 1, :], ALU.max).then_inc(S("ab_abs"), 1)
            dve.wait_ge(S("conv_tanh"), 1)
            order(stt(flat(y_q[:, :, :]), flat(th_q[:, :, :]), 1.0, flat(y_q[:, :, :]), ALU.add, ALU.mult))
            stt(flat(y_kv[:, :, :, :]), flat(th_kv[:, :, :, :]), 1.0, flat(y_kv[:, :, :, :]), ALU.add, ALU.mult).then_inc(S("y_ready"), 1)
            dve.wait_ge(S("ab_act"), 1)
            order(ts(sm[:, 2, :], sm[:, 2, :], 0.5, 0.5, ALU.mult, ALU.add))
            softplus(sm[:, 0, :], sm[:, 1, :], sm[:, 3, :], sm[:, 0, :], 32)
            tneg = sm[:, 4, 0:8]
            order(ts(tneg, tneg, -1.0, None, ALU.mult))
            tt(s32(1), s32(0), bmid(tneg, 4), ALU.mult).then_inc(S("g_ready"), 1)
            for g in range(10):
                dve.wait_ge(S("tr_mm"), g + 1)
                src = ps[:, 4 + g % 3, :]
                if g < 4:
                    ins = nc.vector.tensor_copy(flat(k_tok[:, g, :, :]), src)
                elif g < 8:
                    ins = ts(flat(v_tok[:, g - 4, :, :]), src, 0.5, None, ALU.mult)
                else:
                    ins = nc.vector.tensor_copy(flat(q_tok[:, g - 8, :, :]), src)
                ins.then_inc(S("tr_ev"), 1)
            dve.wait_ge(S("kq_sq"), 1)
            order(red(sm[:, 5, 0:16], sq_kq[:, :, :], AX, ALU.add))
            red(sm[:, 5, 16:24], sq_q[:, :, :], AX, ALU.add).then_inc(S("kq_ss"), 1)
            dve.wait_ge(S("kq_std"), 1)
            order(nc.vector.reciprocal(sm[:, 5, 0:24], sm[:, 5, 0:24]))
            order(ts(sm[:, 5, 0:16], sm[:, 5, 0:16], 0.5, None, ALU.mult))
            order(ts(sm[:, 5, 16:24], sm[:, 5, 16:24], 0.5 * P ** -0.5, None, ALU.mult))
            k3 = k_tok[:, :, :, :].rearrange("p t h n -> p (t h) n")
            q3 = q_tok[:, :, :, :].rearrange("p t h n -> p (t h) n")
            order(tt(k3, k3, bc(sm[:, 5, 0:16], P), ALU.mult))
            tt(q3, q3, bc(sm[:, 5, 16:24], P), ALU.mult).then_inc(S("kq_norm"), 1)
            dve.wait_ge(S("gc_mm"), 1)
            order(nc.vector.tensor_copy(sm[:, 6:8, :], ps[:, 7, 0:64].rearrange("p (a c) -> p a c", a=2)))
            order(nc.vector.tensor_copy(sm[:, 8:10, :], sm[:, 6:8, :]))
            tt(sm[:, 10, :], sm[:, 7, :], sm[:, 6, :], ALU.subtract).then_inc(S("gc_diff"), 1)
            dve.wait_ge(S("gc_exp"), 1)
            order(tt(sm[:, 10, :], sm[:, 10, :], sm[:, 2, :], ALU.mult))
            ts(sm[:, 7, :], sm[:, 8, :], -1.0, None, ALU.mult).then_inc(S("gc_ev"), 1)
            dve.wait_ge(S("gc_ev"), 1)
            tril = cu[:, A_TRIL:A_TRIL + P]
            for d in range(2):
                for t in range(4):
                    e = d * 4 + t
                    cols = slice(t * 8 + d * 4, t * 8 + d * 4 + 4)
                    dve.wait_ge(S("mat_mm"), e + 1)
                    if e > 0:
                        dve.wait_ge(S("mat_ev"), e)
                    b4, b5, b6 = (ps[:, i, :].rearrange("p (h n) -> p h n", h=4) for i in (4, 5, 6))
                    order(tt(dec[:, :, :], b6, bc(sm[:, 6, cols], P), ALU.subtract))
                    ts(dec[:, :, :], dec[:, :, :], 0.0, None, ALU.min).then_inc(S("dec_min"), 1)
                    dve.wait_ge(S("dec_exp"), e + 1)
                    order(tt(dem[:, :, :], dec[:, :, :], bmid(triu if d == 0 else tril, 4), ALU.mult))
                    order(tt(Bm[:, t, :, :], b4, dem[:, :, :], ALU.mult))
                    order(tt(Bm[:, t, :, :], Bm[:, t, :, :], bc(sm[:, 2, cols], P), ALU.mult))
                    if t >= 2:
                        order(tt(attnT[:, d, t - 2, :, :], b5, dem[:, :, :], ALU.mult))
                    strict = cu[:, A_STR + d * P:A_STR + (d + 1) * P]
                    tt(Bm[:, t, :, :], Bm[:, t, :, :], bmid(strict, 4), ALU.mult).then_inc(S("mat_ev"), 1)
                idb = bmid(ident, 16)
                order(nc.vector.tensor_copy(Tm[:, :, :, :].rearrange("p t h n -> p (t h) n"), idb))
                nc.vector.tensor_copy(U[:, d, :, :, :].rearrange("p t h n -> p (t h) n"), idb).then_inc(S("inv_init"), 1)
                dve.wait_ge(S("inv_init"), d + 1)
                for lvl in range(7):
                    size = 1 << lvl
                    pcol, rcol = (0, 1) if d == 0 else (1, 0)
                    mask = cu[:, A_LVL + (d * 7 + lvl) * P:A_LVL + (d * 7 + lvl + 1) * P]

                    def half(ap, which):
                        return ap.rearrange("p h (g two s) -> p h g two s", two=2, s=size)[:, :, :, which, :]
                    for g in range(4):
                        dve.wait_ge(S("inv_x_mm"), d * 28 + lvl * 4 + g + 1)
                        tt(X[:, g, :, :], ps[:, 4 + g, :].rearrange("p (h n) -> p h n", h=4), bmid(mask, 4), ALU.mult)\
                            .then_inc(S("inv_x"), 1)
                    for g in range(4):
                        dve.wait_ge(S("inv_u_mm"), d * 28 + lvl * 4 + g + 1)
                        b = ps[:, 4 + g, :].rearrange("p (w h g s) -> p w h g s", w=2, h=4, s=size)
                        if lvl < 6:
                            Tg = half(Tm[:, g, :, :], pcol)
                            order(tt(Tg, Tg, b[:, 0], ALU.subtract))
                        Ug = half(U[:, d, g, :, :], rcol)
                        tt(Ug, Ug, b[:, 1], ALU.subtract).then_inc(S("inv_u"), 1)
                dve.wait_ge(S("inv_u"), d * 28 + 28)
            order(nc.vector.memset(St[:, :, :, :], 0.0))
            nc.vector.memset(o_tok[:, :, :, :], 0.0).then_inc(S("scan_init"), 1)
            dve.wait_ge(S("scan_init"), 1)
            oc = 0
            for st in range(4):
                tile = lambda d: (st if d == 0 else [1, 0, 3, 2][st])
                cols = lambda d: slice(tile(d) * 8 + d * 4, tile(d) * 8 + d * 4 + 4)
                b4 = lambda i: ps[:, i, :].rearrange("p (h n) -> p h n", h=4)
                for d in range(2):
                    dve.wait_ge(S("scan_p_mm"), st * 2 + d + 1)
                    order(tt(Rm[:, d, :, :], b4(4 + d), bc(sm[:, 7, cols(d)], P), ALU.mult))
                    tt(Rm[:, d, :, :], Rm[:, d, :, :], v_tok[:, tile(d), :, :], ALU.add).then_inc(S("scan_r"), 1)
                if st >= 2:
                    for d in range(2):
                        order(tt(tmp_s[:, d, :, :], b4(6 + d), bc(sm[:, 8, cols(d)], P), ALU.mult))
                        o_ = o_tok[:, tile(d) - 2, :, :]
                        tt(o_, o_, tmp_s[:, d, :, :], ALU.add).then_inc(S("scan_o"), 1)
                        oc += 1
                        dve.wait_ge(S("scan_o"), oc)
                for d in range(2):
                    dve.wait_ge(S("scan_w_mm"), st * 2 + d + 1)
                    order(tt(vn[:, d, :, :], b4(4 + d), bc(sm[:, 2, cols(d)], P), ALU.mult))
                    tt(v2[:, d, :, :], b4(4 + d), bc(sm[:, 10, cols(d)], P), ALU.mult).then_inc(S("scan_v"), 1)
                for d in range(2):
                    dve.wait_ge(S("scan_s_mm"), st * 2 + d + 1)
                    if st >= 2:
                        o_ = o_tok[:, tile(d) - 2, :, :]
                        tt(o_, o_, b4(6 + d), ALU.add).then_inc(S("scan_o"), 1)
                        oc += 1
                        dve.wait_ge(S("scan_o"), oc)
                    order(tt(St[:, d, :, :], St[:, d, :, :], bc(sm[:, 9, cols(d)], P), ALU.mult))
                    tt(St[:, d, :, :], St[:, d, :, :], b4(4 + d), ALU.add).then_inc(S("scan_s"), 1)
                    dve.wait_ge(S("scan_s"), st * 2 + d + 1)
            dve.wait_ge(S("o_sq"), 1)
            red(sm[:, 5, 0:8], o_sq[:, :, :], AX, ALU.add).then_inc(S("o_ss"), 1)
            dve.wait_ge(S("z_tanh"), 1)
            order(stt(th_z[:, :, :], th_z[:, :, :], 1.0, uz[:, 4:8, :], ALU.add, ALU.mult))
            order(ts(th_z[:, :, :], th_z[:, :, :], 0.5, None, ALU.mult))
            dve.wait_ge(S("o_std"), 1)
            order(nc.vector.reciprocal(sm[:, 5, 0:8], sm[:, 5, 0:8]))
            o3 = o_tok[:, :, :, :].rearrange("p t h n -> p (t h) n")
            tt(o3, o3, bc(sm[:, 5, 0:8], P), ALU.mult).then_inc(S("o_norm"), 1)
            dve.wait_ge(S("o_tr"), 1)
            dve.wait_ge(S("split_src"), 5)
            stt(yfd[:, 4:8, :], ps[:, 6:8, :].rearrange("p a (b t) -> p (a b) t", b=2), V("g_gdn"), th_z[:, :, :],
                ALU.mult, ALU.mult).then_inc(S("split_src"), 1)
            dve.wait_ge(S("split_src"), 6)
            split_lo(2, yfd, act_hi[1], act_lo[1])
            dve.wait_ge(S("mod_mm"), 2)
            tt(mod[:, 16:24], ps[:, 5, 0:8], V("b_ada", 8, 16), ALU.add).then_inc(S("mods_done"), 1)
            dve.wait_ge(S("mods_done"), 2)
            order(tt(gs[:, 0, :], mod[:, 16:24], V("g_post_mix", KT), ALU.mult))
            job(N_OUT1, 4)
            residual(2, y1, gs[:, 0, :])
            dve.wait_ge(S("mod_mm"), 3)
            tt(mod[:, 24:48], ps[:, 5, 8:32], V("b_ada", 24, 24), ALU.add).then_inc(S("mods_done"), 1)
            dve.wait_ge(S("mods_done"), 3)
            order(stt(gs[:, 1, :], mod[:, 32:40], 1.0, V("g_pre_ffn", KT), ALU.add, ALU.mult))
            order(tt(gs[:, 2, :], mod[:, 40:48], V("g_post_ffn", KT), ALU.mult))
            dve.wait_ge(S("x_new"), 1)
            modulate(3, 3, x, norm_h1, gs[:, 1, :], mod[:, 24:32], act_hi[1], act_lo[1])
            dve.wait_ge(S("act_ready"), 8)
            nc.vector.memset(gpad[:, :, :, :], 0.0).then_inc(S("gpad_zero"), 1)
            base = order.n
            UP_MARKS = 8

            def up_lo(e, s):
                dve.wait_ge(S("mid_hi"), e - 1)
                b = bass.ds(e - 2, 1)
                tt(mid_lo1[:, b, :], gm[:, s:s + 1, :], mid_hi1[:, b, :].bitcast(f32), ALU.subtract).then_inc(S("mid_ready"), 1)

            def up_silu_a(e, s):
                dve.wait_ge(S("gate_tanh"), e)
                order.mark(stt(gth[:, s, :], gth[:, s, :], 1.0, gacc[:, s, :], ALU.add, ALU.mult))

            def up_silu_b(s, bank, mark):
                dve.wait_ge(S("dve_order"), mark)
                stt(gm[:, s, :], gth[:, s, :], 0.5, ps[:, bank, 0:T], ALU.mult, ALU.mult).then_inc(S("evicted"), 1)

            def up_steps(i, c):
                n, s, e, first = N_UP + c, c % 2, i + c, isinstance(i, int) and i == 0
                order.n = base if first and c == 0 else i * UP_MARKS + (base + c * UP_MARKS - 1)
                w_slot, r_slot = n % 2, (n + 2) % RAW
                dve.wait_ge(S("gate_in"), e + 1)
                acc = gacc[:, s, :].rearrange("p (r w) -> p r w", r=ROWS)
                silu_mark = None
                for at_, tap in enumerate((0, 1, 2, 3, 5, 6, 7, 8)):
                    src = gpad[:, s, tap // 3:tap // 3 + ROWS, tap % 3:tap % 3 + GRID_W]
                    w = vec[:, bass.ds(e + (V1["dwc"] + tap * FB), 1)]
                    if at_:
                        dve.wait_ge(S("dve_order"), tap_mark)
                    ins = stt(acc, src, w, acc, ALU.mult, ALU.add)
                    if at_ < 7:
                        order.mark(ins)
                        tap_mark = order.n
                    else:
                        ins.then_inc(S("gconv"), 1)
                    if at_ == 0 and not (first and c < 2):
                        up_lo(e, s)
                    if 1 <= at_ < 5:
                        if at_ == 1:
                            dve.wait_ge(S("hi_ready"), i + (n + 3))
                        o = slice((at_ - 1) * 512, at_ * 512)
                        ins = tt(w_lo[:, w_slot, o], raw[:, r_slot, o], w_hi[:, w_slot, o].bitcast(f32), ALU.subtract)
                        if at_ == 4:
                            ins.then_inc(S("lo_ready"), 1)
                    if not (first and c == 0):
                        if at_ == 5:
                            up_silu_a(e, 1 - s)
                            silu_mark = order.n
                        if at_ == 6:
                            up_silu_b(1 - s, (c + 3) % 4, silu_mark)

            for c in range(4):
                up_steps(0, c)
            with dve.Fori(1, FB // 4) as i:
                for c in range(4):
                    up_steps(i * 4, c)
            for c in range(FB % 4):
                up_steps(FB // 4 * 4, c)
            order.n = base + FB * UP_MARKS - 1
            up_lo(FB, FB % 2)
            up_silu_a(FB, (FB - 1) % 2)
            up_silu_b((FB - 1) % 2, (FB - 1) % 4, order.n)
            up_lo(FB + 1, (FB - 1) % 2)
            job(N_DOWN, 11)
            residual(4, y_down, gs[:, 2, :])
            dve.wait_ge(S("x_new"), 2)

            for L in range(layers):
                n0 = N_LAYER + L * LAYER_CH
                j0 = J_LAYER + L * LAYER_J
                ns, sp_ = 5 + 4 * L, 4 + 7 * L
                v = lambda name, n=1, i=0: V(name, n, i, L)
                order(ts(sm[:, 6, 8:16], v("lam", 8), -1.0, None, ALU.mult))
                order(ts(sm[:, 6, 0:8], sm[:, 6, 8:16], 0.0, None, ALU.max))
                tt(sm[:, 3, 0:8], sm[:, 6, 8:16], v("lam", 8), ALU.max).then_inc(S("lam_abs"), 1)
                order(ts(gs[:, 3, :], v("b_a", 8), 0.5, None, ALU.mult))
                order(ts(sm[:, 4, 0:8], v("b_x", 8), 0.5, None, ALU.mult))
                dve.wait_ge(S("mod_mm"), 5 + 2 * L)
                tt(mod[:, :], ps[:, 5, 0:48], v("b_ada", 48), ALU.add).then_inc(S("mods_done"), 1)
                dve.wait_ge(S("mods_done"), 4 + L)
                order(stt(gs[:, 0, :], mod[:, 8:16], 1.0, v("g_pre_mix", KT), ALU.add, ALU.mult))
                modulate(ns, sp_, x, a5, gs[:, 0, :], mod[:, 0:8], act_hi[1], act_lo[1])
                order(tt(gs[:, 0, :], mod[:, 16:24], v("g_post_mix", KT), ALU.mult))
                order(stt(gs[:, 1, :], mod[:, 32:40], 1.0, v("g_pre_mlp", KT), ALU.add, ALU.mult))
                order(tt(gs[:, 2, :], mod[:, 40:48], v("g_post_mlp", KT), ALU.mult))
                dve.wait_ge(S("lam_exp"), L + 1)
                softplus(sm[:, 6, 0:8], sm[:, 6, 8:16], sm[:, 3, 0:8], sm[:, 6, 0:8], 8)
                order(ts(sm[:, 6, 16:24], sm[:, 6, 0:8], LRU_C / 2, None, ALU.mult))
                order(ts(sm[:, 6, 24:32], sm[:, 6, 0:8], -LRU_C / 2, None, ALU.mult))
                def group(off, after=(), n0=n0):
                    for c in range(4):
                        n = n0 + off + c
                        prep(n + 2, (n + 2) % RAW, n % 2)
                        for f in (after[c] if c < len(after) else ()):
                            f()

                fm = cu[:, B_FM:B_FM + T]

                def ff():
                    dve.wait_ge(S("ff_mm"), L + 1)
                    y16 = sm[:, 1, 0:16].rearrange("p (t h) -> p t h", t=2)
                    order(tt(y16, ps[:, 7, 0:16].rearrange("p (t h) -> p t h", t=2), bmid(v("b_f", 8), 2), ALU.add))
                    order(ts(sm[:, 2, 0:16], sm[:, 1, 0:16], -1.0, None, ALU.mult))
                    order(ts(sm[:, 0, 0:16], sm[:, 2, 0:16], 0.0, None, ALU.max))
                    tt(sm[:, 3, 0:16], sm[:, 2, 0:16], sm[:, 1, 0:16], ALU.max).then_inc(S("ff_abs"), 1)

                def ff_log():
                    dve.wait_ge(S("ff_exp"), L + 1)
                    softplus(sm[:, 0, 0:16], sm[:, 2, 0:16], sm[:, 3, 0:16], sm[:, 0, 0:16], 16)
                    ts(sm[:, 1, 0:16], sm[:, 0, 0:16], math.sqrt(P), None, ALU.mult).then_inc(S("nlf_ready"), 1)

                def cum():
                    dve.wait_ge(S("cum_mm"), L + 1)
                    ts(sm[:, 5, 0:16], ps[:, 7, 16:32], -1.0, None, ALU.mult).then_inc(S("cum_ev"), 1)
                    dve.wait_ge(S("cum_ev"), L + 1)
                    dve.wait_ge(S("consts_b"), 16)

                def fox_scores(h0):
                    for h in range(h0, h0 + 4):
                        bank = 4 + h % 4
                        dve.wait_ge(S("fox_s_mm"), L * 8 + h + 1)
                        order.mark(stt(fox_s[:, h, 0:P], ps[:, bank, 0:P], sm[:, 5, h:h + 1], fm[:, P:T], ALU.add, ALU.add))
                        stt(fox_s[:, h, P:3 * P], ps[:, bank, P:3 * P], sm[:, 5, 8 + h:9 + h], fm, ALU.add, ALU.add)\
                            .then_inc(S("fox_s_ev"), 1)

                def fox_max():
                    dve.wait_ge(S("fox_s_ev"), L * 8 + 8)
                    dve.wait_ge(S("dve_order"), order.n)
                    order(red(sm[:, 7, 0:8], fox_s[:, :, 0:P], AX, ALU.max, negate=True))
                    order(red(sm[:, 7, 8:16], fox_s[:, :, P:3 * P], AX, ALU.max, negate=True))
                    ts(sm[:, 7, 0:16], sm[:, 7, 0:16], P ** -0.5, None, ALU.mult).then_inc(S("fox_max"), 1)

                def fox_norm():
                    dve.wait_ge(S("fox_e"), 16 * (L + 1))
                    order(nc.vector.reciprocal(sm[:, 7, 16:32], sm[:, 7, 16:32]))
                    order(tt(fox_s[:, :, 0:P], fox_s[:, :, 0:P], bc(sm[:, 7, 16:24], P), ALU.mult))
                    tt(fox_s[:, :, P:3 * P], fox_s[:, :, P:3 * P], bc(sm[:, 7, 24:32], T), ALU.mult).then_inc(S("fox_p"), 1)

                def lo_of(e, src, which):
                    return lambda: split_lo(e, src, act_hi[which], act_lo[which])

                cos, sin = cu[:, B_COS:B_COS + T], cu[:, B_SIN:B_SIN + T]

                def rope_sin():
                    dve.wait_ge(S("rope_mm"), L + 1)
                    order(tt(s1, ps[:, 4:8, :].rearrange("p a (b t) -> p (a b) t", b=2), bmid(sin, 8), ALU.mult))

                def rope_cos():
                    order(tt(s6[:, :, :], s6[:, :, :], bmid(cos, 8), ALU.mult))

                def rope_add():
                    tt(s6[:, :, :], s6[:, :, :], s1, ALU.add).then_inc(S("rope_done"), 1)

                def ret_p():
                    dve.wait_ge(S("ret_s_mm"), L + 1)
                    tt(flat(s1), ps[:, 4:8, :].rearrange("p a b -> p (a b)"), cu[:, B_RET:B_RET + 2048], ALU.mult)\
                        .then_inc(S("ret_p"), 1)

                def fox_merge():
                    dve.wait_ge(S("evicted"), j0 + L_LY)
                    dve.wait_ge(S("g2_tanh"), L + 1)
                    stt(s0, s3[:, :, :], 1.0, s0, ALU.add, ALU.mult).then_inc(S("merge"), 1)

                def ret_mean():
                    dve.wait_ge(S("ret_o"), L + 1)
                    order(red(sm[:, 5, 0:8], s4[:, :, :], AX, ALU.add))
                    order(ts(sm[:, 5, 0:8], sm[:, 5, 0:8], 1.0 / T, None, ALU.mult))

                def ret_centre():
                    tt(s4[:, :, :], s4[:, :, :], bc(sm[:, 5, 0:8], T), ALU.subtract).then_inc(S("ret_mean"), 1)

                def ret_ss():
                    dve.wait_ge(S("ret_sq"), L + 1)
                    red(sm[:, 5, 0:8], s1, AX, ALU.add).then_inc(S("ret_ss"), 1)

                def ret_norm():
                    dve.wait_ge(S("ret_std"), L + 1)
                    order(nc.vector.reciprocal(sm[:, 5, 0:8], sm[:, 5, 0:8]))
                    tt(s4[:, :, :], s4[:, :, :], bc(sm[:, 5, 0:8], T), ALU.mult).then_inc(S("ret_norm"), 1)

                def ret_y():
                    dve.wait_ge(S("ret_gtanh"), L + 1)
                    order(stt(s3[:, :, :], s1, 1.0, s3[:, :, :], ALU.add, ALU.mult))
                    dve.wait_ge(S("ret_tr"), L + 1)
                    for hf in range(2):
                        o = slice(4 * hf, 4 * hf + 4)
                        stt(flat(s3[:, o, :]), ps[:, 4 + 2 * hf:6 + 2 * hf, :].rearrange("p a b -> p (a b)"), 0.5, flat(s3[:, o, :]),
                            ALU.mult, ALU.mult).then_inc(S("split_src"), 1)

                def conv(tap):
                    def f():
                        if tap == 3:
                            dve.wait_ge(S("evicted"), j0 + L_FOXO)
                        back = 3 - tap
                        for b in range(8):
                            w = v("conv_w", 1, tap * 8 + b)
                            if tap == 3:
                                ins = ts(s5[:, b, :], s8[:, b, :], w, v("conv_b", 1, b), ALU.mult, ALU.add)
                            else:
                                ins = stt(s5[:, b, back:T], s8[:, b, 0:T - back], w, s5[:, b, back:T], ALU.mult, ALU.add)
                            if tap == 0 and b % 4 == 3:
                                ins.then_inc(S("split_src"), 1)
                            else:
                                order.mark(ins)
                        dve.wait_ge(S("dve_order"), order.n)
                    return f

                def lru_ix():
                    dve.wait_ge(S("lru_ev"), 16 * L + 8)
                    stt(s8[:, :, :], s8[:, :, :], 1.0, s5[:, :, :], ALU.add, ALU.mult).then_inc(S("lru_ix"), 1)

                def gelu_a():
                    order(tt(s1, s2[:, :, :], s2[:, :, :], ALU.mult))
                    order(ts(s1, s1, 0.044715, 1.0, ALU.mult, ALU.add))

                def gelu_b():
                    tt(s1, s1, s2[:, :, :], ALU.mult).then_inc(S("gelu_in"), 1)

                def gelu_c():
                    dve.wait_ge(S("gelu_tanh"), L + 1)
                    order(stt(s2[:, :, :], s1, 1.0, s2[:, :, :], ALU.add, ALU.mult))

                def lru_a2():
                    dve.wait_ge(S("lru_a"), 8 * (L + 1))
                    order(tt(s1, s7[:, :, :], s7[:, :, :], ALU.mult))

                def lru_v():
                    order(stt(s6[:, :, :], s1, 1.0, s6[:, :, :], ALU.add, ALU.mult))
                    ts(s6[:, :, :], s6[:, :, :], 0.0, None, ALU.max).then_inc(S("lru_v"), 1)

                def lru_u():
                    dve.wait_ge(S("lru_sqrt"), L + 1)
                    dve.wait_ge(S("lru_ix"), L + 1)
                    order(stt(s8[:, :, :], s8[:, :, :], 0.5, s6[:, :, :], ALU.mult, ALU.mult))

                def lru_scan():
                    for b in range(8):
                        order.mark(nc.vector.tensor_tensor_scan(s1[:, b, :], s7[:, b, :], s8[:, b, :], 0.0, ALU.mult, ALU.add))
                    dve.wait_ge(S("dve_order"), order.n)

                def lru_y():
                    for hf in range(2):
                        o = slice(4 * hf, 4 * hf + 4)
                        stt(s2[:, o, :], s2[:, o, :], 0.5, s1[:, o, :], ALU.mult, ALU.mult).then_inc(S("split_src"), 1)

                def ret_gated():
                    dve.wait_ge(S("evicted"), j0 + JL(L_LRUO))
                    dve.wait_ge(S("g0_tanh"), L + 1)
                    order(stt(s3[:, :, :], s4[:, :, :], 1.0, s3[:, :, :], ALU.add, ALU.mult))

                def ret_merge():
                    tt(s0, s0, s3[:, :, :], ALU.add).then_inc(S("merge"), 1)
                    dve.wait_ge(S("merge"), 2 * L + 2)

                def lru_merge(hf):
                    def f():
                        o = slice(4 * hf, 4 * hf + 4)
                        dve.wait_ge(S("evicted"), j0 + JL(L_LRUO) + 2 * (hf + 1))
                        dve.wait_ge(S("g1_tanh"), L + 1)
                        order(stt(s7[:, o, :], s5[:, o, :], 1.0, s7[:, o, :], ALU.add, ALU.mult))
                        order(tt(s0[:, o, :], s0[:, o, :], s7[:, o, :], ALU.add))
                        ts(s0[:, o, :], s0[:, o, :], 0.5, None, ALU.mult).then_inc(S("split_src"), 1)
                    return f

                job(n0 + L_FQK, 8)
                group(L_FV, [[], [], [], [ff]])
                group(L_G2, [[ff_log], [], [cum], [lambda: fox_scores(0)]])
                group(L_RQK, [[lambda: fox_scores(4)], [fox_max]])
                group(L_RV, [[fox_norm]])
                group(L_LX, [[], [rope_sin], [lo_of(sp_ + 1, s4, 0)], [rope_cos]])
                group(L_FOXO, [[rope_add], [ret_p], [conv(3)], [conv(2)]])
                group(L_LY, [[fox_merge], [conv(1)], [conv(0)], [lo_of(sp_ + 2, s5, 0)]])
                n = n0 + L_LRU
                prep(n + 2, (n + 2) % RAW, n % 2)
                lru_ix()
                group(L_RG, [[], [ret_mean], [ret_centre], []])
                group(L_G1, [[ret_ss], [ret_norm], [lru_a2], [lru_v]])
                group(L_G0, [[], [ret_y], [lo_of(sp_ + 3, s3, 0)], [gelu_a, gelu_b]])
                group(L_RETO, [[lru_u], [gelu_c], [lru_scan], [lru_y, lo_of(sp_ + 4, s2, 0)]])
                group(L_LRUO, [[ret_gated], [ret_merge], [lru_merge(0)], [lru_merge(1)]])
                split_lo(sp_ + 5, s0, act_hi[1], act_lo[1])
                group(L_WOUT)
                residual(ns + 1, a5, gs[:, 0, :])
                dve.wait_ge(S("x_new"), 3 + 2 * L)
                modulate(ns + 2, sp_ + 6, x, a5, gs[:, 1, :], mod[:, 24:32], act_hi[1], act_lo[1])
                for hf in range(2):
                    n = n0 + L_MLP + 16 * hf
                    j = j0 + JL(L_MLP) + 16 * hf

                    def mlp_steps(i, c, j=j, hf=hf):
                        s = (j + c) % 2
                        e = 8 * (2 * L + hf) + i + c
                        dve.wait_ge(S("evicted"), i + (j + c + 1))
                        tt(rsq[:, s, :], relu[:, s, :], relu[:, s, :], ALU.mult).then_inc(S("mlp_sq"), 1)
                        dve.wait_ge(S("mlp_hi"), e + 1)
                        b = bass.ds((i + c) * 2, 2)
                        tt(mlp_lo[:, b, :], rsq[:, s, :].rearrange("p (b t) -> p b t", b=2), mlp_hi[:, b, :].bitcast(f32),
                           ALU.subtract).then_inc(S("mlp_ready"), 1)
                    job(n, 8, hook=mlp_steps)
                    job(n + 8, 8)
                dve.wait_ge(S("evicted"), j0 + LAYER_J)
                tt(a5[:, :, :], a5[:, :, :], a4[:, :, :], ALU.add).then_inc(S("y_sum"), 1)
                dve.wait_ge(S("y_sum"), L + 1)
                residual(ns + 3, a5, gs[:, 2, :])
                dve.wait_ge(S("x_new"), 4 + 2 * L)
        return print_left


def _constants():
    i = np.arange(P)
    triu = (i[:, None] <= i[None, :]).astype(np.float64)
    common = np.zeros((P, N_COMMON))
    common[:, C_ID:C_ID + P] = np.eye(P)
    common[:, C_TRIU:C_TRIU + P] = triu
    common[:, C_ONES:C_ONES + P] = 1.0
    common[:, C_OMEAN:C_OMEAN + P] = 1.0 / D
    a = np.zeros((P, N_CU))
    a[:, A_TRIL:A_TRIL + P] = triu.T
    a[:, A_STR:A_STR + P] = triu - np.eye(P)
    a[:, A_STR + P:A_STR + 2 * P] = triu.T - np.eye(P)
    for lvl in range(7):
        size = 1 << lvl
        group, second = i // (2 * size), i % (2 * size) >= size
        m = (group[:, None] == group[None, :]) & second[:, None] & ~second[None, :]
        a[:, A_LVL + lvl * P:A_LVL + (lvl + 1) * P] = m
        a[:, A_LVL + (7 + lvl) * P:A_LVL + (8 + lvl) * P] = m.T
    ang = 2 * np.pi * (i[:, None] * i[None, :] % P) / P
    a[:, A_CC:A_CC + P], a[:, A_SC:A_SC + P] = np.cos(ang), np.sin(ang)
    t = np.arange(T)
    ang = 2 * np.pi * (t[:, None] * t[None, :] % T) / T
    norm = 1.0 / math.sqrt(T * P)
    for tile in range(TT):
        a[:, A_CL + tile * T:A_CL + (tile + 1) * T] = np.cos(ang[tile * P:(tile + 1) * P]) * norm
        a[:, A_SL + tile * T:A_SL + (tile + 1) * T] = -np.sin(ang[tile * P:(tile + 1) * P]) * norm
    b = np.zeros((P, N_CU))
    b[:, B_PERM:B_PERM + P] = np.roll(np.eye(P), P // 2, axis=0)
    half = P // 2
    inv = np.float32(10000.0) ** (-np.arange(half, dtype=np.float32) / np.float32(half))
    ang = (inv[:, None] * t[None, :].astype(np.float32)).astype(np.float64)
    b[:, B_COS:B_COS + T] = np.concatenate([np.cos(ang)] * 2)
    b[:, B_SIN:B_SIN + T] = np.concatenate([-np.sin(ang), np.sin(ang)])
    for h in range(HEADS):
        gamma = 1.0 - 2.0 ** (-5.0 - h)
        w = gamma ** np.abs(t[:, None] - t[None, :]) * P ** -0.5
        w = np.where(t[:, None] // 64 <= t[None, :] // 64, w, 0.0)
        for m in range(TT):
            o = B_RET + (h * 2 + m) * T
            b[:, o:o + T] = w[m * P:(m + 1) * P]
    b[:, B_FM + P:B_FM + T] = np.where(i[None, :] <= i[:, None], 0.0, -1e30)
    return common.astype(np.float32), a.astype(np.float32), b.astype(np.float32)


def _columns_of(v):
    return np.asarray(v).reshape(-1, P).T


def _feat(w):
    k, n = w.shape
    c = w.reshape(k // P, P, n // P, P).transpose(2, 1, 0, 3)
    per = CH // (k // P * P)
    return c.reshape(-1, per, P, k // P * P).transpose(0, 2, 1, 3).reshape(-1, P, CH)


def _tok(w):
    n = w.shape[1]
    return w.reshape(KT, P, n // T, T).transpose(2, 1, 0, 3).reshape(-1, P, CH)


def _stream(a):
    w = np.asarray(a["w_in"])[0]
    u, q, k, v, z = w[:, 0:512], w[:, 512:1024], w[:, 1024:1536], w[:, 1536:2048], w[:, 2048:2560]
    parts = [_feat(q), _feat(k), _feat(v), _feat(u), _feat(z), _feat(np.asarray(a["w_out"])[0])]
    up = np.asarray(a["w_up"])[0].reshape(D, 2, FB, P).transpose(0, 2, 1, 3).reshape(D, 2 * D_FF)
    parts.append(_feat(up))
    down = np.asarray(a["w_down"])[0].reshape(FB, P, KT, P).transpose(2, 0, 1, 3).reshape(-1, 16, P, P)
    parts.append(down.transpose(0, 2, 1, 3).reshape(-1, P, CH))
    for L in range(LAYERS):
        g = lambda name: np.asarray(a[name])[L]
        w = g("w_in_2")
        cut = np.cumsum([0, 512, 512, 1024, 1024, 1024, 1024, 1024, 1024, 1024, 8, 3072])
        rq, rk, rv, rg, lx, ly, fq, fk, fv, ff, gates = (w[:, cut[i]:cut[i + 1]] for i in range(11))
        g0, g1, g2 = gates[:, 0:D], gates[:, D:2 * D], gates[:, 2 * D:]
        lru = np.concatenate([g("lru_w_a_2"), g("lru_w_x_2")]).transpose(1, 0, 2).reshape(1, P, CH)
        parts += [_feat(fq), _feat(fk), _tok(fv), _feat(g2), _feat(rq), _feat(rk), _tok(rv), _feat(lx),
                  _feat(g("fox_w_o_2")), _feat(ly), lru, _feat(rg), _feat(g1), _feat(g0),
                  _feat(g("ret_w_o_2")), _feat(g("lru_w_o_2")), _feat(g("w_out_2"))]
        w1, w2 = g("mlp_w1_2"), g("mlp_w2_2")
        for hf in range(2):
            parts += [_feat(w1[:, hf * 2048:(hf + 1) * 2048]), _feat(w2[hf * 2048:(hf + 1) * 2048])]
    return np.concatenate(parts)


def _vectors(a):
    out = np.zeros((P, NV), np.float32)

    def put(at, v):
        out[:, at:at + v.shape[1]] = v
    rows = lambda v: np.broadcast_to(np.asarray(v).reshape(1, -1), (P, np.asarray(v).size))
    for name in ("c", "c_ctx", "c_2", "b_ada", "g_pre_mix", "g_post_mix", "g_pre_ffn", "g_post_ffn", "g_gdn"):
        put(V1[name], _columns_of(a[name]))
    put(V1["conv"], _columns_of(a["w_qkv_conv"]))
    put(V1["dwc"], _columns_of(a["w_dwc"]))
    put(V1["dt_bias"], rows(a["dt_bias"]))
    put(V1["a_log"], rows(a["a_log"]))
    for L in range(LAYERS):
        at = VEC_FIRST + L * VEC_LAYER
        for name, key in (("b_ada", "ada_b_2"), ("g_pre_mix", "norm_pre_mix_2"), ("g_post_mix", "norm_post_mix_2"),
                          ("g_pre_mlp", "norm_pre_mlp_2"), ("g_post_mlp", "norm_post_mlp_2"), ("conv_w", "conv_w_2"),
                          ("conv_b", "conv_b_2"), ("b_a", "lru_b_a_2"), ("b_x", "lru_b_x_2"), ("lam", "lru_lambda_2")):
            put(at + VL[name], _columns_of(np.asarray(a[key])[L]))
        put(at + VL["b_f"], rows(np.asarray(a["fox_b_f_2"])[L]))
    return out


def arrays_of(inputs):
    a = {k: np.asarray(v) for k, v in inputs.items()}
    common, ca, cb = _constants()
    small = np.zeros((P, N_SW), np.float32)
    small[:, SW_AB:SW_AB + 128] = a["w_in"][0][:, 2560:2576].reshape(KT, P, 16).transpose(1, 0, 2).reshape(P, 128)
    for L in range(LAYERS):
        ff = a["w_in_2"][L][:, 8192:8200]
        small[:, SW_FF + L * 64:SW_FF + (L + 1) * 64] = ff.reshape(KT, P, 8).transpose(1, 0, 2).reshape(P, 64)
    small[:, SW_WF:] = a["w_fourier"][0].transpose(1, 0, 2).reshape(P, 512)
    ada = np.concatenate([_tok(a["w_ada"][0])] + [_tok(a["ada_w_2"][L]) for L in range(LAYERS)])
    feat = lambda t: np.ascontiguousarray(t[0].reshape(T, KT, P).transpose(2, 1, 0))
    return {"xT": feat(a["x"]), "ctxT": feat(a["ctx"]), "stream": _stream(a), "ada": ada, "small_w": small,
            "vecs": _vectors(a), "consts_common": common, "consts_a": ca[:, :N_CA], "consts_b": cb[:, :N_CB]}


def kernel(**inputs):
    import concourse.bacc as bacc
    from concourse.bass_utils import run_bass_kernel_spmd

    nc = bacc.Bacc("TRN2", target_bir_lowering=False, num_devices=1)
    arrays = {k: np.ascontiguousarray(v) for k, v in arrays_of(inputs).items()}
    io = {k: nc.dram_tensor(k, v.shape, mybir.dt.float32, kind="ExternalInput").ap() for k, v in arrays.items()}
    io["out"] = nc.dram_tensor("out", [P, KT, T], mybir.dt.float32, kind="ExternalOutput").ap()
    io["ada_part"] = nc.dram_tensor("ada_part", [24 * (1 + LAYERS), P, T], mybir.dt.float32).ap()
    build_program(nc, io)
    got = run_bass_kernel_spmd(nc, [arrays], core_ids=[0]).results[0]["out"]
    return np.ascontiguousarray(np.asarray(got).reshape(P, KT, T).transpose(2, 1, 0)).reshape(1, T, D)
```

```python
import math
from contextlib import ExitStack

import numpy as np

import concourse.bass as bass
from concourse import mybir

P = 128
D = 1024
KT = D // P
T = 256
TT = T // P
EPS = 1e-6
CH = 2048
RAW = 4
D_FF = 2816
FB = D_FF // P
GRID_W = 64
ROWS = T // GRID_W
HEADS = 4
MLP_B = 4096 // P
LRU_C = 8.0

N_Q, N_KV, N_UZ = 0, 2, 6
N_OUT1, N_UP, N_DOWN = 10, 14, 36
N_LAYER = 47
(L_FQK, L_FV, L_G2, L_RQK, L_RV, L_LX, L_FOXO, L_LY, L_LRU, L_RG, L_G1, L_G0, L_RETO, L_LRUO, L_WOUT, L_MLP) = (
    0, 8, 12, 16, 20, 24, 28, 32, 36, 37, 41, 45, 49, 53, 57, 61)
LAYER_CH = 93
LAYERS = 2

V1 = {}
VL = {}


def _columns():
    at = 0
    for name, n in (("c", KT), ("c_ctx", KT), ("c_2", KT), ("b_ada", 48), ("g_pre_mix", KT), ("g_post_mix", KT),
                    ("g_pre_ffn", KT), ("g_post_ffn", KT), ("conv", 36), ("g_gdn", 1), ("dwc", 9 * FB),
                    ("dt_bias", 8), ("a_log", 8)):
        V1[name] = at
        at += n
    first = at
    at = 0
    for name, n in (("b_ada", 48), ("g_pre_mix", KT), ("g_post_mix", KT), ("g_pre_mlp", KT), ("g_post_mlp", KT),
                    ("conv_w", 32), ("conv_b", 8), ("b_a", 8), ("b_x", 8), ("lam", 8), ("b_f", 8)):
        VL[name] = at
        at += n
    return first, at


VEC_FIRST, VEC_LAYER = _columns()
NV = VEC_FIRST + LAYERS * VEC_LAYER

C_ID, C_TRIU, C_ONES, C_OMEAN = 0, 128, 256, 384
N_COMMON = 512
A_TRIL, A_STR, A_LVL, A_CC, A_SC, A_CL, A_SL = 0, 128, 384, 384 + 14 * 128, 384 + 15 * 128, 384 + 16 * 128, 384 + 16 * 128 + 512
N_CA = A_SL + 512
B_PERM, B_COS, B_SIN, B_RET, B_FM = 0, 128, 384, 640, 640 + 2048
N_CB = B_FM + 256
N_CU = max(N_CA, N_CB)
SW_AB, SW_FF, SW_WF = 0, 128, 256
N_SW = 768


def build_program(nc, io, layers=LAYERS):
    f32, f32r = mybir.dt.float32, mybir.dt.float32r
    ALU, ACT, AX = mybir.AluOpType, mybir.ActivationFunctionType, mybir.AxisListType.X
    total = N_LAYER + LAYER_CH * layers
    ADA_FIRST = 8
    ADA_N = 24 * (1 + layers) - ADA_FIRST
    ctx = ExitStack()
    with ctx:
        place = [16512]

        def room(nbytes):
            at = place[0]
            place[0] += nbytes
            assert place[0] <= 229344, place[0]
            return at

        def at(name, shape, offset, dt=f32):
            return nc.alloc_sbuf_tensor_at(name, shape, dt, offset=offset)

        def new(name, shape, dt=f32):
            n = 4
            for s in shape[1:]:
                n *= s
            return at(name, shape, room((n + 31) // 32 * 32), dt)

        raw = new("raw", [P, RAW, CH])
        w_hi = new("w_hi", [P, 2, CH], f32r)
        w_lo = new("w_lo", [P, 2, CH], f32r)
        x = new("x", [P, KT, T])
        F = [room(8192) for _ in range(4)]
        act_hi = [at(f"act_hi{i}", [P, KT, T], F[i], f32r) for i in range(2)]
        act_lo = [at(f"act_lo{i}", [P, KT, T], F[2 + i], f32r) for i in range(2)]
        R = [room(8192), room(8192)]
        ada_raw = at("ada_raw", [P, 2, CH], R[0])
        ada_acc = new("ada_acc", [P, 2, T])
        cc = new("consts_common", [P, N_COMMON])
        cu = new("consts_stage", [P, N_CU])
        vec = new("vectors", [P, NV])
        sw = new("small_weights", [P, N_SW])
        sw_hi = new("small_hi", [P, 256], f32r)
        sw_lo = new("small_lo", [P, 256], f32r)
        cs = new("silu_c", [P, 3, KT])
        cth = new("silu_c_tanh", [P, 3 * KT])
        mod = new("mod", [P, 48])
        mod_ctx = new("mod_ctx", [P, 16])
        gs = new("gain_scale", [P, 4, KT])
        eps = new("eps", [P, 1])
        std = new("std", [P, T])
        rstd = new("rstd", [P, T])
        sm = new("smalls", [P, 12, 32])
        A = [room(8192) for _ in range(7)]
        ident, triu, ones, omean = (cc[:, o:o + P] for o in (C_ID, C_TRIU, C_ONES, C_OMEAN))

        ps = ctx.enter_context(nc.psum_tensor("ps", [P, 8, 512], f32))
        sems = {}

        def S(name):
            if name not in sems:
                sems[name] = ctx.enter_context(nc.semaphore(name))
            return sems[name]

        for s in range(RAW):
            S(f"raw_loaded{s}")
        block = ctx.enter_context(nc.Block())

        class Order:

            def __init__(self, eng, name):
                self.eng, self.sem, self.n = eng, S(name), 0

            def mark(self, ins):
                ins.then_inc(self.sem, 1)
                self.n = self.n + 1

            def __call__(self, ins):
                self.mark(ins)
                self.eng.wait_ge(self.sem, self.n)

        def bc(ap, n):
            ap = ap.unsqueeze(len(ap.shape))
            return ap.to_broadcast(list(ap.shape[:-1]) + [n])

        def bmid(ap, n):
            ap = ap.unsqueeze(1)
            return ap.to_broadcast([ap.shape[0], n, ap.shape[2]])

        def flat(ap):
            s = ap.shape
            return ap if len(s) == 2 else ap.rearrange("p a b -> p (a b)") if len(s) == 3 else ap.rearrange("p a b c -> p (a b c)")

        def V(name, n=1, i=0, layer=None):
            o = V1[name] if layer is None else VEC_FIRST + layer * VEC_LAYER + VL[name]
            return vec[:, o + i:o + i + n]

        pre_kv = at("pre_kv", [P, 8, 2, T + 2], A[0])
        pre_q = at("pre_q", [P, 4, T + 2], A[0] + 16512)
        assert 16512 + 4 * 258 * 4 <= 24576
        uz = at("uz", [P, 8, T], A[3])
        y_kv = at("y_kv", [P, 8, 2, T], A[4])
        y_q = at("y_q", [P, 4, T], A[6])
        th_kv = at("th_kv", [P, 8, 2, T], A[0])
        th_q = at("th_q", [P, 4, T], A[0] + 16384)
        k_tok = at("k_tok", [P, 4, 4, P], F[0])
        v_tok = at("v_tok", [P, 4, 4, P], F[1])
        q_tok = at("q_tok", [P, 2, 4, P], F[2])
        sq_kq = at("sq_kq", [P, 16, P], A[0])
        sq_q = at("sq_q", [P, 8, P], A[1])
        kT = at("kT", [P, 4, 4, P], A[1])
        qT = at("qT", [P, 2, 4, P], F[2] + 4096)
        attnT = at("attnT", [P, 2, 2, 4, P], A[2])
        U = at("U", [P, 2, 4, 4, P], A[4])
        Bm = at("Bm", [P, 4, 4, P], A[0])
        Tm = at("Tm", [P, 4, 4, P], A[6])
        X = at("X", [P, 4, 4, P], F[3])
        dec = at("dec", [P, 2, 4, P], F[3])
        dem = at("dem", [P, 2, 4, P], F[3] + 4096)
        St = at("state", [P, 2, 4, P], A[0])
        o_tok = at("o_tok", [P, 2, 4, P], A[0] + 4096)
        Rm = at("Rm", [P, 2, 4, P], A[6])
        vn = at("vn", [P, 2, 4, P], A[6] + 4096)
        v2 = at("v2", [P, 2, 4, P], F[3])
        tmp_s = at("tmp_s", [P, 2, 4, P], F[3] + 4096)
        o_sq = at("o_sq", [P, 8, P], A[6])
        th_z = at("th_z", [P, 4, T], F[2])
        yfd = at("yfd", [P, 8, T], A[6])
        m1 = at("m1", [P, 4, 2, P], A[2])
        Z = at("Z", [P, 2, 4, 2, P], A[1])
        norm_sq1, norm_h1 = at("norm_sq1", [P, KT, T], A[4]), at("norm_h1", [P, KT, T], A[5])
        xc = at("xc", [P, KT, T], A[3])
        ada_f, ada_a, ada_6 = at("ada_f", [P, 4, CH], F[0]), at("ada_a", [P, 3, CH], A[0]), at("ada_6", [P, 1, CH], A[6])
        mod_rows = at("mod_rows", [2, CH], F[0])
        ada_first = [ada_f[:, i, :] for i in range(4)] + [ada_a[:, i, :] for i in range(3)] + [ada_6[:, 0, :]]
        ada_in16 = at("ada_in16", [P, 16, T], A[0])
        ada_in = at("ada_in", [P, 16, T], R[0])
        y1 = at("y1", [P, KT, T], A[5])
        mid_hi1 = at("mid_hi1", [P, FB, T], A[0], f32r)
        mid_lo1 = at("mid_lo1", [P, FB, T], A[0] + FB * T * 4, f32r)
        ft = A[0] + 2 * FB * T * 4
        gpad = at("gpad", [P, 2, ROWS + 2, GRID_W + 2], ft)
        gacc = at("gacc", [P, 2, T], ft + 3168)
        gth = at("gth", [P, 2, T], ft + 3168 + 2048)
        gm = at("gm", [P, 2, T], ft + 3168 + 4096)
        assert ft + 3168 + 6144 <= A[6] + 8192
        y_down = at("y_down", [P, KT, T], F[0])
        sq_down = at("sq_down", [P, KT, T], F[2])
        s01 = at("s01", [P, 2 * KT, T], A[0])
        s0, s1 = s01[:, 0:KT, :], s01[:, KT:2 * KT, :]
        s2, s3, s4, s5, s6 = (at(f"s{i}", [P, KT, T], A[i]) for i in range(2, 7))
        s7, s8 = at("s7", [P, KT, T], R[0]), at("s8", [P, KT, T], R[1])
        a4, a5, a6 = s4, s5, s6
        vtok_f, vtok_r = at("vtok_f", [P, 2, D], A[2]), at("vtok_r", [P, 2, D], R[0])
        mlp_hi = at("mlp_hi", [P, 16, T], A[0], f32r)
        mlp_lo = at("mlp_lo", [P, 16, T], A[2], f32r)
        relu = at("relu", [P, 2, 512], A[6])
        rsq = at("rsq", [P, 2, 512], A[6] + 4096)
        fox_s = at("fox_s", [P, 8, 384], A[4])
        fox_pt = at("fox_pt", [P, 8, 384], A[0])

        MAT_BANK = (4, 1)
        J_OUT1, J_UP, J_DOWN = 10, 14, 36
        J_LAYER = 44
        def JL(o):
            return o if o <= L_LRU else o - 1
        LAYER_J = 92

        def loop_part(n0, count):
            k = count // 4 * 4 - (4 if n0 + count + 2 > total and count % 4 == 0 else 0)
            return k if k >= 8 else 0

        def source(e):
            return e if e < 4 else 4 + (e - 4) // 7 * 6 + ((e - 4) % 7 - ((e - 4) % 7 > 1))

        @block.sync
        def _(sp):
            sp.dma_start(vec[:, :], io["vecs"]).then_inc(S("vec_loaded"), 16)
            sp.dma_start(cc[:, :], io["consts_common"]).then_inc(S("x_loaded"), 16)
            sp.dma_start(xc[:, :, :], io["ctxT"]).then_inc(S("x_loaded"), 16)
            sp.dma_start(x[:, :, :], io["xT"]).then_inc(S("x_loaded"), 16)
            for m in range(ADA_FIRST):
                sp.dma_start(ada_first[m], io["ada"][m]).then_inc(S(f"ada_first{m}"), 16)

            def load(n, s):
                sp.dma_start(raw[:, s:s + 1, :], io["stream"][bass.ds(n, 1)].rearrange("a p n -> p a n"))\
                  .then_inc(S(f"raw_loaded{s}"), 16)

            load(0, 0)
            load(1, 1)
            sp.dma_start(sw[:, :], io["small_w"]).then_inc(S("small_loaded"), 16)
            sp.dma_start(cu[:, 0:N_CA], io["consts_a"]).then_inc(S("small_loaded"), 16)
            for s in range(2, RAW):
                load(s, s)
            rounds = total // RAW
            with sp.Fori(1, rounds) as i:
                for s in range(RAW):
                    sp.wait_ge(S("lo_ready"), i * RAW + (s - RAW + 1))
                    load(i * RAW + s, s)
            for n in range(rounds * RAW, total):
                sp.wait_ge(S("lo_ready"), n - RAW + 1)
                load(n, n % RAW)
            sp.wait_ge(S("x_new"), 2 * (2 + 2 * layers))
            sp.dma_start(io["out"], x[:, :, :]).then_inc(S("stored"), 16)
            sp.wait_ge(S("stored"), 16)

        @block.gpsimd
        def _(pool):
            order = Order(pool, "pool_order")

            def load(m, s):
                pool.dma_start(ada_raw[:, s:s + 1, :], io["ada"][bass.ds(m + ADA_FIRST, 1)].rearrange("a p n -> p a n"))\
                    .then_inc(S(f"ada_loaded{s}"), 16)

            def chunk(half, s, which, more):
                m = half * 2 + s
                order.n = m * 4
                pool.wait_ge(S(f"ada_loaded{s}"), half * 16 + 16)
                r = ada_raw[:, s, :].rearrange("p (k n) -> p k n", k=KT)
                order(nc.gpsimd.tensor_tensor(r, r, bc(cs[:, which, :], T), ALU.mult))
                order(nc.gpsimd.tensor_tensor(r[:, 0:4, :], r[:, 0:4, :], r[:, 4:8, :], ALU.add))
                order(nc.gpsimd.tensor_tensor(r[:, 0:2, :], r[:, 0:2, :], r[:, 2:4, :], ALU.add))
                if not (isinstance(half, int) and half == 0):
                    pool.wait_ge(S(f"ada_stored{s}"), half * 16)
                order(nc.gpsimd.tensor_tensor(ada_acc[:, s, :], r[:, 0, :], r[:, 1, :], ALU.add))
                pool.dma_start(io["ada_part"][bass.ds(m + ADA_FIRST, 1)].rearrange("a p n -> p a n"), ada_acc[:, s:s + 1, :])\
                    .then_inc(S(f"ada_stored{s}"), 16)
                if more:
                    load(m + 2, s)

            load(0, 0)
            load(1, 1)
            pool.wait_ge(S("cs_ready"), 1)
            for s in range(2):
                chunk(0, s, 0, True)
            with pool.Fori(1, 8 if layers else 7) as i:
                for s in range(2):
                    chunk(i, s, 0, True)
            if layers:
                with pool.Fori(8, ADA_N // 2 - 1) as i:
                    for s in range(2):
                        chunk(i, s, 2, True)
            for s in range(2):
                chunk(ADA_N // 2 - 1, s, 2 if layers else 0, False)
            for s in range(2):
                pool.wait_ge(S(f"ada_stored{s}"), ADA_N // 2 * 16)
            for L in range(layers):
                if L > 0:
                    pool.wait_ge(S("split_src"), 2 * source(4 + 7 * (L - 1) + 5) + 2)
                first = 24 * (L + 1)
                pool.dma_start(ada_in[:, :, :], io["ada_part"][first:first + 16].rearrange("c p n -> p c n"))\
                    .then_inc(S("ada_layer"), 16)
                pool.wait_ge(S("mod_mm"), 4 + 2 * L)
                pool.dma_start(ada_in[:, 0:8, :], io["ada_part"][first + 16:first + 24].rearrange("c p n -> p c n"))\
                    .then_inc(S("ada_layer"), 16)

        @block.tensor
        def _(pe):
            mm, tr = nc.tensor.matmul, nc.tensor.transpose

            def mm3(out, ah, al, bh, bl, first, last):
                mm(out, ah, bh, start=first, stop=False)
                mm(out, ah, bl, start=False, stop=False)
                return mm(out, al, bh, start=False, stop=last)

            def begin(n, j, strict=False):
                pe.wait_ge(S("lo_ready"), n + 1)
                if j is None:
                    return
                if strict:
                    pe.wait_ge(S("evicted"), j)
                elif not isinstance(j, int) or j >= 2:
                    pe.wait_ge(S("evicted"), j - 1)

            def feat_chunk(wp, bank, s, ready=None):
                if ready is not None:
                    pe.wait_ge(S("act_ready"), ready - 1)
                for b in range(2):
                    for k in range(KT):
                        if ready is not None and b == 0 and k == 4:
                            pe.wait_ge(S("act_ready"), ready)
                        o = (b * KT + k) * P
                        last = mm3(ps[:, bank, b * T:(b + 1) * T], w_hi[:, wp, o:o + P], w_lo[:, wp, o:o + P],
                                   act_hi[s][:, k, :], act_lo[s][:, k, :], k == 0, k == KT - 1)
                return last

            def tok_chunk(wp, bank, s):
                for t in range(TT):
                    for k in range(KT):
                        last = mm3(ps[:, bank, t * T:(t + 1) * T], act_hi[s][:, k, t * P:(t + 1) * P],
                                   act_lo[s][:, k, t * P:(t + 1) * P], w_hi[:, wp, k * T:(k + 1) * T],
                                   w_lo[:, wp, k * T:(k + 1) * T], k == 0, k == KT - 1)
                return last

            def job(fn, n0, j0, count, s, strict=False):
                def four(i, m):
                    for c in range(m):
                        begin(i + (n0 + c), i + (j0 + c), strict and isinstance(i, int) and i + c == 0)
                        fn((n0 + c) % 2, (j0 + c) % 2, s).then_inc(S("chunk_done"), 1)
                if count >= 8:
                    if strict:
                        four(0, 4)
                        with pe.Fori(1, count // 4) as i:
                            four(i * 4, 4)
                    else:
                        with pe.Fori(0, count // 4) as i:
                            four(i * 4, 4)
                    if count % 4:
                        four(count // 4 * 4, count % 4)
                else:
                    four(0, count)

            def deep_chunk(wp, bank, s, ready=None):
                for k in range(16):
                    if ready is not None and k >= 10 and k % 2 == 0:
                        pe.wait_ge(S("mlp_ready"), ready - 7 + k // 2)
                    last = mm3(ps[:, bank, 0:T], w_hi[:, wp, k * P:(k + 1) * P], w_lo[:, wp, k * P:(k + 1) * P],
                               mlp_hi[:, k, :], mlp_lo[:, k, :], k == 0, k == 15)
                return last

            def norm_half(k, sq, hf):
                pe.wait_ge(S("norm_sq"), 2 * k + hf + 1)
                for b in range(4 * hf, 4 * hf + 4):
                    last = mm(ps[:, 7, 0:T], omean, sq[:, b, :], start=b == 0, stop=b == KT - 1)
                if hf == 1:
                    last.then_inc(S("norm_ms"), 1)

            def norm(k, sq):
                norm_half(k, sq, 0)
                norm_half(k, sq, 1)

            def keep_warm(n, bank=6):
                for _ in range(n):
                    mm(ps[:, bank, :], ident, cc[:, :], start=True, stop=True)

            def mods(loads, src, first, count, col0, loaded="ada_in"):
                pe.wait_ge(S(loaded), 16 * loads)
                for c in range(first, first + count):
                    o = c % 2 * P
                    last = mm(ps[:, 5, col0 + c:col0 + c + 1], src[:, c // 2, o:o + P], ones[:, 0:1],
                              start=True, stop=True)
                last.then_inc(S("mod_mm"), 1)

            pe.wait_ge(S("x_loaded"), 3 * 16)
            norm(0, norm_sq1)
            pe.wait_ge(S("cs_ready"), 1)
            for m in range(ADA_FIRST):
                pe.wait_ge(S(f"ada_first{m}"), 16)
                for k in range(KT):
                    last = mm(ps[0:2, 1 + m // 2, m % 2 * T:(m % 2 + 1) * T], cs[:, 0:2, k],
                              ada_first[m][:, k * T:(k + 1) * T], start=k == 0, stop=k == KT - 1)
            last.then_inc(S("mod_rows_mm"), 1)
            pe.wait_ge(S("mod_rows_ev"), 1)
            for c in range(2 * ADA_FIRST):
                last = mm(ps[:, 5, 2 * c:2 * c + 2], mod_rows[:, c * P:(c + 1) * P], ident[0:2, 0:2], start=True, stop=True)
            last.then_inc(S("mod_mm"), 1)
            pe.wait_ge(S("norm_std"), 1)
            norm(1, norm_sq1)
            pe.wait_ge(S("act_ready"), 4)
            job(feat_chunk, N_Q, 0, 2, 1)
            for c in range(4):
                n = N_KV + c
                begin(n, n)
                bank = n % 2 * 2
                if c == 0:
                    pe.wait_ge(S("evicted"), 2)
                feat_chunk(n % 2, bank, 0)
                feat_chunk(n % 2, bank + 1, 1).then_inc(S("chunk_done"), 1)
            pe.wait_ge(S("sw_lo"), 1)
            pe.wait_ge(S("small_loaded"), 2 * 16)
            for t in range(4):
                s, tt = t // 2, t % 2
                for k in range(KT):
                    last = mm3(ps[:, 7, t * 16:t * 16 + 16], act_hi[s][:, k, tt * P:tt * P + P],
                               act_lo[s][:, k, tt * P:tt * P + P], sw_hi[:, k * 16:k * 16 + 16],
                               sw_lo[:, k * 16:k * 16 + 16], k == 0, k == KT - 1)
            last.then_inc(S("ab_mm"), 1)
            job(feat_chunk, N_UZ, N_UZ, 4, 1, strict=True)
            pe.wait_ge(S("y_ready"), 1)
            groups = [("k", t) for t in range(4)] + [("v", t) for t in range(4)] + [("q", t) for t in range(2)]
            for g, (kind, t) in enumerate(groups):
                if g >= 3:
                    pe.wait_ge(S("tr_ev"), g - 2)
                for h in range(HEADS):
                    src = y_q[:, h, t * P:(t + 1) * P] if kind == "q" else \
                        y_kv[:, h + (4 if kind == "v" else 0), t // 2, t % 2 * P:t % 2 * P + P]
                    last = tr(ps[:, 4 + g % 3, h * P:(h + 1) * P], src, ident)
                last.then_inc(S("tr_mm"), 1)
            pe.wait_ge(S("kq_norm"), 1)
            pe.wait_ge(S("tr_ev"), 10)
            for g in range(6):
                if g >= 3:
                    pe.wait_ge(S("trb_ev"), g - 2)
                for h in range(HEADS):
                    src = k_tok[:, g, h, :] if g < 4 else q_tok[:, g - 4, h, :]
                    last = tr(ps[:, 4 + g % 3, h * P:(h + 1) * P], src, ident)
                last.then_inc(S("trb_mm"), 1)
            pe.wait_ge(S("g_ready"), 1)
            g_ = sm[:, 1, :].rearrange("p (t c) -> p t c", t=4)
            tril = cu[:, A_TRIL:A_TRIL + P]
            for t in range(4):
                mm(ps[:, 7, t * 8:t * 8 + 4], triu, g_[:, t, 0:4], start=True, stop=True)
                mm(ps[:, 7, t * 8 + 4:t * 8 + 8], tril, g_[:, t, 4:8], start=True, stop=True)
                last = mm(ps[:, 7, 32 + t * 8:32 + t * 8 + 8], ones, g_[:, t, :], start=True, stop=True)
            last.then_inc(S("gc_mm"), 1)
            pe.wait_ge(S("trb_ev"), 6)
            pe.wait_ge(S("gc_ev"), 1)
            inv = 0
            seen_ev = 0
            for d in range(2):
                for t in range(4):
                    e = d * 4 + t
                    bank = MAT_BANK[e % 2]
                    if e > 1:
                        pe.wait_ge(S("mat_ev"), e - 1)
                    for h in range(HEADS):
                        mm(ps[:, bank, h * P:(h + 1) * P], kT[:, t, h, :], kT[:, t, h, :], start=True, stop=True)
                    if t >= 2:
                        for h in range(HEADS):
                            mm(ps[:, bank + 1, h * P:(h + 1) * P], kT[:, t, h, :], qT[:, t - 2, h, :], start=True, stop=True)
                    for h in range(HEADS):
                        col = d * 4 + h
                        last = mm(ps[:, bank + 2, h * P:(h + 1) * P], g_[:, t, col:col + 1].to_broadcast([P, P]),
                                  triu if d == 0 else tril, start=True, stop=True)
                    last.then_inc(S("mat_mm"), 1)
                    if t >= 1:
                        keep_warm(3 if t < 3 else 6, bank=0)
                pe.wait_ge(S("mat_ev"), 4 * (d + 1))
                for lvl in range(7):
                    size = 1 << lvl
                    pcol, rcol = (0, 1) if d == 0 else (1, 0)
                    def half(ap, which):
                        return ap.rearrange("p (g two s) -> p g two s", two=2, s=size)[:, :, which, :]
                    for g in range(4):
                        if lvl > 0:
                            pe.wait_ge(S("inv_u"), d * 28 + (lvl - 1) * 4 + g + 1)
                        for h in range(HEADS):
                            last = mm(ps[:, 4 + g, h * P:(h + 1) * P], Bm[:, g, h, :],
                                      ident if lvl == 0 else Tm[:, g, h, :], start=True, stop=True)
                        last.then_inc(S("inv_x_mm"), 1)
                    if lvl == 0:
                        keep_warm(3, bank=0)
                        continue
                    for g in range(4):
                        pe.wait_ge(S("inv_x"), d * 24 + (lvl - 1) * 4 + g + 1)
                        for h in range(HEADS):
                            if lvl < 6:
                                mm(ps[:, 4 + g, h * 64:(h + 1) * 64], U[:, d, g, h, :], half(X[:, g, h, :], pcol),
                                   start=True, stop=True)
                            last = mm(ps[:, 4 + g, 256 + h * 64:256 + (h + 1) * 64], X[:, g, h, :],
                                      half(U[:, d, g, h, :], rcol), start=True, stop=True)
                        last.then_inc(S("inv_u_mm"), 1)
                pe.wait_ge(S("inv_u"), d * 28 + 28)
            pe.wait_ge(S("scan_init"), 1)
            for st in range(4):
                for d in range(2):
                    e = st * 2 + d
                    t = (st if d == 0 else [1, 0, 3, 2][st])
                    if st > 0:
                        pe.wait_ge(S("scan_s"), e - 1)
                    for h in range(HEADS):
                        last = mm(ps[:, 4 + d, h * P:(h + 1) * P], kT[:, t, h, :], St[:, d, h, :], start=True, stop=True)
                    if t >= 2:
                        if st == 3:
                            pe.wait_ge(S("scan_o"), 2 * (d + 1))
                        for h in range(HEADS):
                            last = mm(ps[:, 6 + d, h * P:(h + 1) * P], qT[:, t - 2, h, :], St[:, d, h, :], start=True, stop=True)
                    last.then_inc(S("scan_p_mm"), 1)
                for d in range(2):
                    e = st * 2 + d
                    t = (st if d == 0 else [1, 0, 3, 2][st])
                    pe.wait_ge(S("scan_r"), e + 1)
                    for h in range(HEADS):
                        last = mm(ps[:, 4 + d, h * P:(h + 1) * P], U[:, d, t, h, :], Rm[:, d, h, :], start=True, stop=True)
                    last.then_inc(S("scan_w_mm"), 1)
                for d in range(2):
                    e = st * 2 + d
                    t = (st if d == 0 else [1, 0, 3, 2][st])
                    pe.wait_ge(S("scan_v"), e + 1)
                    for h in range(HEADS):
                        last = mm(ps[:, 4 + d, h * P:(h + 1) * P], k_tok[:, t, h, :], v2[:, d, h, :], start=True, stop=True)
                    if st >= 2:
                        pe.wait_ge(S("scan_o"), (st - 2) * 4 + d * 1 + 1)
                        for h in range(HEADS):
                            last = mm(ps[:, 6 + d, h * P:(h + 1) * P], attnT[:, d, t - 2, h, :], vn[:, d, h, :], start=True, stop=True)
                    last.then_inc(S("scan_s_mm"), 1)
            pe.wait_ge(S("scan_s"), 8)
            CC, SC = cu[:, A_CC:A_CC + P], cu[:, A_SC:A_SC + P]
            pe.wait_ge(S("scan_o"), 8)
            for g in range(4):
                wf = sw[:, SW_WF + g * P:SW_WF + (g + 1) * P]
                o = g % 2 * T
                mm(ps[:, 4 + g // 2, o:o + P], CC, wf, start=True, stop=True)
                last = mm(ps[:, 4 + g // 2, o + P:o + T], SC, wf, start=True, stop=True)
            last.then_inc(S("four_mm"), 1)
            pe.wait_ge(S("four_ev"), 1)
            for t in range(2):
                for g in range(4):
                    last = mm(ps[:, 4 + t * 2 + g // 2, g % 2 * T:g % 2 * T + T], uz[:, g, t * P:(t + 1) * P],
                              flat(m1[:, g, :, :]), start=True, stop=True)
            last.then_inc(S("four_mm"), 1)
            pe.wait_ge(S("four_ev"), 2)
            for g in range(4):
                for t in range(2):
                    for m, base in enumerate((A_CL, A_SL)):
                        last = mm(ps[:, 4 + g // 2, g % 2 * T:g % 2 * T + T], Z[:, t, g, m, :],
                                  cu[:, base + t * T:base + (t + 1) * T], start=(t + m == 0), stop=(t + m == 2))
            last.then_inc(S("four_mm"), 1)
            pe.wait_ge(S("o_norm"), 1)
            for h in range(HEADS):
                for t in range(2):
                    last = tr(ps[:, 6 + h // 2, h % 2 * T + t * P:h % 2 * T + t * P + P], o_tok[:, t, h, :], ident)
            last.then_inc(S("o_tr"), 1)
            pe.wait_ge(S("act_ready"), 6)
            mods(1, ada_in16, 0, 8, 0)
            job(feat_chunk, N_OUT1, J_OUT1, 3, 1, strict=True)
            norm_half(2, norm_sq1, 0)
            job(feat_chunk, N_OUT1 + 3, J_OUT1 + 3, 1, 1)
            norm_half(2, norm_sq1, 1)
            mods(1, ada_in16, 8, 24, 0)
            norm(3, norm_sq1)
            keep_warm(9)
            pe.wait_ge(S("act_ready"), 8)
            def up(i, m):
                for c in range(m):
                    pe.wait_ge(S("lo_ready"), i + (N_UP + c + 1))
                    pe.wait_ge(S("evicted"), i + (J_UP + c - 3) if not isinstance(i, int) or i > 0 else J_UP)
                    feat_chunk((N_UP + c) % 2, c % 4, 1).then_inc(S("chunk_done"), 1)
            up(0, 4)
            with pe.Fori(1, FB // 4) as i:
                up(i * 4, 4)
            up(FB // 4 * 4, FB % 4)
            if layers:
                pe.wait_ge(S("mods_done"), 3)
                mods(1, ada_in, 0, 32, 0, "ada_layer")
            pe.wait_ge(S("mid_ready"), FB - 3)
            for o in range(KT):
                for k in range(FB):
                    i = o * FB + k
                    n, b = N_DOWN + i // 16, i % 16
                    if b == 0:
                        pe.wait_ge(S("lo_ready"), n + 1)
                    if o == 0 and k >= FB - 3:
                        pe.wait_ge(S("mid_ready"), k + 1)
                    if k == 0:
                        pe.wait_ge(S("evicted"), J_DOWN + (o - 1 if o >= 1 else 0))
                    last = mm3(ps[:, o % 2, 0:T], w_hi[:, n % 2, b * P:(b + 1) * P], w_lo[:, n % 2, b * P:(b + 1) * P],
                               mid_hi1[:, k, :], mid_lo1[:, k, :], k == 0, k == FB - 1)
                    if b == 15:
                        last.then_inc(S("chunk_done"), 1)
                if o == 5:
                    norm_half(4, sq_down, 0)
            norm_half(4, sq_down, 1)
            if layers:
                mods(2, ada_in, 0, 16, 32, "ada_layer")

            for L in range(layers):
                n0, j0 = N_LAYER + L * LAYER_CH, J_LAYER + L * LAYER_J
                ns, ar = 5 + 4 * L, 8 + 14 * L
                keep_warm(6 if L > 0 else 2)
                norm(ns, a6)
                keep_warm(9)
                def group(fn, off, src, after=(), ready=None, n0=n0, j0=j0):
                    for c in range(4):
                        begin(n0 + off + c, j0 + JL(off) + c)
                        more = {"ready": ready} if c == 0 and ready is not None else {}
                        fn((n0 + off + c) % 2, (j0 + JL(off) + c) % 2, src, **more).then_inc(S("chunk_done"), 1)
                        if c < len(after) and after[c]:
                            after[c]()

                nlf = sm[:, 1, 0:16].rearrange("p (t h) -> p t h", t=2)

                def ff():
                    for t in range(2):
                        for k in range(KT):
                            o = SW_FF + L * 64 + k * 8
                            last = mm3(ps[:, 7, t * 8:t * 8 + 8], act_hi[1][:, k, t * P:(t + 1) * P],
                                       act_lo[1][:, k, t * P:(t + 1) * P], sw_hi[:, o:o + 8], sw_lo[:, o:o + 8],
                                       k == 0, k == KT - 1)
                    last.then_inc(S("ff_mm"), 1)

                def cum():
                    pe.wait_ge(S("nlf_ready"), L + 1)
                    mm(ps[:, 7, 16:24], triu, nlf[:, 0, :], start=True, stop=True)
                    mm(ps[:, 7, 24:32], ones, nlf[:, 0, :], start=True, stop=False)
                    mm(ps[:, 7, 24:32], triu, nlf[:, 1, :], start=False, stop=True).then_inc(S("cum_mm"), 1)

                def fox_scores(h0):
                    if h0 == 0:
                        pe.wait_ge(S("evicted"), j0 + L_FV)
                        pe.wait_ge(S("cum_ev"), L + 1)
                    for h in range(h0, h0 + 4):
                        if h >= 4:
                            pe.wait_ge(S("fox_s_ev"), L * 8 + h - 3)
                        q, k, bank = s0[:, h, :], s1[:, h, :], 4 + h % 4
                        t0, t1 = ps[:, bank, 0:P], ps[:, bank, P:P + T]
                        mm(t0, q[:, 0:P], k[:, 0:P], start=True, stop=False)
                        mm(t0, nlf[:, 0, h:h + 1].to_broadcast([P, P]), triu, start=False, stop=True)
                        mm(t1, q[:, P:T], k, start=True, stop=False)
                        mm(t1, nlf[:, 0, h:h + 1].to_broadcast([P, P]), cc[:, C_TRIU:C_TRIU + T], start=False, stop=False)
                        mm(ps[:, bank, T:T + P], nlf[:, 1, h:h + 1].to_broadcast([P, P]), triu, start=False, stop=True)\
                            .then_inc(S("fox_s_mm"), 1)

                def fox_tr(h0):
                    if h0 == 0:
                        pe.wait_ge(S("fox_p"), L + 1)
                    for h in range(h0, h0 + 4):
                        if h >= 4:
                            pe.wait_ge(S("fox_t_ev"), L * 8 + h - 3)
                        bank = 4 + h % 4
                        tr(ps[:, bank, 0:P], fox_s[:, h, 0:P], ident)
                        tr(ps[:, bank, P:2 * P], fox_s[:, h, P:2 * P], ident)
                        tr(ps[:, bank, 2 * P:3 * P], fox_s[:, h, 2 * P:3 * P], ident).then_inc(S("fox_t_mm"), 1)

                def fox_out():
                    pe.wait_ge(S("fox_t_ev"), L * 8 + 8)
                    for h in range(8):
                        o = h % 2 * T
                        v_ = vtok_f[:, :, h * P:(h + 1) * P]
                        mm(ps[:, 4 + h // 2, o:o + T], v_[:, 0, :], fox_pt[:, h, 0:T], start=True, stop=False)
                        last = mm(ps[:, 4 + h // 2, o + P:o + T], v_[:, 1, :], fox_pt[:, h, T:T + P], start=False, stop=True)
                    last.then_inc(S("fox_o_mm"), 1)

                def rope():
                    pe.wait_ge(S("fox_o"), L + 1)
                    for b in range(8):
                        last = mm(ps[:, 4 + b // 2, b % 2 * T:b % 2 * T + T], cu[:, B_PERM:B_PERM + P], s6[:, b, :],
                                  start=True, stop=True)
                    last.then_inc(S("rope_mm"), 1)

                def ret_scores():
                    pe.wait_ge(S("rope_done"), L + 1)
                    for h in range(HEADS):
                        for m in range(2):
                            last = mm(ps[:, 4 + h, m * T:(m + 1) * T], s6[:, 4 + h, m * P:(m + 1) * P], s6[:, h, :],
                                      start=True, stop=True)
                    last.then_inc(S("ret_s_mm"), 1)

                def ret_out():
                    pe.wait_ge(S("ret_p"), L + 1)
                    for t in range(2):
                        for h in range(HEADS):
                            out = ps[:, 4 + t * 2 + h // 2, h % 2 * T:h % 2 * T + T]
                            for m in range(t + 1):
                                last = mm(out, s1[:, h * 2 + m, t * P:(t + 1) * P], vtok_r[:, m, h * T:(h + 1) * T],
                                          start=m == 0, stop=m == t)
                    last.then_inc(S("ret_o_mm"), 1)

                def ret_tr():
                    pe.wait_ge(S("ret_norm"), L + 1)
                    pe.wait_ge(S("lru_ev"), 16 * (L + 1))
                    o_ = s4[:, :, :].rearrange("p (t h) n -> p t h n", t=2)
                    for b in range(8):
                        for t in range(2):
                            last = tr(ps[:, 4 + b // 2, b % 2 * T + t * P:b % 2 * T + t * P + P],
                                      o_[:, t, b // 2, b % 2 * P:b % 2 * P + P], ident)
                    last.then_inc(S("ret_tr"), 1)

                group(feat_chunk, L_FQK, 1, ready=ar + 2)
                group(feat_chunk, L_FQK + 4, 1)
                group(tok_chunk, L_FV, 1, [None, None, None, ff])
                group(feat_chunk, L_G2, 1, [None, None, cum, lambda: fox_scores(0)])
                group(feat_chunk, L_RQK, 1, [lambda: fox_scores(4)])
                group(tok_chunk, L_RV, 1, [None, None, lambda: fox_tr(0), lambda: fox_tr(4)])
                group(feat_chunk, L_LX, 1, [fox_out, rope])
                group(feat_chunk, L_FOXO, 0, [None, ret_scores, ret_out], ready=ar + 4)
                group(feat_chunk, L_LY, 1)
                pe.wait_ge(S("act_ready"), ar + 6)
                n = n0 + L_LRU
                begin(n, j0 + JL(L_LRU), strict=True)
                pe.wait_ge(S("ret_o"), L + 1)
                for b in list(range(8, 16)) + list(range(8)):
                    bank = (4 if b < 8 else 0) + b % 8 // 2
                    last = mm3(ps[:, bank, b % 2 * T:b % 2 * T + T], w_hi[:, n % 2, b * P:(b + 1) * P],
                               w_lo[:, n % 2, b * P:(b + 1) * P], act_hi[0][:, b % 8, :], act_lo[0][:, b % 8, :], True, True)
                    if b == 15:
                        last.then_inc(S("lru_x_mm"), 1)
                last.then_inc(S("chunk_done"), 1)
                pe.wait_ge(S("lru_ev"), 16 * L + 4)
                group(feat_chunk, L_RG, 1)
                group(feat_chunk, L_G1, 1, [None, None, ret_tr])
                group(feat_chunk, L_G0, 1)
                group(feat_chunk, L_RETO, 0, ready=ar + 8)
                group(feat_chunk, L_LRUO, 0, ready=ar + 10)
                group(feat_chunk, L_WOUT, 1, [None, None, lambda: norm_half(ns + 1, a6, 0)], ready=ar + 12)
                norm_half(ns + 1, a6, 1)
                keep_warm(6)
                norm(ns + 2, a6)
                keep_warm(9)
                for hf in range(2):
                    n = n0 + L_MLP + 16 * hf
                    j = j0 + JL(L_MLP) + 16 * hf
                    if hf == 0:
                        begin(n, j)
                        feat_chunk(n % 2, j % 2, 1, ready=ar + 14).then_inc(S("chunk_done"), 1)
                        job(feat_chunk, n + 1, j + 1, 3, 1)
                        job(feat_chunk, n + 4, j + 4, 4, 1)
                    else:
                        job(feat_chunk, n, j, 8, 1)
                    if L + 1 < layers:
                        pe.wait_ge(S("mods_done"), 4 + L)
                        mods(3 + 2 * L + hf, ada_in, 0, 32 - 16 * hf, 32 * hf, "ada_layer")
                    all_ready = 8 * (2 * L + hf + 1)
                    pe.wait_ge(S("mlp_ready"), all_ready - 3)
                    begin(n + 8, j + 8)
                    deep_chunk((n + 8) % 2, (j + 8) % 2, 1, ready=all_ready).then_inc(S("chunk_done"), 1)
                    job(deep_chunk, n + 9, j + 9, 3, 1)
                    if hf == 0:
                        job(deep_chunk, n + 12, j + 12, 4, 1)
                    else:
                        job(deep_chunk, n + 12, j + 12, 2, 1)
                        norm_half(ns + 3, a6, 0)
                        job(deep_chunk, n + 14, j + 14, 2, 1)
                norm_half(ns + 3, a6, 1)

        @block.scalar
        def _(act):
            act_ = nc.scalar.activation

            def prep(n, s4, s2):
                if isinstance(n, int):
                    if n >= total:
                        return
                    rnd = n // RAW * 16 + 16
                    act.wait_ge(S(f"raw_loaded{s4}"), rnd)
                    if n >= 2:
                        act.wait_ge(S("chunk_done"), n - 1)
                else:
                    act.wait_ge(S(f"raw_loaded{s4}"), n[1])
                    act.wait_ge(S("chunk_done"), n[0] - 1)
                act_(w_hi[:, s2, :], raw[:, s4, :], ACT.Copy).then_inc(S("hi_ready"), 1)

            def evict(dst, bank, n_done, func=ACT.Copy, scale=1.0, src=None):
                act.wait_ge(S("chunk_done"), n_done + 1)
                act_(dst, ps[:, bank, :] if src is None else src, func, scale=scale).then_inc(S("evicted"), 1)

            def job(n0, j0, count, dst, func=ACT.Copy, scale=1.0, sl=slice(0, 512), hook=None):
                def four(i, m):
                    for c in range(m):
                        n = n0 + c + 2
                        if isinstance(i, int):
                            prep(i + n, (i + n) % RAW, (i + n) % 2)
                        else:
                            prep((i + n, i * (16 // RAW) + (n // RAW * 16 + 16)), n % RAW, n % 2)
                        if hook:
                            hook(i, c)
                        else:
                            evict(dst(i + c), (j0 + c) % 2, i + (n0 + c), func, scale, ps[:, (j0 + c) % 2, sl])
                looped = loop_part(n0, count)
                if looped:
                    with act.Fori(0, looped // 4) as i:
                        four(i * 4, 4)
                for r in range(looped, count, 4):
                    four(r, min(4, count - r))

            def square(src, sq, hf, sem, n):
                o = slice(4 * hf, 4 * hf + 4)
                act.wait_ge(S(sem), n)
                act_(sq[:, o, :], src[:, o, :], ACT.Square).then_inc(S("norm_sq"), 1)

            def norm(k, src, sq, first=None, second=None):
                if second is None:
                    for hf in range(2):
                        o = slice(4 * hf, 4 * hf + 4)
                        act_(sq[:, o, :], src[:, o, :], ACT.Square).then_inc(S("norm_sq"), 1)
                else:
                    if first is not None:
                        square(src, sq, 0, *first)
                    square(src, sq, 1, *second)
                act.wait_ge(S("norm_ms"), k + 1)
                act_(std[:, :], ps[:, 7, 0:T], ACT.Sqrt, bias=eps[:, :]).then_inc(S("norm_std"), 1)

            def split(e, src, hi):
                for hf in range(2):
                    act.wait_ge(S("split_src"), 2 * source(e) + hf + 1)
                    act_(hi[:, 4 * hf:4 * hf + 4, :], src[:, 4 * hf:4 * hf + 4, :], ACT.Copy).then_inc(S("split_hi"), 1)

            def load_ada(k, dst, first, count):
                last = first + count - ADA_FIRST
                for s in range(2):
                    act.wait_ge(S(f"ada_stored{s}"), (last + 1 - s) // 2 * 16)
                act.dma_start(dst[:, :, :], io["ada_part"][first:first + count].rearrange("c p n -> p c n")).then_inc(S("ada_in"), 16)

            act.wait_ge(S("vec_loaded"), 16)
            act_(cth[:, :], vec[:, 0:3 * KT], ACT.Tanh, scale=0.5).then_inc(S("c_tanh"), 1)
            act.wait_ge(S("eps_set"), 1)
            act.wait_ge(S("x_loaded"), 3 * 16)
            norm(0, xc, norm_sq1)
            act.wait_ge(S("mod_rows_mm"), 1)
            act_(mod_rows[:, :].rearrange("p (a b) -> p a b", a=4), ps[0:2, 1:5, :], ACT.Copy).then_inc(S("mod_rows_ev"), 1)
            act.wait_ge(S("norm_rstd"), 1)
            norm(1, x, norm_sq1)
            split(0, norm_h1, act_hi[0])
            prep(0, 0, 0)
            prep(1, 1, 1)
            split(1, norm_h1, act_hi[1])
            act.wait_ge(S("small_loaded"), 2 * 16)
            act_(sw_hi[:, :], sw[:, 0:256], ACT.Copy).then_inc(S("sw_hi"), 1)
            for c in range(2):
                n = N_Q + c
                prep(n + 2, (n + 2) % RAW, n % 2)
                act.wait_ge(S("chunk_done"), n + 1)
                if c == 0:
                    act.wait_ge(S("pads"), 3)
                act_(pre_q[:, 2 * c:2 * c + 2, 1:T + 1], ps[:, n % 2, :].rearrange("p (b t) -> p b t", b=2), ACT.Copy)\
                    .then_inc(S("evicted"), 1)
            for c in range(4):
                n = N_KV + c
                prep(n + 2, (n + 2) % RAW, n % 2)
                act.wait_ge(S("chunk_done"), n + 1)
                bank = n % 2 * 2
                act_(pre_kv[:, 2 * c:2 * c + 2, :, 1:T + 1],
                     ps[:, bank:bank + 2, :].rearrange("p s (b t) -> p b s t", b=2), ACT.Copy).then_inc(S("evicted"), 1)
            act.wait_ge(S("conv"), 1)
            act_(th_kv[:, :, :, :], y_kv[:, :, :, :], ACT.Tanh, scale=0.5)
            act_(th_q[:, :, :], y_q[:, :, :], ACT.Tanh, scale=0.5).then_inc(S("conv_tanh"), 1)
            job(N_UZ, N_UZ, 1, lambda i: flat(uz[:, 2 * i:2 * i + 2, :]))
            ab = sm[:, 0, :]
            act.wait_ge(S("ab_abs"), 1)
            act_(sm[:, 2, :], sm[:, 2, :], ACT.Tanh, scale=0.5)
            act_(sm[:, 3, :], sm[:, 3, :], ACT.Exp, scale=-1.0)
            act_(sm[:, 4, 0:8], V("a_log", 8), ACT.Exp).then_inc(S("ab_act"), 1)
            job(N_UZ + 1, N_UZ + 1, 3, lambda i: flat(uz[:, 2 * i + 2:2 * i + 4, :]))
            act.wait_ge(S("tr_ev"), 10)
            act_(sq_kq[:, :, :], k_tok[:, :, :, :].rearrange("p t h n -> p (t h) n"), ACT.Square)
            act_(sq_q[:, :, :], q_tok[:, :, :, :].rearrange("p t h n -> p (t h) n"), ACT.Square).then_inc(S("kq_sq"), 1)
            act.wait_ge(S("kq_ss"), 1)
            act_(sm[:, 5, 0:24], sm[:, 5, 0:24], ACT.Sqrt, scale=0.25, bias=eps[:, :]).then_inc(S("kq_std"), 1)
            for g in range(6):
                act.wait_ge(S("trb_mm"), g + 1)
                dst = kT[:, g, :, :] if g < 4 else qT[:, g - 4, :, :]
                act_(flat(dst), ps[:, 4 + g % 3, :], ACT.Copy).then_inc(S("trb_ev"), 1)
            act.wait_ge(S("gc_diff"), 1)
            act_(sm[:, 8:11, :], sm[:, 8:11, :], ACT.Exp).then_inc(S("gc_exp"), 1)
            for e in range(8):
                act.wait_ge(S("dec_min"), e + 1)
                act_(dec[:, e % 2, :, :], dec[:, e % 2, :, :], ACT.Exp).then_inc(S("dec_exp"), 1)
            act.wait_ge(S("scan_o"), 8)
            act_(th_z[:, :, :], uz[:, 4:8, :], ACT.Tanh, scale=0.5).then_inc(S("z_tanh"), 1)
            act_(o_sq[:, :, :], o_tok[:, :, :, :].rearrange("p t h n -> p (t h) n"), ACT.Square).then_inc(S("o_sq"), 1)
            act.wait_ge(S("o_ss"), 1)
            act_(sm[:, 5, 0:8], sm[:, 5, 0:8], ACT.Sqrt, scale=1.0 / P, bias=eps[:, :]).then_inc(S("o_std"), 1)
            act.wait_ge(S("four_mm"), 1)
            act_(m1[:, :, :, :].rearrange("p (a g) m n -> p a (g m n)", a=2), ps[:, 4:6, :], ACT.Copy).then_inc(S("four_ev"), 1)
            act.wait_ge(S("four_mm"), 2)
            act_(Z[:, :, :, :, :].rearrange("p t (a g) m n -> p (t a) (g m n)", a=2), ps[:, 4:8, :], ACT.Copy)\
                .then_inc(S("four_ev"), 1)
            act.wait_ge(S("four_mm"), 3)
            act.wait_ge(S("o_ss"), 1)
            act_(yfd[:, 0:4, :].rearrange("p (a b) t -> p a (b t)", a=2), ps[:, 4:6, :], ACT.Copy).then_inc(S("split_src"), 1)
            split(2, yfd, act_hi[1])
            load_ada(1, ada_in16, 8, 16)
            job(N_OUT1, J_OUT1, 2, lambda i: flat(y1[:, 2 * i:2 * i + 2, :]))
            square(y1, norm_sq1, 0, "evicted", J_OUT1 + 2)
            job(N_OUT1 + 2, J_OUT1 + 2, 2, lambda i: flat(y1[:, 2 * i + 4:2 * i + 6, :]))
            norm(2, y1, norm_sq1, second=("evicted", J_OUT1 + 4))
            norm(3, x, norm_sq1, ("x_new", 1), ("x_new", 2))
            split(3, norm_h1, act_hi[1])
            def up_steps(i, c):
                n, s, e, first = N_UP + c, c % 2, i + c, isinstance(i, int) and i == 0
                act.wait_ge(S("chunk_done"), i + (n + 1))
                if not (first and c < 2):
                    act.wait_ge(S("evicted"), i + (J_UP + c - 1))
                act_(gpad[:, s, 1:ROWS + 1, 1:GRID_W + 1],
                     ps[:, c % 4, T:2 * T].rearrange("p (r w) -> p r w", r=ROWS), ACT.Copy)
                act_(gacc[:, s, :], ps[:, c % 4, T:2 * T], ACT.Copy, scale=vec[:, bass.ds(e + (V1["dwc"] + 4 * FB), 1)])\
                    .then_inc(S("gate_in"), 1)
                if isinstance(i, int):
                    prep(i + n + 2, (i + n + 2) % RAW, (i + n) % 2)
                else:
                    prep((i + (n + 2), i * (16 // RAW) + ((n + 2) // RAW * 16 + 16)), (n + 2) % RAW, n % 2)
                if not (first and c == 0):
                    up_silu(i, c)

            def up_silu(i, c):
                s = (c + 1) % 2
                act.wait_ge(S("gconv"), i + c)
                act_(gth[:, s, :], gacc[:, s, :], ACT.Tanh, scale=0.5).then_inc(S("gate_tanh"), 1)
                act.wait_ge(S("evicted"), i + (J_UP + c))
                act_(mid_hi1[:, bass.ds(i + (c - 1), 1), :], gm[:, s:s + 1, :], ACT.Copy).then_inc(S("mid_hi"), 1)
            act.wait_ge(S("gpad_zero"), 1)
            for c in range(4):
                up_steps(0, c)
            with act.Fori(1, FB // 4) as i:
                for c in range(4):
                    up_steps(i * 4, c)
            for c in range(FB % 4):
                up_steps(FB // 4 * 4, c)
            up_silu(FB // 4 * 4, FB % 4)
            outs = 0
            for c in range(11):
                n = N_DOWN + c
                prep(n + 2, (n + 2) % RAW, n % 2)
                while outs < KT and (outs * FB + FB - 1) // 16 == c:
                    evict(y_down[:, outs, :], outs % 2, n, src=ps[:, outs % 2, 0:T])
                    outs += 1
                    if outs == 4:
                        square(y_down, sq_down, 0, "evicted", J_DOWN + 4)
            norm(4, y_down, sq_down, second=("evicted", J_DOWN + 8))

            for L in range(layers):
                n0, j0 = N_LAYER + L * LAYER_CH, J_LAYER + L * LAYER_J
                ns, sp_ = 5 + 4 * L, 4 + 7 * L
                if L == 0:
                    act.dma_start(cu[:, 0:N_CB], io["consts_b"]).then_inc(S("consts_b"), 16)
                norm(ns, x, a6, ("x_new", 4 * L + 3), ("x_new", 4 * L + 4))
                split(sp_, a5, act_hi[1])
                act.wait_ge(S("lam_abs"), L + 1)
                act_(sm[:, 3, 0:8], sm[:, 3, 0:8], ACT.Exp, scale=-1.0).then_inc(S("lam_exp"), 1)
                def group(off, dst, after=(), n0=n0, j0=j0):
                    for c in range(4):
                        n = n0 + off + c
                        prep(n + 2, (n + 2) % RAW, n % 2)
                        evict(dst(c), (j0 + JL(off) + c) % 2, n)
                        if c < len(after) and after[c]:
                            after[c]()

                def to(t):
                    return lambda c: flat(t[:, 2 * c:2 * c + 2, :])

                def hi_of(e, src, hi):
                    return lambda: split(e, src, hi)

                def ff_exp():
                    act.wait_ge(S("ff_abs"), L + 1)
                    act_(sm[:, 3, 0:16], sm[:, 3, 0:16], ACT.Exp, scale=-1.0).then_inc(S("ff_exp"), 1)

                def fox_exp(h0):
                    act.wait_ge(S("fox_max"), L + 1)
                    for h in range(h0, h0 + 4):
                        for t in range(2):
                            s_ = fox_s[:, h, 0:P] if t == 0 else fox_s[:, h, P:3 * P]
                            c = t * 8 + h
                            act_(s_, s_, ACT.Exp, scale=P ** -0.5, bias=sm[:, 7, c:c + 1],
                                 accum_out=sm[:, 7, 16 + c:17 + c]).then_inc(S("fox_e"), 1)

                def fox_tr(h0):
                    for h in range(h0, h0 + 4):
                        act.wait_ge(S("fox_t_mm"), L * 8 + h + 1)
                        act_(fox_pt[:, h, :], ps[:, 4 + h % 4, 0:384], ACT.Copy).then_inc(S("fox_t_ev"), 1)

                def fox_out():
                    act.wait_ge(S("fox_o_mm"), L + 1)
                    act_(s4[:, :, :].rearrange("p (a b) n -> p a (b n)", a=4), ps[:, 4:8, :], ACT.Copy).then_inc(S("fox_o"), 1)

                def fox_split():
                    act.wait_ge(S("fox_o"), L + 1)
                    for hf in range(2):
                        act_(act_hi[0][:, 4 * hf:4 * hf + 4, :], s4[:, 4 * hf:4 * hf + 4, :], ACT.Copy).then_inc(S("split_hi"), 1)

                def tanh_gate(t, name, n_done):
                    def f():
                        act.wait_ge(S("evicted"), n_done)
                        act_(t[:, :, :], t[:, :, :], ACT.Tanh, scale=0.5).then_inc(S(name), 1)
                    return f

                def ret_out():
                    act.wait_ge(S("ret_o_mm"), L + 1)
                    act_(s4[:, :, :].rearrange("p (a b) n -> p a (b n)", a=4), ps[:, 4:8, :], ACT.Copy).then_inc(S("ret_o"), 1)

                def ret_sq():
                    act.wait_ge(S("ret_mean"), L + 1)
                    act_(s1[:, :, :], s4[:, :, :], ACT.Square).then_inc(S("ret_sq"), 1)

                def ret_std():
                    act.wait_ge(S("ret_ss"), L + 1)
                    act_(sm[:, 5, 0:8], sm[:, 5, 0:8], ACT.Sqrt, scale=1.0 / T, bias=eps[:, :]).then_inc(S("ret_std"), 1)

                def ret_gate():
                    act.wait_ge(S("lru_v"), L + 1)
                    act.wait_ge(S("evicted"), j0 + JL(L_G1))
                    act_(s1[:, :, :], s3[:, :, :], ACT.Tanh, scale=0.5).then_inc(S("ret_gtanh"), 1)

                def lru_gates(bs):
                    for b in bs:
                        bank = (4 if b < 8 else 0) + b % 8 // 2
                        dst = s7 if b < 8 else s8
                        act_(dst[:, b % 8, :], ps[:, bank, b % 2 * T:b % 2 * T + T], ACT.Tanh, scale=0.5,
                             bias=gs[:, 3, b:b + 1] if b < 8 else sm[:, 4, b - 8:b - 7]).then_inc(S("lru_ev"), 1)

                def lru_th():
                    act.wait_ge(S("lru_ev"), 16 * (L + 1))
                    for b in range(8):
                        act_(s6[:, b, :], s7[:, b, :], ACT.Tanh, scale=sm[:, 6, 16 + b:17 + b], bias=sm[:, 6, 16 + b:17 + b])\
                            .then_inc(S("lru_th"), 1)

                def lru_a():
                    act.wait_ge(S("lru_th"), 8 * (L + 1))
                    for b in range(8):
                        act_(s7[:, b, :], s7[:, b, :], ACT.Exp, scale=sm[:, 6, 24 + b:25 + b], bias=sm[:, 6, 24 + b:25 + b])\
                            .then_inc(S("lru_a"), 1)

                def lru_sqrt():
                    act.wait_ge(S("lru_v"), L + 1)
                    act_(s6[:, :, :], s6[:, :, :], ACT.Sqrt).then_inc(S("lru_sqrt"), 1)

                def gelu():
                    act.wait_ge(S("gelu_in"), L + 1)
                    act_(s1[:, :, :], s1[:, :, :], ACT.Tanh, scale=math.sqrt(2.0 / math.pi)).then_inc(S("gelu_tanh"), 1)

                job(n0 + L_FQK, j0 + L_FQK, 8, lambda i: s01[:, :, :].rearrange("p (a b) n -> p a (b n)", b=2)[:, bass.ds(i, 1), :])
                group(L_FV, lambda c: vtok_f[:, :, c * T:(c + 1) * T], [None, None, None, ff_exp])
                group(L_G2, to(s3))
                group(L_RQK, to(s6), [None, None, lambda: fox_exp(0), lambda: fox_exp(4)])
                act.wait_ge(S("mods_done"), 4 + L)
                group(L_RV, lambda c: vtok_r[:, :, c * T:(c + 1) * T], [None, None, lambda: fox_tr(0), lambda: fox_tr(4)])
                group(L_LX, to(s8), [fox_out, fox_split])
                group(L_FOXO, to(s0), [tanh_gate(s3, "g2_tanh", j0 + L_RQK), None, ret_out])
                group(L_LY, to(s2), [None, None, None, hi_of(sp_ + 2, s5, act_hi[0])])
                n = n0 + L_LRU
                act.wait_ge(S("lru_x_mm"), L + 1)
                lru_gates(range(8, 16))
                prep(n + 2, (n + 2) % RAW, n % 2)
                act.wait_ge(S("chunk_done"), n + 1)
                lru_gates(range(0, 4))
                act.wait_ge(S("merge"), 2 * L + 1)

                def rest():
                    lru_gates(range(4, 8))

                def ret_gates():
                    ret_gate()
                    lru_sqrt()
                group(L_RG, to(s3), [rest, lru_th, lru_a, ret_sq])
                group(L_G1, to(s5), [ret_std])
                act.wait_ge(S("ret_tr"), L + 1)
                group(L_G0, to(s4), [ret_gates, hi_of(sp_ + 3, s3, act_hi[0])])
                group(L_RETO, to(s3), [gelu, tanh_gate(s5, "g1_tanh", j0 + JL(L_G1) + 4), tanh_gate(s4, "g0_tanh", j0 + JL(L_RETO)),
                                       hi_of(sp_ + 4, s2, act_hi[0])])
                group(L_LRUO, to(s7))
                split(sp_ + 5, s0, act_hi[1])
                group(L_WOUT, to(s5), [None, lambda: square(a5, a6, 0, "evicted", j0 + JL(L_WOUT) + 2)])
                norm(ns + 1, a5, a6, second=("evicted", j0 + JL(L_MLP)))
                norm(ns + 2, x, a6, ("x_new", 4 * L + 5), ("x_new", 4 * L + 6))
                split(sp_ + 6, a5, act_hi[1])
                for hf in range(2):
                    n = n0 + L_MLP + 16 * hf
                    j = j0 + JL(L_MLP) + 16 * hf

                    def mlp_steps(i, c, n=n, j=j, hf=hf):
                        s = (j + c) % 2
                        e = 8 * (2 * L + hf) + i + c
                        evict(relu[:, s, :], s, i + (n + c), ACT.Relu)
                        act.wait_ge(S("mlp_sq"), e + 1)
                        act_(mlp_hi[:, bass.ds((i + c) * 2, 2), :], rsq[:, s, :].rearrange("p (b t) -> p b t", b=2), ACT.Copy)\
                            .then_inc(S("mlp_hi"), 1)
                    job(n, j, 8, None, hook=mlp_steps)
                    if hf == 0:
                        job(n + 8, j + 8, 8, lambda i: a4[:, bass.ds(i, 1), :], sl=slice(0, T))
                    else:
                        job(n + 8, j + 8, 4, lambda i: a5[:, i:i + 1, :], sl=slice(0, T))
                        job(n + 12, j + 12, 1, lambda i: a5[:, i + 4:i + 5, :], sl=slice(0, T))
                        square(a5, a6, 0, "y_sum", 2 * L + 1)
                        job(n + 13, j + 13, 3, lambda i: a5[:, i + 5:i + 6, :], sl=slice(0, T))
                norm(ns + 3, a5, a6, second=("y_sum", 2 * L + 2))

        @block.vector
        def _(dve):
            order = Order(dve, "dve_order")
            tt, ts, stt = nc.vector.tensor_tensor, nc.vector.tensor_scalar, nc.vector.scalar_tensor_tensor
            red = nc.vector.tensor_reduce

            def prep(n, s4, s2):
                if isinstance(n, int) and n >= total:
                    return
                dve.wait_ge(S("hi_ready"), n + 1)
                tt(w_lo[:, s2, :], raw[:, s4, :], w_hi[:, s2, :].bitcast(f32), ALU.subtract).then_inc(S("lo_ready"), 1)

            def job(n0, count, hook=None):
                def four(i, m):
                    for c in range(m):
                        n = n0 + c + 2
                        prep(i + n, n % RAW, n % 2)
                        if hook:
                            hook(i, c)
                looped = loop_part(n0, count)
                if looped:
                    with dve.Fori(0, looped // 4) as i:
                        four(i * 4, 4)
                for r in range(looped, count, 4):
                    four(r, min(4, count - r))

            def rs(k, src, dst):
                dve.wait_ge(S("norm_std"), k + 1)
                nc.vector.reciprocal(rstd[:, :], std[:, :]).then_inc(S("norm_rstd"), 1)
                dve.wait_ge(S("norm_rstd"), k + 1)
                marks = []
                for hf in range(2):
                    o = slice(4 * hf, 4 * hf + 4)
                    order.mark(tt(dst[:, o, :], src[:, o, :], bmid(rstd[:, :], 4), ALU.mult))
                    marks.append(order.n)
                return marks

            def split_lo(e, src, hi, lo):
                for hf in range(2):
                    o = slice(4 * hf, 4 * hf + 4)
                    dve.wait_ge(S("split_hi"), 2 * e + hf + 1)
                    tt(lo[:, o, :], src[:, o, :], hi[:, o, :].bitcast(f32), ALU.subtract).then_inc(S("act_ready"), 1)

            def modulate(k, e, src, dst, g, sh, hi, lo):
                marks = rs(k, src, dst)
                for b in range(KT):
                    if b % 4 == 0:
                        dve.wait_ge(S("dve_order"), marks[b // 4])
                    ins = ts(dst[:, b, :], dst[:, b, :], g[:, b:b + 1], sh[:, b:b + 1], ALU.mult, ALU.add)
                    if b % 4 == 3:
                        ins.then_inc(S("split_src"), 1)
                    else:
                        order.mark(ins)
                dve.wait_ge(S("split_src"), 2 * source(e) + 2)
                split_lo(e, dst, hi, lo)

            def residual(k, y, g):
                marks = rs(k, y, y)
                for b in range(KT):
                    if b % 4 == 0:
                        dve.wait_ge(S("dve_order"), marks[b // 4])
                    ins = stt(x[:, b, :], y[:, b, :], g[:, b:b + 1], x[:, b, :], ALU.mult, ALU.add)
                    if b % 4 == 3:
                        ins.then_inc(S("x_new"), 1)
                    else:
                        order.mark(ins)

            def softplus(dst, z, e, m, n):
                t1, t2 = sm[:, 11, 0:n], z
                order(ts(t1, e, 2.0, None, ALU.add))
                order(nc.vector.reciprocal(t1, t1))
                order(tt(t2, e, t1, ALU.mult))
                order(tt(t1, t2, t2, ALU.mult))
                order(ts(e, t1, 1.0 / 17, 1.0 / 15, ALU.mult, ALU.add))
                for odd in (13, 11, 9, 7, 5, 3, 1):
                    order(tt(e, e, t1, ALU.mult))
                    order(ts(e, e, 1.0 / odd, None, ALU.add))
                order(tt(e, e, t2, ALU.mult))
                order(stt(dst, e, 2.0, m, ALU.mult, ALU.add))

            nc.vector.memset(eps[:, :], EPS).then_inc(S("eps_set"), 1)
            dve.wait_ge(S("c_tanh"), 1)
            c3 = cs[:, :, :].rearrange("p a k -> p (a k)")
            order(ts(cth[:, :], cth[:, :], 0.5, 0.5, ALU.mult, ALU.add))
            tt(c3, cth[:, :], vec[:, 0:3 * KT], ALU.mult).then_inc(S("cs_ready"), 1)
            dve.wait_ge(S("cs_ready"), 1)
            dve.wait_ge(S("mod_mm"), 1)
            both = ps[:, 5, 0:32].rearrange("p (c a) -> p a c", a=2)
            order(tt(mod_ctx[:, :], both[:, 1, :], V("b_ada", 16), ALU.add))
            tt(mod[:, 0:16], both[:, 0, :], V("b_ada", 16), ALU.add).then_inc(S("mods_done"), 1)
            dve.wait_ge(S("mods_done"), 1)
            order(stt(gs[:, 0, :], mod_ctx[:, 8:16], 1.0, V("g_pre_mix", KT), ALU.add, ALU.mult))
            order(stt(gs[:, 1, :], mod[:, 8:16], 1.0, V("g_pre_mix", KT), ALU.add, ALU.mult))
            dve.wait_ge(S("norm_sq"), 2)
            modulate(0, 0, xc, norm_h1, gs[:, 0, :], mod_ctx[:, 0:8], act_hi[0], act_lo[0])
            dve.wait_ge(S("act_ready"), 2)
            prep(0, 0, 0)
            prep(1, 1, 1)
            modulate(1, 1, x, norm_h1, gs[:, 1, :], mod[:, 0:8], act_hi[1], act_lo[1])
            dve.wait_ge(S("sw_hi"), 1)
            tt(sw_lo[:, :], sw[:, 0:256], sw_hi[:, :].bitcast(f32), ALU.subtract).then_inc(S("sw_lo"), 1)
            nc.vector.memset(pre_kv[:, :, :, 0:T + 2:T + 1], 0.0).then_inc(S("pads"), 1)
            nc.vector.memset(pre_q[:, :, 0:1], 0.0).then_inc(S("pads"), 1)
            nc.vector.memset(pre_q[:, :, T + 1:T + 2], 0.0).then_inc(S("pads"), 1)
            job(N_Q, 2)
            def conv_q():
                dve.wait_ge(S("evicted"), 2)
                for i in range(3):
                    for b in range(4):
                        w = V("conv", 1, i * 12 + b)
                        order.mark(ts(y_q[:, b, :], pre_q[:, b, 0:T], w, None, ALU.mult) if i == 0 else
                                   stt(y_q[:, b, :], pre_q[:, b, i:T + i], w, y_q[:, b, :], ALU.mult, ALU.add))
                    dve.wait_ge(S("dve_order"), order.n)

            def conv_kv(c):
                dve.wait_ge(S("evicted"), c + 3)
                for i in range(3):
                    for b in (2 * c, 2 * c + 1):
                        w = V("conv", 1, i * 12 + 4 + b)
                        y, src = y_kv[:, b, :, :], pre_kv[:, b, :, i:T + i]
                        ins = ts(y, src, w, None, ALU.mult) if i == 0 else stt(y, src, w, y, ALU.mult, ALU.add)
                        if b == 7 and i == 2:
                            ins.then_inc(S("conv"), 1)
                        else:
                            order.mark(ins)
                    dve.wait_ge(S("dve_order"), order.n)

            for c in range(4):
                job(N_KV + c, 1)
                if c == 0:
                    conv_q()
                else:
                    conv_kv(c - 1)
            conv_kv(3)
            dve.wait_ge(S("conv_tanh"), 1)
            order(stt(flat(y_q[:, :, :]), flat(th_q[:, :, :]), 1.0, flat(y_q[:, :, :]), ALU.add, ALU.mult))
            stt(flat(y_kv[:, :, :, :]), flat(th_kv[:, :, :, :]), 1.0, flat(y_kv[:, :, :, :]), ALU.add, ALU.mult).then_inc(S("y_ready"), 1)
            job(N_UZ, 1)
            dve.wait_ge(S("ab_mm"), 1)
            abp = ps[:, 7, 0:64].rearrange("p (t c) -> p t c", t=4)
            s32 = lambda i: sm[:, i, :].rearrange("p (t c) -> p t c", t=4)
            order(nc.vector.tensor_copy(s32(2), abp[:, :, 0:8]))
            order(tt(s32(1), abp[:, :, 8:16], bmid(V("dt_bias", 8), 4), ALU.add))
            order(ts(s32(0), s32(1), 0.0, None, ALU.max))
            order(ts(sm[:, 3, :], sm[:, 1, :], -1.0, None, ALU.mult))
            tt(sm[:, 3, :], sm[:, 3, :], sm[:, 1, :], ALU.max).then_inc(S("ab_abs"), 1)
            job(N_UZ + 1, 1)
            dve.wait_ge(S("ab_act"), 1)
            order(ts(sm[:, 2, :], sm[:, 2, :], 0.5, 0.5, ALU.mult, ALU.add))
            softplus(sm[:, 0, :], sm[:, 1, :], sm[:, 3, :], sm[:, 0, :], 32)
            tneg = sm[:, 4, 0:8]
            order(ts(tneg, tneg, -1.0, None, ALU.mult))
            tt(s32(1), s32(0), bmid(tneg, 4), ALU.mult).then_inc(S("g_ready"), 1)
            job(N_UZ + 2, 2)
            for g in range(10):
                dve.wait_ge(S("tr_mm"), g + 1)
                src = ps[:, 4 + g % 3, :]
                if g < 4:
                    ins = nc.vector.tensor_copy(flat(k_tok[:, g, :, :]), src)
                elif g < 8:
                    ins = ts(flat(v_tok[:, g - 4, :, :]), src, 0.5, None, ALU.mult)
                else:
                    ins = nc.vector.tensor_copy(flat(q_tok[:, g - 8, :, :]), src)
                ins.then_inc(S("tr_ev"), 1)
            dve.wait_ge(S("kq_sq"), 1)
            order(red(sm[:, 5, 0:16], sq_kq[:, :, :], AX, ALU.add))
            red(sm[:, 5, 16:24], sq_q[:, :, :], AX, ALU.add).then_inc(S("kq_ss"), 1)
            dve.wait_ge(S("kq_std"), 1)
            order(nc.vector.reciprocal(sm[:, 5, 0:24], sm[:, 5, 0:24]))
            order(ts(sm[:, 5, 0:16], sm[:, 5, 0:16], 0.5, None, ALU.mult))
            order(ts(sm[:, 5, 16:24], sm[:, 5, 16:24], 0.5 * P ** -0.5, None, ALU.mult))
            k3 = k_tok[:, :, :, :].rearrange("p t h n -> p (t h) n")
            q3 = q_tok[:, :, :, :].rearrange("p t h n -> p (t h) n")
            order(tt(k3, k3, bc(sm[:, 5, 0:16], P), ALU.mult))
            tt(q3, q3, bc(sm[:, 5, 16:24], P), ALU.mult).then_inc(S("kq_norm"), 1)
            dve.wait_ge(S("gc_mm"), 1)
            order(nc.vector.tensor_copy(sm[:, 6:8, :], ps[:, 7, 0:64].rearrange("p (a c) -> p a c", a=2)))
            order(nc.vector.tensor_copy(sm[:, 8:10, :], sm[:, 6:8, :]))
            tt(sm[:, 10, :], sm[:, 7, :], sm[:, 6, :], ALU.subtract).then_inc(S("gc_diff"), 1)
            dve.wait_ge(S("gc_exp"), 1)
            order(tt(sm[:, 10, :], sm[:, 10, :], sm[:, 2, :], ALU.mult))
            ts(sm[:, 7, :], sm[:, 8, :], -1.0, None, ALU.mult).then_inc(S("gc_ev"), 1)
            dve.wait_ge(S("gc_ev"), 1)
            tril = cu[:, A_TRIL:A_TRIL + P]
            def mat_decay(d, t):
                e, cols = d * 4 + t, slice(t * 8 + d * 4, t * 8 + d * 4 + 4)
                dve.wait_ge(S("mat_mm"), e + 1)
                b6 = ps[:, MAT_BANK[e % 2] + 2, :].rearrange("p (h n) -> p h n", h=4)
                order(tt(dec[:, e % 2, :, :], b6, bc(sm[:, 6, cols], P), ALU.subtract))
                ts(dec[:, e % 2, :, :], dec[:, e % 2, :, :], 0.0, None, ALU.min).then_inc(S("dec_min"), 1)

            def mat_tile(d, t):
                e, cols = d * 4 + t, slice(t * 8 + d * 4, t * 8 + d * 4 + 4)
                b4, b5 = (ps[:, MAT_BANK[e % 2] + i, :].rearrange("p (h n) -> p h n", h=4) for i in range(2))
                dm, bt = dem[:, e % 2, :, :], Bm[:, t, :, :]
                dve.wait_ge(S("dec_exp"), e + 1)
                order(tt(dm, dec[:, e % 2, :, :], bmid(triu if d == 0 else tril, 4), ALU.mult))
                order.mark(tt(bt, b4, dm, ALU.mult))
                done = order.n
                if t >= 2:
                    order.mark(tt(attnT[:, d, t - 2, :, :], b5, dm, ALU.mult))
                dve.wait_ge(S("dve_order"), done)
                order(tt(bt, bt, bc(sm[:, 2, cols], P), ALU.mult))
                strict = cu[:, A_STR + d * P:A_STR + (d + 1) * P]
                tt(bt, bt, bmid(strict, 4), ALU.mult).then_inc(S("mat_ev"), 1)

            for d in range(2):
                mat_decay(d, 0)
                for t in range(4):
                    if t < 3:
                        mat_decay(d, t + 1)
                    mat_tile(d, t)
                for lvl in range(7):
                    size = 1 << lvl
                    pcol, rcol = (0, 1) if d == 0 else (1, 0)
                    mask = cu[:, A_LVL + (d * 7 + lvl) * P:A_LVL + (d * 7 + lvl + 1) * P]

                    def half(ap, which):
                        return ap.rearrange("p h (g two s) -> p h g two s", two=2, s=size)[:, :, :, which, :]
                    if lvl == 0:
                        dve.wait_ge(S("mat_ev"), 4 * (d + 1))
                        other = cu[:, A_LVL + (1 - d) * 7 * P:A_LVL + ((1 - d) * 7 + 1) * P]
                        for g in range(4):
                            order.mark(tt(U[:, d, g, :, :], Bm[:, g, :, :], bmid(other, 4), ALU.mult))
                        for g in range(4):
                            dve.wait_ge(S("inv_x_mm"), d * 28 + g + 1)
                            order(tt(Tm[:, g, :, :], ps[:, 4 + g, :].rearrange("p (h n) -> p h n", h=4), bmid(mask, 4), ALU.mult))
                            order.mark(tt(Tm[:, g, :, :], bmid(ident, 4), Tm[:, g, :, :], ALU.subtract))
                            tt(U[:, d, g, :, :], bmid(ident, 4), U[:, d, g, :, :], ALU.subtract).then_inc(S("inv_u"), 1)
                        continue
                    for g in range(4):
                        if lvl == 1:
                            dve.wait_ge(S("inv_u"), d * 28 + g + 1)
                            dve.wait_ge(S("dve_order"), order.n)
                        dve.wait_ge(S("inv_x_mm"), d * 28 + lvl * 4 + g + 1)
                        tt(X[:, g, :, :], ps[:, 4 + g, :].rearrange("p (h n) -> p h n", h=4), bmid(mask, 4), ALU.mult)\
                            .then_inc(S("inv_x"), 1)
                    for g in range(4):
                        dve.wait_ge(S("inv_u_mm"), d * 24 + (lvl - 1) * 4 + g + 1)
                        b = ps[:, 4 + g, :].rearrange("p (w h g s) -> p w h g s", w=2, h=4, s=size)
                        if lvl < 6:
                            Tg = half(Tm[:, g, :, :], pcol)
                            order(tt(Tg, Tg, b[:, 0], ALU.subtract))
                        Ug = half(U[:, d, g, :, :], rcol)
                        tt(Ug, Ug, b[:, 1], ALU.subtract).then_inc(S("inv_u"), 1)
                dve.wait_ge(S("inv_u"), d * 28 + 28)
            order(nc.vector.memset(St[:, :, :, :], 0.0))
            nc.vector.memset(o_tok[:, :, :, :], 0.0).then_inc(S("scan_init"), 1)
            dve.wait_ge(S("scan_init"), 1)
            oc = 0
            for st in range(4):
                tile = lambda d: (st if d == 0 else [1, 0, 3, 2][st])
                cols = lambda d: slice(tile(d) * 8 + d * 4, tile(d) * 8 + d * 4 + 4)
                b4 = lambda i: ps[:, i, :].rearrange("p (h n) -> p h n", h=4)
                for d in range(2):
                    dve.wait_ge(S("scan_p_mm"), st * 2 + d + 1)
                    order(tt(Rm[:, d, :, :], b4(4 + d), bc(sm[:, 7, cols(d)], P), ALU.mult))
                    tt(Rm[:, d, :, :], Rm[:, d, :, :], v_tok[:, tile(d), :, :], ALU.add).then_inc(S("scan_r"), 1)
                if st >= 2:
                    for d in range(2):
                        order(tt(tmp_s[:, d, :, :], b4(6 + d), bc(sm[:, 8, cols(d)], P), ALU.mult))
                        o_ = o_tok[:, tile(d) - 2, :, :]
                        tt(o_, o_, tmp_s[:, d, :, :], ALU.add).then_inc(S("scan_o"), 1)
                        oc += 1
                        dve.wait_ge(S("scan_o"), oc)
                for d in range(2):
                    dve.wait_ge(S("scan_w_mm"), st * 2 + d + 1)
                    order(tt(vn[:, d, :, :], b4(4 + d), bc(sm[:, 2, cols(d)], P), ALU.mult))
                    tt(v2[:, d, :, :], b4(4 + d), bc(sm[:, 10, cols(d)], P), ALU.mult).then_inc(S("scan_v"), 1)
                for d in range(2):
                    dve.wait_ge(S("scan_s_mm"), st * 2 + d + 1)
                    if st >= 2:
                        o_ = o_tok[:, tile(d) - 2, :, :]
                        tt(o_, o_, b4(6 + d), ALU.add).then_inc(S("scan_o"), 1)
                        oc += 1
                        dve.wait_ge(S("scan_o"), oc)
                    order(tt(St[:, d, :, :], St[:, d, :, :], bc(sm[:, 9, cols(d)], P), ALU.mult))
                    tt(St[:, d, :, :], St[:, d, :, :], b4(4 + d), ALU.add).then_inc(S("scan_s"), 1)
                    dve.wait_ge(S("scan_s"), st * 2 + d + 1)
            dve.wait_ge(S("o_sq"), 1)
            red(sm[:, 5, 0:8], o_sq[:, :, :], AX, ALU.add).then_inc(S("o_ss"), 1)
            dve.wait_ge(S("z_tanh"), 1)
            order(stt(th_z[:, :, :], th_z[:, :, :], 1.0, uz[:, 4:8, :], ALU.add, ALU.mult))
            order(ts(th_z[:, :, :], th_z[:, :, :], 0.5, None, ALU.mult))
            dve.wait_ge(S("o_std"), 1)
            order(nc.vector.reciprocal(sm[:, 5, 0:8], sm[:, 5, 0:8]))
            o3 = o_tok[:, :, :, :].rearrange("p t h n -> p (t h) n")
            tt(o3, o3, bc(sm[:, 5, 0:8], P), ALU.mult).then_inc(S("o_norm"), 1)
            dve.wait_ge(S("o_tr"), 1)
            dve.wait_ge(S("split_src"), 5)
            stt(yfd[:, 4:8, :], ps[:, 6:8, :].rearrange("p a (b t) -> p (a b) t", b=2), V("g_gdn"), th_z[:, :, :],
                ALU.mult, ALU.mult).then_inc(S("split_src"), 1)
            dve.wait_ge(S("split_src"), 6)
            split_lo(2, yfd, act_hi[1], act_lo[1])
            dve.wait_ge(S("mod_mm"), 2)
            tt(mod[:, 16:24], ps[:, 5, 0:8], V("b_ada", 8, 16), ALU.add).then_inc(S("mods_done"), 1)
            dve.wait_ge(S("mods_done"), 2)
            order(tt(gs[:, 0, :], mod[:, 16:24], V("g_post_mix", KT), ALU.mult))
            job(N_OUT1, 4)
            residual(2, y1, gs[:, 0, :])
            dve.wait_ge(S("mod_mm"), 3)
            tt(mod[:, 24:48], ps[:, 5, 8:32], V("b_ada", 24, 24), ALU.add).then_inc(S("mods_done"), 1)
            dve.wait_ge(S("mods_done"), 3)
            order(stt(gs[:, 1, :], mod[:, 32:40], 1.0, V("g_pre_ffn", KT), ALU.add, ALU.mult))
            order(tt(gs[:, 2, :], mod[:, 40:48], V("g_post_ffn", KT), ALU.mult))
            dve.wait_ge(S("x_new"), 2)
            modulate(3, 3, x, norm_h1, gs[:, 1, :], mod[:, 24:32], act_hi[1], act_lo[1])
            dve.wait_ge(S("act_ready"), 8)
            nc.vector.memset(gpad[:, :, :, :], 0.0).then_inc(S("gpad_zero"), 1)
            base = order.n
            UP_MARKS = 8

            def up_lo(e, s):
                dve.wait_ge(S("mid_hi"), e - 1)
                b = bass.ds(e - 2, 1)
                tt(mid_lo1[:, b, :], gm[:, s:s + 1, :], mid_hi1[:, b, :].bitcast(f32), ALU.subtract).then_inc(S("mid_ready"), 1)

            def up_silu_a(e, s):
                dve.wait_ge(S("gate_tanh"), e)
                order.mark(stt(gth[:, s, :], gth[:, s, :], 1.0, gacc[:, s, :], ALU.add, ALU.mult))

            def up_silu_b(s, bank, mark):
                dve.wait_ge(S("dve_order"), mark)
                stt(gm[:, s, :], gth[:, s, :], 0.5, ps[:, bank, 0:T], ALU.mult, ALU.mult).then_inc(S("evicted"), 1)

            def up_steps(i, c):
                n, s, e, first = N_UP + c, c % 2, i + c, isinstance(i, int) and i == 0
                order.n = base if first and c == 0 else i * UP_MARKS + (base + c * UP_MARKS - 1)
                w_slot, r_slot = n % 2, (n + 2) % RAW
                dve.wait_ge(S("gate_in"), e + 1)
                acc = gacc[:, s, :].rearrange("p (r w) -> p r w", r=ROWS)
                silu_mark = None
                for at_, tap in enumerate((0, 1, 2, 3, 5, 6, 7, 8)):
                    src = gpad[:, s, tap // 3:tap // 3 + ROWS, tap % 3:tap % 3 + GRID_W]
                    w = vec[:, bass.ds(e + (V1["dwc"] + tap * FB), 1)]
                    if at_:
                        dve.wait_ge(S("dve_order"), tap_mark)
                    ins = stt(acc, src, w, acc, ALU.mult, ALU.add)
                    if at_ < 7:
                        order.mark(ins)
                        tap_mark = order.n
                    else:
                        ins.then_inc(S("gconv"), 1)
                    if at_ == 0 and not (first and c < 2):
                        up_lo(e, s)
                    if 1 <= at_ < 5:
                        if at_ == 1:
                            dve.wait_ge(S("hi_ready"), i + (n + 3))
                        o = slice((at_ - 1) * 512, at_ * 512)
                        ins = tt(w_lo[:, w_slot, o], raw[:, r_slot, o], w_hi[:, w_slot, o].bitcast(f32), ALU.subtract)
                        if at_ == 4:
                            ins.then_inc(S("lo_ready"), 1)
                    if not (first and c == 0):
                        if at_ == 5:
                            up_silu_a(e, 1 - s)
                            silu_mark = order.n
                        if at_ == 6:
                            up_silu_b(1 - s, (c + 3) % 4, silu_mark)

            for c in range(4):
                up_steps(0, c)
            with dve.Fori(1, FB // 4) as i:
                for c in range(4):
                    up_steps(i * 4, c)
            for c in range(FB % 4):
                up_steps(FB // 4 * 4, c)
            order.n = base + FB * UP_MARKS - 1
            up_lo(FB, FB % 2)
            up_silu_a(FB, (FB - 1) % 2)
            up_silu_b((FB - 1) % 2, (FB - 1) % 4, order.n)
            up_lo(FB + 1, (FB - 1) % 2)
            job(N_DOWN, 11)
            residual(4, y_down, gs[:, 2, :])
            dve.wait_ge(S("x_new"), 4)

            for L in range(layers):
                n0 = N_LAYER + L * LAYER_CH
                j0 = J_LAYER + L * LAYER_J
                ns, sp_ = 5 + 4 * L, 4 + 7 * L
                v = lambda name, n=1, i=0: V(name, n, i, L)
                order(ts(sm[:, 6, 8:16], v("lam", 8), -1.0, None, ALU.mult))
                order(ts(sm[:, 6, 0:8], sm[:, 6, 8:16], 0.0, None, ALU.max))
                tt(sm[:, 3, 0:8], sm[:, 6, 8:16], v("lam", 8), ALU.max).then_inc(S("lam_abs"), 1)
                order(ts(gs[:, 3, :], v("b_a", 8), 0.5, None, ALU.mult))
                order(ts(sm[:, 4, 0:8], v("b_x", 8), 0.5, None, ALU.mult))
                dve.wait_ge(S("mod_mm"), 5 + 2 * L)
                tt(mod[:, :], ps[:, 5, 0:48], v("b_ada", 48), ALU.add).then_inc(S("mods_done"), 1)
                dve.wait_ge(S("mods_done"), 4 + L)
                order(stt(gs[:, 0, :], mod[:, 8:16], 1.0, v("g_pre_mix", KT), ALU.add, ALU.mult))
                modulate(ns, sp_, x, a5, gs[:, 0, :], mod[:, 0:8], act_hi[1], act_lo[1])
                order(tt(gs[:, 0, :], mod[:, 16:24], v("g_post_mix", KT), ALU.mult))
                order(stt(gs[:, 1, :], mod[:, 32:40], 1.0, v("g_pre_mlp", KT), ALU.add, ALU.mult))
                order(tt(gs[:, 2, :], mod[:, 40:48], v("g_post_mlp", KT), ALU.mult))
                dve.wait_ge(S("lam_exp"), L + 1)
                softplus(sm[:, 6, 0:8], sm[:, 6, 8:16], sm[:, 3, 0:8], sm[:, 6, 0:8], 8)
                order(ts(sm[:, 6, 16:24], sm[:, 6, 0:8], LRU_C / 2, None, ALU.mult))
                order(ts(sm[:, 6, 24:32], sm[:, 6, 0:8], -LRU_C / 2, None, ALU.mult))
                def group(off, after=(), n0=n0):
                    for c in range(4):
                        n = n0 + off + c
                        prep(n + 2, (n + 2) % RAW, n % 2)
                        for f in (after[c] if c < len(after) else ()):
                            f()

                fm = cu[:, B_FM:B_FM + T]

                def ff():
                    dve.wait_ge(S("ff_mm"), L + 1)
                    y16 = sm[:, 1, 0:16].rearrange("p (t h) -> p t h", t=2)
                    order(tt(y16, ps[:, 7, 0:16].rearrange("p (t h) -> p t h", t=2), bmid(v("b_f", 8), 2), ALU.add))
                    order(ts(sm[:, 2, 0:16], sm[:, 1, 0:16], -1.0, None, ALU.mult))
                    order(ts(sm[:, 0, 0:16], sm[:, 2, 0:16], 0.0, None, ALU.max))
                    tt(sm[:, 3, 0:16], sm[:, 2, 0:16], sm[:, 1, 0:16], ALU.max).then_inc(S("ff_abs"), 1)

                def ff_log():
                    dve.wait_ge(S("ff_exp"), L + 1)
                    softplus(sm[:, 0, 0:16], sm[:, 2, 0:16], sm[:, 3, 0:16], sm[:, 0, 0:16], 16)
                    ts(sm[:, 1, 0:16], sm[:, 0, 0:16], math.sqrt(P), None, ALU.mult).then_inc(S("nlf_ready"), 1)

                def cum():
                    dve.wait_ge(S("cum_mm"), L + 1)
                    ts(sm[:, 5, 0:16], ps[:, 7, 16:32], -1.0, None, ALU.mult).then_inc(S("cum_ev"), 1)
                    dve.wait_ge(S("cum_ev"), L + 1)
                    dve.wait_ge(S("consts_b"), 16)

                def fox_scores(h0):
                    for h in range(h0, h0 + 4):
                        bank = 4 + h % 4
                        dve.wait_ge(S("fox_s_mm"), L * 8 + h + 1)
                        order.mark(stt(fox_s[:, h, 0:P], ps[:, bank, 0:P], sm[:, 5, h:h + 1], fm[:, P:T], ALU.add, ALU.add))
                        stt(fox_s[:, h, P:3 * P], ps[:, bank, P:3 * P], sm[:, 5, 8 + h:9 + h], fm, ALU.add, ALU.add)\
                            .then_inc(S("fox_s_ev"), 1)

                def fox_max():
                    dve.wait_ge(S("fox_s_ev"), L * 8 + 8)
                    dve.wait_ge(S("dve_order"), order.n)
                    order(red(sm[:, 7, 0:8], fox_s[:, :, 0:P], AX, ALU.max, negate=True))
                    order(red(sm[:, 7, 8:16], fox_s[:, :, P:3 * P], AX, ALU.max, negate=True))
                    ts(sm[:, 7, 0:16], sm[:, 7, 0:16], P ** -0.5, None, ALU.mult).then_inc(S("fox_max"), 1)

                def fox_norm():
                    dve.wait_ge(S("fox_e"), 16 * (L + 1))
                    order(nc.vector.reciprocal(sm[:, 7, 16:32], sm[:, 7, 16:32]))
                    order(tt(fox_s[:, :, 0:P], fox_s[:, :, 0:P], bc(sm[:, 7, 16:24], P), ALU.mult))
                    tt(fox_s[:, :, P:3 * P], fox_s[:, :, P:3 * P], bc(sm[:, 7, 24:32], T), ALU.mult).then_inc(S("fox_p"), 1)

                def lo_of(e, src, which):
                    return lambda: split_lo(e, src, act_hi[which], act_lo[which])

                cos, sin = cu[:, B_COS:B_COS + T], cu[:, B_SIN:B_SIN + T]

                def rope_sin():
                    dve.wait_ge(S("rope_mm"), L + 1)
                    order(tt(s1, ps[:, 4:8, :].rearrange("p a (b t) -> p (a b) t", b=2), bmid(sin, 8), ALU.mult))

                def rope_cos():
                    order(tt(s6[:, :, :], s6[:, :, :], bmid(cos, 8), ALU.mult))

                def rope_add():
                    tt(s6[:, :, :], s6[:, :, :], s1, ALU.add).then_inc(S("rope_done"), 1)

                def ret_p():
                    dve.wait_ge(S("ret_s_mm"), L + 1)
                    tt(flat(s1), ps[:, 4:8, :].rearrange("p a b -> p (a b)"), cu[:, B_RET:B_RET + 2048], ALU.mult)\
                        .then_inc(S("ret_p"), 1)

                def fox_merge():
                    dve.wait_ge(S("evicted"), j0 + L_LY)
                    dve.wait_ge(S("g2_tanh"), L + 1)
                    stt(s0, s3[:, :, :], 1.0, s0, ALU.add, ALU.mult).then_inc(S("merge"), 1)

                def ret_mean():
                    dve.wait_ge(S("ret_o"), L + 1)
                    order(red(sm[:, 5, 0:8], s4[:, :, :], AX, ALU.add))
                    order(ts(sm[:, 5, 0:8], sm[:, 5, 0:8], 1.0 / T, None, ALU.mult))

                def ret_centre():
                    tt(s4[:, :, :], s4[:, :, :], bc(sm[:, 5, 0:8], T), ALU.subtract).then_inc(S("ret_mean"), 1)

                def ret_ss():
                    dve.wait_ge(S("ret_sq"), L + 1)
                    red(sm[:, 5, 0:8], s1, AX, ALU.add).then_inc(S("ret_ss"), 1)

                def ret_norm():
                    dve.wait_ge(S("ret_std"), L + 1)
                    order(nc.vector.reciprocal(sm[:, 5, 0:8], sm[:, 5, 0:8]))
                    tt(s4[:, :, :], s4[:, :, :], bc(sm[:, 5, 0:8], T), ALU.mult).then_inc(S("ret_norm"), 1)

                def ret_y():
                    dve.wait_ge(S("ret_gtanh"), L + 1)
                    order(stt(s3[:, :, :], s1, 1.0, s3[:, :, :], ALU.add, ALU.mult))
                    dve.wait_ge(S("ret_tr"), L + 1)
                    for hf in range(2):
                        o = slice(4 * hf, 4 * hf + 4)
                        stt(flat(s3[:, o, :]), ps[:, 4 + 2 * hf:6 + 2 * hf, :].rearrange("p a b -> p (a b)"), 0.5, flat(s3[:, o, :]),
                            ALU.mult, ALU.mult).then_inc(S("split_src"), 1)

                def conv(tap):
                    def f():
                        if tap == 3:
                            dve.wait_ge(S("evicted"), j0 + L_FOXO)
                        back = 3 - tap
                        for b in range(8):
                            w = v("conv_w", 1, tap * 8 + b)
                            if tap == 3:
                                ins = ts(s5[:, b, :], s8[:, b, :], w, v("conv_b", 1, b), ALU.mult, ALU.add)
                            else:
                                ins = stt(s5[:, b, back:T], s8[:, b, 0:T - back], w, s5[:, b, back:T], ALU.mult, ALU.add)
                            if tap == 0 and b % 4 == 3:
                                ins.then_inc(S("split_src"), 1)
                            else:
                                order.mark(ins)
                        dve.wait_ge(S("dve_order"), order.n)
                    return f

                def lru_ix():
                    dve.wait_ge(S("lru_ev"), 16 * L + 8)
                    stt(s8[:, :, :], s8[:, :, :], 1.0, s5[:, :, :], ALU.add, ALU.mult).then_inc(S("lru_ix"), 1)

                def gelu_a():
                    order(tt(s1, s2[:, :, :], s2[:, :, :], ALU.mult))
                    order(ts(s1, s1, 0.044715, 1.0, ALU.mult, ALU.add))

                def gelu_b():
                    tt(s1, s1, s2[:, :, :], ALU.mult).then_inc(S("gelu_in"), 1)

                def gelu_c():
                    dve.wait_ge(S("gelu_tanh"), L + 1)
                    order(stt(s2[:, :, :], s1, 1.0, s2[:, :, :], ALU.add, ALU.mult))

                def lru_a2():
                    dve.wait_ge(S("lru_a"), 8 * (L + 1))
                    order(tt(s1, s7[:, :, :], s7[:, :, :], ALU.mult))

                def lru_v():
                    order(stt(s6[:, :, :], s1, 1.0, s6[:, :, :], ALU.add, ALU.mult))
                    ts(s6[:, :, :], s6[:, :, :], 0.0, None, ALU.max).then_inc(S("lru_v"), 1)

                def lru_u():
                    dve.wait_ge(S("lru_sqrt"), L + 1)
                    dve.wait_ge(S("lru_ix"), L + 1)
                    order(stt(s8[:, :, :], s8[:, :, :], 0.5, s6[:, :, :], ALU.mult, ALU.mult))

                def lru_scan():
                    for b in range(8):
                        order.mark(nc.vector.tensor_tensor_scan(s1[:, b, :], s7[:, b, :], s8[:, b, :], 0.0, ALU.mult, ALU.add))
                    dve.wait_ge(S("dve_order"), order.n)

                def lru_y():
                    for hf in range(2):
                        o = slice(4 * hf, 4 * hf + 4)
                        stt(s2[:, o, :], s2[:, o, :], 0.5, s1[:, o, :], ALU.mult, ALU.mult).then_inc(S("split_src"), 1)

                def ret_gated():
                    dve.wait_ge(S("evicted"), j0 + JL(L_LRUO))
                    dve.wait_ge(S("g0_tanh"), L + 1)
                    order(stt(s3[:, :, :], s4[:, :, :], 1.0, s3[:, :, :], ALU.add, ALU.mult))

                def ret_merge():
                    tt(s0, s0, s3[:, :, :], ALU.add).then_inc(S("merge"), 1)
                    dve.wait_ge(S("merge"), 2 * L + 2)

                def lru_merge(hf):
                    def f():
                        o = slice(4 * hf, 4 * hf + 4)
                        dve.wait_ge(S("evicted"), j0 + JL(L_LRUO) + 2 * (hf + 1))
                        dve.wait_ge(S("g1_tanh"), L + 1)
                        order(stt(s7[:, o, :], s5[:, o, :], 1.0, s7[:, o, :], ALU.add, ALU.mult))
                        order(tt(s0[:, o, :], s0[:, o, :], s7[:, o, :], ALU.add))
                        ts(s0[:, o, :], s0[:, o, :], 0.5, None, ALU.mult).then_inc(S("split_src"), 1)
                    return f

                job(n0 + L_FQK, 8)
                group(L_FV, [[], [], [], [ff]])
                group(L_G2, [[ff_log], [], [cum], [lambda: fox_scores(0)]])
                group(L_RQK, [[lambda: fox_scores(4)], [fox_max]])
                group(L_RV, [[fox_norm]])
                group(L_LX, [[], [rope_sin], [lo_of(sp_ + 1, s4, 0)], [rope_cos]])
                group(L_FOXO, [[rope_add], [ret_p], [conv(3)], [conv(2)]])
                group(L_LY, [[fox_merge], [conv(1)], [conv(0)], [lo_of(sp_ + 2, s5, 0)]])
                n = n0 + L_LRU
                prep(n + 2, (n + 2) % RAW, n % 2)
                lru_ix()
                group(L_RG, [[], [ret_mean], [ret_centre], []])
                group(L_G1, [[ret_ss], [ret_norm], [lru_a2], [lru_v]])
                group(L_G0, [[], [ret_y], [lo_of(sp_ + 3, s3, 0)], [gelu_a, gelu_b]])
                group(L_RETO, [[lru_u], [gelu_c], [lru_scan], [lru_y, lo_of(sp_ + 4, s2, 0)]])
                group(L_LRUO, [[ret_gated], [ret_merge], [lru_merge(0)], [lru_merge(1)]])
                split_lo(sp_ + 5, s0, act_hi[1], act_lo[1])
                group(L_WOUT)
                residual(ns + 1, a5, gs[:, 0, :])
                dve.wait_ge(S("x_new"), 4 * L + 6)
                modulate(ns + 2, sp_ + 6, x, a5, gs[:, 1, :], mod[:, 24:32], act_hi[1], act_lo[1])
                for hf in range(2):
                    n = n0 + L_MLP + 16 * hf
                    j = j0 + JL(L_MLP) + 16 * hf

                    def mlp_steps(i, c, j=j, hf=hf):
                        s = (j + c) % 2
                        e = 8 * (2 * L + hf) + i + c
                        dve.wait_ge(S("evicted"), i + (j + c + 1))
                        tt(rsq[:, s, :], relu[:, s, :], relu[:, s, :], ALU.mult).then_inc(S("mlp_sq"), 1)
                        dve.wait_ge(S("mlp_hi"), e + 1)
                        b = bass.ds((i + c) * 2, 2)
                        tt(mlp_lo[:, b, :], rsq[:, s, :].rearrange("p (b t) -> p b t", b=2), mlp_hi[:, b, :].bitcast(f32),
                           ALU.subtract).then_inc(S("mlp_ready"), 1)
                    job(n, 8, hook=mlp_steps)
                    if hf == 0:
                        job(n + 8, 8)
                    else:
                        for half in range(2):
                            if half == 0:
                                job(n + 8, 5)
                            else:
                                job(n + 13, 3)
                            o = slice(4 * half, 4 * half + 4)
                            dve.wait_ge(S("evicted"), j0 + LAYER_J - 4 + 4 * half)
                            tt(a5[:, o, :], a5[:, o, :], a4[:, o, :], ALU.add).then_inc(S("y_sum"), 1)
                dve.wait_ge(S("y_sum"), 2 * L + 2)
                residual(ns + 3, a5, gs[:, 2, :])
                dve.wait_ge(S("x_new"), 4 * L + 8)


def _constants():
    i = np.arange(P)
    triu = (i[:, None] <= i[None, :]).astype(np.float64)
    common = np.zeros((P, N_COMMON))
    common[:, C_ID:C_ID + P] = np.eye(P)
    common[:, C_TRIU:C_TRIU + P] = triu
    common[:, C_ONES:C_ONES + P] = 1.0
    common[:, C_OMEAN:C_OMEAN + P] = 1.0 / D
    a = np.zeros((P, N_CU))
    a[:, A_TRIL:A_TRIL + P] = triu.T
    a[:, A_STR:A_STR + P] = triu - np.eye(P)
    a[:, A_STR + P:A_STR + 2 * P] = triu.T - np.eye(P)
    for lvl in range(7):
        size = 1 << lvl
        group, second = i // (2 * size), i % (2 * size) >= size
        m = (group[:, None] == group[None, :]) & second[:, None] & ~second[None, :]
        a[:, A_LVL + lvl * P:A_LVL + (lvl + 1) * P] = m
        a[:, A_LVL + (7 + lvl) * P:A_LVL + (8 + lvl) * P] = m.T
    ang = 2 * np.pi * (i[:, None] * i[None, :] % P) / P
    a[:, A_CC:A_CC + P], a[:, A_SC:A_SC + P] = np.cos(ang), np.sin(ang)
    t = np.arange(T)
    ang = 2 * np.pi * (t[:, None] * t[None, :] % T) / T
    norm = 1.0 / math.sqrt(T * P)
    for tile in range(TT):
        a[:, A_CL + tile * T:A_CL + (tile + 1) * T] = np.cos(ang[tile * P:(tile + 1) * P]) * norm
        a[:, A_SL + tile * T:A_SL + (tile + 1) * T] = -np.sin(ang[tile * P:(tile + 1) * P]) * norm
    b = np.zeros((P, N_CU))
    b[:, B_PERM:B_PERM + P] = np.roll(np.eye(P), P // 2, axis=0)
    half = P // 2
    inv = np.float32(10000.0) ** (-np.arange(half, dtype=np.float32) / np.float32(half))
    ang = (inv[:, None] * t[None, :].astype(np.float32)).astype(np.float64)
    b[:, B_COS:B_COS + T] = np.concatenate([np.cos(ang)] * 2)
    b[:, B_SIN:B_SIN + T] = np.concatenate([-np.sin(ang), np.sin(ang)])
    for h in range(HEADS):
        gamma = 1.0 - 2.0 ** (-5.0 - h)
        w = gamma ** np.abs(t[:, None] - t[None, :]) * P ** -0.5
        w = np.where(t[:, None] // 64 <= t[None, :] // 64, w, 0.0)
        for m in range(TT):
            o = B_RET + (h * 2 + m) * T
            b[:, o:o + T] = w[m * P:(m + 1) * P]
    b[:, B_FM + P:B_FM + T] = np.where(i[None, :] <= i[:, None], 0.0, -1e30)
    return common.astype(np.float32), a.astype(np.float32), b.astype(np.float32)


def _columns_of(v):
    return np.asarray(v).reshape(-1, P).T


def _feat(w):
    k, n = w.shape
    c = w.reshape(k // P, P, n // P, P).transpose(2, 1, 0, 3)
    per = CH // (k // P * P)
    return c.reshape(-1, per, P, k // P * P).transpose(0, 2, 1, 3).reshape(-1, P, CH)


def _tok(w):
    n = w.shape[1]
    return w.reshape(KT, P, n // T, T).transpose(2, 1, 0, 3).reshape(-1, P, CH)


def _stream(a):
    w = np.asarray(a["w_in"])[0]
    u, q, k, v, z = w[:, 0:512], w[:, 512:1024], w[:, 1024:1536], w[:, 1536:2048], w[:, 2048:2560]
    parts = [_feat(q), _feat(k), _feat(v), _feat(u), _feat(z), _feat(np.asarray(a["w_out"])[0])]
    up = np.asarray(a["w_up"])[0].reshape(D, 2, FB, P).transpose(0, 2, 1, 3).reshape(D, 2 * D_FF)
    parts.append(_feat(up))
    down = np.asarray(a["w_down"])[0].reshape(FB, P, KT, P).transpose(2, 0, 1, 3).reshape(-1, 16, P, P)
    parts.append(down.transpose(0, 2, 1, 3).reshape(-1, P, CH))
    for L in range(LAYERS):
        g = lambda name: np.asarray(a[name])[L]
        w = g("w_in_2")
        cut = np.cumsum([0, 512, 512, 1024, 1024, 1024, 1024, 1024, 1024, 1024, 8, 3072])
        rq, rk, rv, rg, lx, ly, fq, fk, fv, ff, gates = (w[:, cut[i]:cut[i + 1]] for i in range(11))
        g0, g1, g2 = gates[:, 0:D], gates[:, D:2 * D], gates[:, 2 * D:]
        lru = np.concatenate([g("lru_w_a_2"), g("lru_w_x_2")]).transpose(1, 0, 2).reshape(1, P, CH)
        parts += [_feat(fq), _feat(fk), _tok(fv), _feat(g2), _feat(rq), _feat(rk), _tok(rv), _feat(lx),
                  _feat(g("fox_w_o_2")), _feat(ly), lru, _feat(rg), _feat(g1), _feat(g0),
                  _feat(g("ret_w_o_2")), _feat(g("lru_w_o_2")), _feat(g("w_out_2"))]
        w1, w2 = g("mlp_w1_2"), g("mlp_w2_2")
        for hf in range(2):
            parts += [_feat(w1[:, hf * 2048:(hf + 1) * 2048]), _feat(w2[hf * 2048:(hf + 1) * 2048])]
    return np.concatenate(parts)


def _vectors(a):
    out = np.zeros((P, NV), np.float32)

    def put(at, v):
        out[:, at:at + v.shape[1]] = v
    rows = lambda v: np.broadcast_to(np.asarray(v).reshape(1, -1), (P, np.asarray(v).size))
    for name in ("c", "c_ctx", "c_2", "b_ada", "g_pre_mix", "g_post_mix", "g_pre_ffn", "g_post_ffn", "g_gdn"):
        put(V1[name], _columns_of(a[name]))
    put(V1["conv"], _columns_of(a["w_qkv_conv"]))
    put(V1["dwc"], _columns_of(a["w_dwc"]))
    put(V1["dt_bias"], rows(a["dt_bias"]))
    put(V1["a_log"], rows(a["a_log"]))
    for L in range(LAYERS):
        at = VEC_FIRST + L * VEC_LAYER
        for name, key in (("b_ada", "ada_b_2"), ("g_pre_mix", "norm_pre_mix_2"), ("g_post_mix", "norm_post_mix_2"),
                          ("g_pre_mlp", "norm_pre_mlp_2"), ("g_post_mlp", "norm_post_mlp_2"), ("conv_w", "conv_w_2"),
                          ("conv_b", "conv_b_2"), ("b_a", "lru_b_a_2"), ("b_x", "lru_b_x_2"), ("lam", "lru_lambda_2")):
            put(at + VL[name], _columns_of(np.asarray(a[key])[L]))
        put(at + VL["b_f"], rows(np.asarray(a["fox_b_f_2"])[L]))
    return out


def arrays_of(inputs):
    a = {k: np.asarray(v) for k, v in inputs.items()}
    common, ca, cb = _constants()
    small = np.zeros((P, N_SW), np.float32)
    small[:, SW_AB:SW_AB + 128] = a["w_in"][0][:, 2560:2576].reshape(KT, P, 16).transpose(1, 0, 2).reshape(P, 128)
    for L in range(LAYERS):
        ff = a["w_in_2"][L][:, 8192:8200]
        small[:, SW_FF + L * 64:SW_FF + (L + 1) * 64] = ff.reshape(KT, P, 8).transpose(1, 0, 2).reshape(P, 64)
    small[:, SW_WF:] = a["w_fourier"][0].transpose(1, 0, 2).reshape(P, 512)
    ada = np.concatenate([_tok(a["w_ada"][0])] + [_tok(a["ada_w_2"][L]) for L in range(LAYERS)])
    feat = lambda t: np.ascontiguousarray(t[0].reshape(T, KT, P).transpose(2, 1, 0))
    return {"xT": feat(a["x"]), "ctxT": feat(a["ctx"]), "stream": _stream(a), "ada": ada, "small_w": small,
            "vecs": _vectors(a), "consts_common": common, "consts_a": ca[:, :N_CA], "consts_b": cb[:, :N_CB]}


def kernel(**inputs):
    import concourse.bacc as bacc
    from concourse.bass_utils import run_bass_kernel_spmd

    nc = bacc.Bacc("TRN2", target_bir_lowering=False, num_devices=1)
    arrays = {k: np.ascontiguousarray(v) for k, v in arrays_of(inputs).items()}
    io = {k: nc.dram_tensor(k, v.shape, mybir.dt.float32, kind="ExternalInput").ap() for k, v in arrays.items()}
    io["out"] = nc.dram_tensor("out", [P, KT, T], mybir.dt.float32, kind="ExternalOutput").ap()
    io["ada_part"] = nc.dram_tensor("ada_part", [24 * (1 + LAYERS), P, T], mybir.dt.float32).ap()
    build_program(nc, io)
    got = run_bass_kernel_spmd(nc, [arrays], core_ids=[0]).results[0]["out"]
    return np.ascontiguousarray(np.asarray(got).reshape(P, KT, T).transpose(2, 1, 0)).reshape(1, T, D)
```
